# Optimizing a Trainium2 kernel written in Bass

```python
import jax
import jax.numpy as jnp
from jax import lax
import numpy as np
import jax, jax.numpy as jnp

D_MODEL = 1024
BATCH = 1
SEQ = 256
DEPTH = 2

HEAD_DIM = 64
EPS = 1e-6
MLA_HEADS = 8
MLA_NOPE = 64
MLA_ROPE = 32
MLA_V = 64
Q_LORA = 384
KV_LORA = 256
ROPE_THETA = 10000.0
Q_BLOCK = 128
DIL_HEADS = 8
DIL_PATTERNS = ((128, 1), (512, 4), (2048, 16))
DIL_BLOCK = max(w // d for (w, d) in DIL_PATTERNS)
MOBA_HEADS = 16
MOBA_BLOCK = 256
MOBA_TOPK = 3
MOBA_QCHUNK = 16
D_FF = 4 * D_MODEL
PLE_DIM = 256
N_EVEN = (DEPTH + 1) // 2
N_ODD = DEPTH // 2
EVEN_IN = Q_LORA + KV_LORA + MLA_ROPE + 3 * DIL_HEADS * HEAD_DIM
EVEN_MIX = MLA_HEADS * MLA_V + DIL_HEADS * HEAD_DIM
ODD_MIX = MOBA_HEADS * HEAD_DIM


def rms_norm(x, g):
    xf = x.astype(jnp.float32)
    y = xf * lax.rsqrt(jnp.mean(xf * xf, axis=-1, keepdims=True) + EPS)
    return (y * g.astype(jnp.float32)).astype(x.dtype)

def alibi_slopes(n):
    return 2.0 ** (-8.0 * jnp.arange(1, n + 1, dtype=jnp.float32) / n)

def apply_rope(x, positions):
    half = x.shape[-1] // 2
    inv_freq = ROPE_THETA ** (-jnp.arange(half, dtype=jnp.float32) / half)
    ang = positions.astype(jnp.float32)[..., None] * inv_freq
    ang = ang.reshape(ang.shape[:2] + (1,) * (x.ndim - 3) + (half,))
    cos, sin = jnp.cos(ang), jnp.sin(ang)
    xf = x.astype(jnp.float32)
    x1, x2 = xf[..., :half], xf[..., half:]
    return jnp.concatenate([x1 * cos - x2 * sin, x1 * sin + x2 * cos], axis=-1).astype(x.dtype)

def causal_attention_blocks(q, k, v, scale):
    B, S, H, Dk = q.shape
    nq = S // Q_BLOCK
    qb = q.reshape(B, nq, Q_BLOCK, H, Dk).swapaxes(0, 1)
    kpos = jnp.arange(S)

    def one(args):
        qi, i = args
        s = jnp.einsum('bqhd,bkhd->bhqk', qi, k, preferred_element_type=jnp.float32) * scale
        qpos = i * Q_BLOCK + jnp.arange(Q_BLOCK)
        s = jnp.where(kpos[None, :] <= qpos[:, None], s, -jnp.inf)
        pr = jax.nn.softmax(s, axis=-1).astype(v.dtype)
        return jnp.einsum('bhqk,bkhd->bqhd', pr, v)

    out = lax.map(one, (qb, jnp.arange(nq)))
    return out.swapaxes(0, 1).reshape(B, S, H, v.shape[-1])

def dilated_branch(q, k, v, slopes, scale, window, dil):
    B, S, H, Dh = q.shape
    L = S // dil
    nb = -(-L // DIL_BLOCK)
    Lp = nb * DIL_BLOCK
    reach = window // dil

    def to_class(a):
        a = a.reshape(B, L, dil, H, Dh).transpose(0, 2, 1, 3, 4)
        a = jnp.pad(a, ((0, 0), (0, 0), (0, Lp - L), (0, 0), (0, 0)))
        return a.reshape(B, dil, nb, DIL_BLOCK, H, Dh)

    def with_prev(a):
        prev = jnp.pad(a, ((0, 0), (0, 0), (1, 0), (0, 0), (0, 0), (0, 0)))[:, :, :nb]
        return jnp.concatenate([prev, a], axis=3)

    qc = to_class(q)
    kk = with_prev(to_class(k))
    vv = with_prev(to_class(v))
    s = jnp.einsum('bgnqhd,bgnkhd->bghnqk', qc, kk, preferred_element_type=jnp.float32) * scale
    qi = jnp.arange(DIL_BLOCK)[:, None]
    ki = jnp.arange(2 * DIL_BLOCK)[None, :]
    step = DIL_BLOCK + qi - ki
    key_idx = jnp.arange(nb)[:, None, None] * DIL_BLOCK - DIL_BLOCK + ki[None]
    mask = (step >= 0) & (step <= reach) & (key_idx >= 0)
    bias = slopes[:, None, None, None] * (step * dil).astype(jnp.float32)
    s = jnp.where(mask, s - bias, -jnp.inf)
    m = jnp.max(s, axis=-1, keepdims=True)
    e = jnp.exp(s - m)
    den = jnp.sum(e, axis=-1, keepdims=True)
    o = jnp.einsum('bghnqk,bgnkhd->bgnqhd', (e / den).astype(v.dtype), vv)
    lse = (m + jnp.log(den))[..., 0]
    o = o.reshape(B, dil, Lp, H, Dh)[:, :, :L].transpose(0, 2, 1, 3, 4).reshape(B, S, H, Dh)
    lse = lse.reshape(B, dil, H, Lp)[..., :L].transpose(0, 3, 1, 2).reshape(B, S, H)
    return o, lse

def dilated_attention(q, k, v, slopes, scale):
    outs, lses = [], []
    for (w, d) in DIL_PATTERNS:
        o, l = dilated_branch(q, k, v, slopes, scale, w, d)
        outs.append(o)
        lses.append(l)
    wts = jax.nn.softmax(jnp.stack(lses, axis=0), axis=0)
    out = jnp.einsum('pbsh,pbshd->bshd', wts, jnp.stack(outs, axis=0).astype(jnp.float32))
    return out.astype(q.dtype)

def moba_attention(q, k, v, slopes, scale):
    B, S, H, Dh = q.shape
    nb = -(-S // MOBA_BLOCK)
    Sp = nb * MOBA_BLOCK

    def to_blocks(a):
        a = jnp.pad(a, ((0, 0), (0, Sp - S), (0, 0), (0, 0)))
        return a.reshape(B, nb, MOBA_BLOCK, H, Dh).transpose(0, 3, 1, 2, 4)

    kb, vb = to_blocks(k), to_blocks(v)
    k_mean = jnp.mean(kb.astype(jnp.float32), axis=3)
    t = jnp.arange(S)
    own = t // MOBA_BLOCK
    gate = jnp.einsum('bshd,bhnd->bshn', q.astype(jnp.float32), k_mean)
    fully_past = jnp.arange(nb)[None, :] < own[:, None]
    gate = jnp.where(fully_past[None, :, None, :], gate, -jnp.inf)
    n_sel = min(MOBA_TOPK, nb)
    _, sel = lax.top_k(gate, n_sel)
    sel_ok = sel < own[None, :, None, None]
    nc = S // MOBA_QCHUNK

    def chunk(a):
        return a.reshape((B, nc, MOBA_QCHUNK) + a.shape[2:]).swapaxes(0, 1)

    b_ix = jnp.arange(B)[:, None, None, None]
    h_ix = jnp.arange(H)[None, None, :, None]
    k_in = jnp.arange(MOBA_BLOCK)
    n_sel_keys = n_sel * MOBA_BLOCK

    def one(args):
        qi, si, oki, ti = args
        ob = ti[0] // MOBA_BLOCK
        k_own = lax.dynamic_index_in_dim(kb, ob, axis=2, keepdims=False)
        v_own = lax.dynamic_index_in_dim(vb, ob, axis=2, keepdims=False)
        k_sel = kb[b_ix, h_ix, si]
        v_sel = vb[b_ix, h_ix, si]
        s_sel = jnp.einsum('bqhd,bqhjkd->bqhjk', qi, k_sel, preferred_element_type=jnp.float32) * scale
        s_own = jnp.einsum('bqhd,bhkd->bqhk', qi, k_own, preferred_element_type=jnp.float32) * scale
        d_sel = (ti[None, :, None, None, None] - (si[..., None] * MOBA_BLOCK + k_in)).astype(jnp.float32)
        s_sel = jnp.where(oki[..., None], s_sel - slopes[:, None, None] * d_sel, -jnp.inf)
        d_own = ti[:, None] - (ob * MOBA_BLOCK + k_in)[None, :]
        s_own = jnp.where((d_own >= 0)[None, :, None, :],
                          s_own - slopes[None, None, :, None] * d_own.astype(jnp.float32)[None, :, None, :],
                          -jnp.inf)
        s_all = jnp.concatenate([s_sel.reshape(s_sel.shape[:3] + (n_sel_keys,)), s_own], axis=-1)
        probs = jax.nn.softmax(s_all, axis=-1).astype(v.dtype)
        p_sel = probs[..., :n_sel_keys].reshape(s_sel.shape)
        p_own = probs[..., n_sel_keys:]
        return (jnp.einsum('bqhjk,bqhjkd->bqhd', p_sel, v_sel)
                + jnp.einsum('bqhk,bhkd->bqhd', p_own, v_own))

    out = lax.map(one, (chunk(q), chunk(sel), chunk(sel_ok), t.reshape(nc, MOBA_QCHUNK)))
    return out.swapaxes(0, 1).reshape(B, S, H, Dh)

def even_mixer(hn, positions, w_in, cq_norm, ckv_norm, w_uq, w_ukv, qn_nope, qn_rope,
               kn_nope, kn_rope, dil_qn, dil_kn, w_out):
    B, S, _ = hn.shape
    z = hn @ w_in
    o1 = Q_LORA
    o2 = o1 + KV_LORA
    o3 = o2 + MLA_ROPE
    dw = DIL_HEADS * HEAD_DIM
    c_q = rms_norm(z[..., :o1], cq_norm)
    c_kv = rms_norm(z[..., o1:o2], ckv_norm)
    q = (c_q @ w_uq).reshape(B, S, MLA_HEADS, MLA_NOPE + MLA_ROPE)
    q_nope = rms_norm(q[..., :MLA_NOPE], qn_nope)
    q_rope = apply_rope(rms_norm(q[..., MLA_NOPE:], qn_rope), positions)
    kv = (c_kv @ w_ukv).reshape(B, S, MLA_HEADS, MLA_NOPE + MLA_V)
    k_nope = rms_norm(kv[..., :MLA_NOPE], kn_nope)
    v_a = kv[..., MLA_NOPE:]
    k_rope = apply_rope(rms_norm(z[..., o2:o3], kn_rope), positions)
    k_rope = jnp.broadcast_to(k_rope[:, :, None, :], (B, S, MLA_HEADS, MLA_ROPE))
    q_a = jnp.concatenate([q_nope, q_rope], axis=-1)
    k_a = jnp.concatenate([k_nope, k_rope], axis=-1)
    out_a = causal_attention_blocks(q_a, k_a, v_a, (MLA_NOPE + MLA_ROPE) ** -0.5)
    q_b = rms_norm(z[..., o3:o3 + dw].reshape(B, S, DIL_HEADS, HEAD_DIM), dil_qn)
    k_b = rms_norm(z[..., o3 + dw:o3 + 2 * dw].reshape(B, S, DIL_HEADS, HEAD_DIM), dil_kn)
    v_b = z[..., o3 + 2 * dw:o3 + 3 * dw].reshape(B, S, DIL_HEADS, HEAD_DIM)
    out_b = dilated_attention(q_b, k_b, v_b, alibi_slopes(DIL_HEADS), HEAD_DIM ** -0.5)
    mixed = jnp.concatenate([out_a.reshape(B, S, MLA_HEADS * MLA_V),
                             out_b.reshape(B, S, dw)], axis=-1)
    return mixed @ w_out

def odd_mixer(hn, w_in, qn, kn, w_out):
    B, S, _ = hn.shape
    z = (hn @ w_in).reshape(B, S, 3, MOBA_HEADS, HEAD_DIM)
    q = rms_norm(z[:, :, 0], qn)
    k = rms_norm(z[:, :, 1], kn)
    v = z[:, :, 2]
    o = moba_attention(q, k, v, alibi_slopes(MOBA_HEADS), HEAD_DIM ** -0.5)
    return o.reshape(B, S, ODD_MIX) @ w_out

def first_inputs(seed: int = 0) -> dict:
    key = jax.random.key(seed)
    ks = iter(jax.random.split(key, 32))

    def w(shape, fan_in):
        return jax.random.normal(next(ks), shape, jnp.float32) * (fan_in ** -0.5)

    def gain(shape):
        return 1.0 + 0.05 * jax.random.normal(next(ks), shape, jnp.float32)

    x = jax.random.normal(next(ks), (BATCH, SEQ, D_MODEL), jnp.float32)
    p = jax.random.normal(next(ks), (DEPTH, BATCH, SEQ, PLE_DIM), jnp.float32)
    positions = jnp.broadcast_to(jnp.arange(SEQ, dtype=jnp.int32), (BATCH, SEQ))
    return {
        'x': x,
        'p': p,
        'positions': positions,
        'e_w_in': w((N_EVEN, D_MODEL, EVEN_IN), D_MODEL),
        'e_cq_norm': gain((N_EVEN, Q_LORA)),
        'e_ckv_norm': gain((N_EVEN, KV_LORA)),
        'e_w_uq': w((N_EVEN, Q_LORA, MLA_HEADS * (MLA_NOPE + MLA_ROPE)), Q_LORA),
        'e_w_ukv': w((N_EVEN, KV_LORA, MLA_HEADS * (MLA_NOPE + MLA_V)), KV_LORA),
        'e_qn_nope': gain((N_EVEN, MLA_NOPE)),
        'e_qn_rope': gain((N_EVEN, MLA_ROPE)),
        'e_kn_nope': gain((N_EVEN, MLA_NOPE)),
        'e_kn_rope': gain((N_EVEN, MLA_ROPE)),
        'e_dil_qn': gain((N_EVEN, HEAD_DIM)),
        'e_dil_kn': gain((N_EVEN, HEAD_DIM)),
        'e_w_out': w((N_EVEN, EVEN_MIX, D_MODEL), EVEN_MIX),
        'o_w_in': w((N_ODD, D_MODEL, 3 * ODD_MIX), D_MODEL),
        'o_qn': gain((N_ODD, HEAD_DIM)),
        'o_kn': gain((N_ODD, HEAD_DIM)),
        'o_w_out': w((N_ODD, ODD_MIX, D_MODEL), ODD_MIX),
        'mix_norm': gain((DEPTH, D_MODEL)),
        'ff_norm': gain((DEPTH, D_MODEL)),
        'w_ff1': w((DEPTH, D_MODEL, D_FF), D_MODEL),
        'w_ff2': w((DEPTH, D_FF, D_MODEL), D_FF),
        'ple_norm': gain((DEPTH, D_MODEL)),
        'w_ple_gate': w((DEPTH, D_MODEL, D_MODEL), D_MODEL),
        'w_ple_proj': w((DEPTH, PLE_DIM, D_MODEL), PLE_DIM),
    }

def first_block(x, p, positions, e_w_in, e_cq_norm, e_ckv_norm, e_w_uq, e_w_ukv, e_qn_nope,
              e_qn_rope, e_kn_nope, e_kn_rope, e_dil_qn, e_dil_kn, e_w_out, o_w_in, o_qn,
              o_kn, o_w_out, mix_norm, ff_norm, w_ff1, w_ff2, ple_norm, w_ple_gate, w_ple_proj):
    h = x
    for i in range(DEPTH):
        j = i // 2
        hn = rms_norm(h, mix_norm[i])
        if i % 2 == 0:
            mix = even_mixer(hn, positions, e_w_in[j], e_cq_norm[j], e_ckv_norm[j], e_w_uq[j],
                             e_w_ukv[j], e_qn_nope[j], e_qn_rope[j], e_kn_nope[j], e_kn_rope[j],
                             e_dil_qn[j], e_dil_kn[j], e_w_out[j])
        else:
            mix = odd_mixer(hn, o_w_in[j], o_qn[j], o_kn[j], o_w_out[j])
        h = h + mix
        u = jax.nn.relu(rms_norm(h, ff_norm[i]) @ w_ff1[i])
        h = h + (u * u) @ w_ff2[i]
        g = jax.nn.sigmoid(rms_norm(h, ple_norm[i]) @ w_ple_gate[i])
        h = h + g * (p[i] @ w_ple_proj[i])
    return h


GRID_W = 64
CTX_LEN = 256
CONV_W = 1024
CONV_K = 3
N_HEADS = 8
N_KV_HEADS = 2
HEAD_DIM_2 = 128
GROUP = N_HEADS // N_KV_HEADS
ROPE_AXIS_DIM = HEAD_DIM_2 // 2
ROPE_PAIRS = ROPE_AXIS_DIM // 2
ATTN_SCALE = HEAD_DIM_2 ** -0.5
GLA_HEADS = 4
GLA_DK = D_MODEL // 2
GLA_DV = D_MODEL
GLA_DKH = GLA_DK // GLA_HEADS
GLA_DVH = GLA_DV // GLA_HEADS
GLA_RANK = 16
GLA_TAU = 16.0
GLA_CHUNK = 64
N_BRANCH = 3

IN_SPLITS = (CONV_W, CONV_W, CONV_W, CONV_W,
             N_HEADS * HEAD_DIM_2, N_KV_HEADS * HEAD_DIM_2, N_KV_HEADS * HEAD_DIM_2,
             N_HEADS * HEAD_DIM_2,
             GLA_DK, GLA_DK, GLA_DV, GLA_RANK, GLA_RANK, GLA_DV,
             N_BRANCH * D_MODEL)
IN_WIDTH = sum(IN_SPLITS)


def _rmsnorm(x, g):
    xf = x.astype(jnp.float32)
    y = xf * lax.rsqrt(jnp.mean(xf * xf, axis=-1, keepdims=True) + EPS)
    return (y * g.astype(jnp.float32)).astype(x.dtype)

def _split_proj(p):
    offsets = np.cumsum(IN_SPLITS)[:-1].tolist()
    return jnp.split(p, offsets, axis=-1)

def _short_conv(u, w):
    up = jnp.pad(u, ((0, 0), (1, 1), (0, 0)))
    return w[0] * up[:, :-2] + w[1] * up[:, 1:-1] + w[2] * up[:, 2:]

def _axial_rope_tables(n_tokens):
    n_rows = n_tokens // GRID_W
    row = jnp.repeat(jnp.arange(n_rows, dtype=jnp.float32), GRID_W)
    col = jnp.tile(jnp.arange(GRID_W, dtype=jnp.float32), n_rows)
    freqs = ROPE_THETA ** (-jnp.arange(ROPE_PAIRS, dtype=jnp.float32) * 2.0 / ROPE_AXIS_DIM)
    ang = jnp.stack([row[:, None] * freqs, col[:, None] * freqs], axis=1)
    return jnp.cos(ang), jnp.sin(ang)

def _apply_rope(x, cos, sin):
    b_, t_, h_, _ = x.shape
    xr = x.reshape(b_, t_, h_, 2, 2, ROPE_PAIRS)
    x1, x2 = xr[..., 0, :], xr[..., 1, :]
    c_, s_ = cos[None, :, None], sin[None, :, None]
    out = jnp.stack([x1 * c_ - x2 * s_, x2 * c_ + x1 * s_], axis=-2)
    return out.reshape(b_, t_, h_, HEAD_DIM_2).astype(x.dtype)

def _attn_heads(q, k, v, q_g, k_g, rope):
    b_, t_ = q.shape[:2]
    q = _rmsnorm(q.reshape(b_, t_, N_HEADS, HEAD_DIM_2), q_g)
    k = _rmsnorm(k.reshape(b_, t_, N_KV_HEADS, HEAD_DIM_2), k_g)
    v = v.reshape(b_, t_, N_KV_HEADS, HEAD_DIM_2)
    if rope is not None:
        q = _apply_rope(q, *rope)
        k = _apply_rope(k, *rope)
    return q, k, v

def _sdpa_blocks(q, keys, vals):
    b_, t_ = q.shape[:2]
    nb = t_ // Q_BLOCK
    qb = q.reshape(b_, nb, Q_BLOCK, N_KV_HEADS, GROUP, HEAD_DIM_2).transpose(1, 0, 2, 3, 4, 5)

    def one_block(qblk):
        s = jnp.einsum('bqkgd,bskd->bkgqs', qblk, keys).astype(jnp.float32) * ATTN_SCALE
        p = jax.nn.softmax(s, axis=-1).astype(vals.dtype)
        return jnp.einsum('bkgqs,bskd->bqkgd', p, vals)

    o = lax.map(one_block, qb)
    return o.transpose(1, 0, 2, 3, 4, 5).reshape(b_, t_, N_HEADS * HEAD_DIM_2)

def _gla_inputs(q, k, v, r_f, r_b, w_df, b_df, w_db, b_db):
    b_, t_ = q.shape[:2]
    q = q.reshape(b_, t_, GLA_HEADS, GLA_DKH) * (GLA_DKH ** -0.5)
    k = k.reshape(b_, t_, GLA_HEADS, GLA_DKH)
    v = v.reshape(b_, t_, GLA_HEADS, GLA_DVH)
    la_f = (jax.nn.log_sigmoid((r_f @ w_df + b_df).astype(jnp.float32)) / GLA_TAU).reshape(b_, t_, GLA_HEADS, GLA_DKH)
    la_b = (jax.nn.log_sigmoid((r_b @ w_db + b_db).astype(jnp.float32)) / GLA_TAU).reshape(b_, t_, GLA_HEADS, GLA_DKH)
    return q, k, v, la_f, la_b

def _gla_scan(q, k, v, log_a, s0):
    b_, t_, h_, _ = q.shape
    dv = v.shape[-1]
    nc = t_ // GLA_CHUNK

    def chunks(a):
        return a.astype(jnp.float32).reshape(b_, nc, GLA_CHUNK, h_, a.shape[-1]).transpose(1, 0, 3, 2, 4)

    mask = jnp.tril(jnp.ones((GLA_CHUNK, GLA_CHUNK), dtype=bool))

    def step(s, inp):
        qc, kc, vc, ac = inp
        bcum = jnp.cumsum(ac, axis=2)
        o_inter = jnp.einsum('bhtd,bhde->bhte', qc * jnp.exp(bcum), s)
        diff = bcum[:, :, :, None, :] - bcum[:, :, None, :, :]
        decay = jnp.exp(jnp.where(mask[:, :, None], diff, -jnp.inf))
        att = jnp.einsum('bhtd,bhsd,bhtsd->bhts', qc, kc, decay)
        o_intra = jnp.einsum('bhts,bhse->bhte', att, vc)
        b_last = bcum[:, :, -1:, :]
        s_new = jnp.exp(b_last[:, :, 0, :])[..., None] * s + jnp.einsum('bhsd,bhse->bhde', kc * jnp.exp(b_last - bcum), vc)
        return s_new, o_inter + o_intra

    s_f, o = lax.scan(step, s0, (chunks(q), chunks(k), chunks(v), chunks(log_a)))
    o = o.transpose(1, 0, 3, 2, 4).reshape(b_, t_, h_, dv)
    return o.astype(v.dtype), s_f

def _flip(a):
    return jnp.flip(a, axis=1)

def _gla_bidirectional(ctx_in, lat_in):
    qc, kc, vc, lfc, lbc = ctx_in
    ql, kl, vl, lfl, lbl = lat_in
    s0 = jnp.zeros((qc.shape[0], GLA_HEADS, GLA_DKH, GLA_DVH), jnp.float32)
    o_cf, s_f = _gla_scan(qc, kc, vc, lfc, s0)
    o_cb, s_b = _gla_scan(_flip(qc), _flip(kc), _flip(vc), _flip(lbc), s0)
    o_lf, _ = _gla_scan(ql, kl, vl, lfl, s_f)
    o_lb, _ = _gla_scan(_flip(ql), _flip(kl), _flip(vl), _flip(lbl), s_b)
    return o_lf + _flip(o_lb), o_cf + _flip(o_cb)

def _mixer_output(parts, att_o, gla_o, conv_w_l, gla_g_l, w_br_conv_l, w_br_attn_l, w_br_gla_l, b_gate_l, w_out_l):
    a_b, a_c, a_x, a_z = parts[0], parts[1], parts[2], parts[3]
    z_attn, z_gla, mg = parts[7], parts[13], parts[14]
    b_, t_ = a_b.shape[:2]
    br_a = ((a_b * _short_conv(a_c * a_x, conv_w_l)) * jax.nn.silu(a_z)) @ w_br_conv_l
    br_b = (att_o * jax.nn.silu(z_attn)) @ w_br_attn_l
    br_c = (_rmsnorm(gla_o, gla_g_l).reshape(b_, t_, GLA_DV) * jax.nn.silu(z_gla)) @ w_br_gla_l
    g_a, g_b, g_c = jnp.split(jax.nn.sigmoid(mg + b_gate_l), N_BRANCH, axis=-1)
    return (g_a * br_a + g_b * br_b + g_c * br_c) @ w_out_l

def second_inputs(seed: int = 0) -> dict:
    key = jax.random.key(seed)
    ks = jax.random.split(key, 24)
    n = jax.random.normal
    f32 = jnp.float32
    return {
        "x": n(ks[0], (BATCH, SEQ, D_MODEL), f32),
        "c": n(ks[1], (BATCH, D_MODEL), f32),
        "ctx": n(ks[2], (BATCH, CTX_LEN, D_MODEL), f32),
        "c_ctx": n(ks[3], (D_MODEL,), f32),
        "w_ada": n(ks[4], (DEPTH, D_MODEL, 3 * D_MODEL), f32) * D_MODEL ** -0.5,
        "b_ada": 0.02 * n(ks[5], (DEPTH, 3 * D_MODEL), f32),
        "g_pre": 1.0 + 0.02 * n(ks[6], (DEPTH, D_MODEL), f32),
        "g_post": 1.0 + 0.02 * n(ks[7], (DEPTH, D_MODEL), f32),
        "w_in": n(ks[8], (DEPTH, D_MODEL, IN_WIDTH), f32) * D_MODEL ** -0.5,
        "conv_w": n(ks[9], (DEPTH, CONV_K, CONV_W), f32) * CONV_K ** -0.5,
        "q_norm_g": 1.0 + 0.02 * n(ks[10], (DEPTH, HEAD_DIM_2), f32),
        "k_norm_g": 1.0 + 0.02 * n(ks[11], (DEPTH, HEAD_DIM_2), f32),
        "w_decay_fwd": n(ks[12], (DEPTH, GLA_RANK, GLA_DK), f32) * GLA_RANK ** -0.5,
        "b_decay_fwd": 0.01 * n(ks[13], (DEPTH, GLA_DK), f32),
        "w_decay_bwd": n(ks[14], (DEPTH, GLA_RANK, GLA_DK), f32) * GLA_RANK ** -0.5,
        "b_decay_bwd": 0.01 * n(ks[15], (DEPTH, GLA_DK), f32),
        "gla_norm_g": 1.0 + 0.02 * n(ks[16], (DEPTH, GLA_DVH), f32),
        "w_br_conv": n(ks[17], (DEPTH, CONV_W, D_MODEL), f32) * CONV_W ** -0.5,
        "w_br_attn": n(ks[18], (DEPTH, N_HEADS * HEAD_DIM_2, D_MODEL), f32) * (N_HEADS * HEAD_DIM_2) ** -0.5,
        "w_br_gla": n(ks[19], (DEPTH, GLA_DV, D_MODEL), f32) * GLA_DV ** -0.5,
        "b_gate": 0.02 * n(ks[20], (DEPTH, N_BRANCH * D_MODEL), f32),
        "w_out": n(ks[21], (DEPTH, D_MODEL, D_MODEL), f32) * D_MODEL ** -0.5,
    }

def second_block(x, c, ctx, c_ctx, w_ada, b_ada, g_pre, g_post, w_in, conv_w, q_norm_g, k_norm_g,
              w_decay_fwd, b_decay_fwd, w_decay_bwd, b_decay_bwd, gla_norm_g,
              w_br_conv, w_br_attn, w_br_gla, b_gate, w_out):
    n_tok = x.shape[1]
    rope = _axial_rope_tables(n_tok)
    xc = ctx
    for l in range(DEPTH):
        last = l == DEPTH - 1
        mod_l = jax.nn.silu(c) @ w_ada[l] + b_ada[l]
        sh_l, sc_l, gt_l = jnp.split(mod_l[:, None, :], 3, axis=-1)
        mod_c = jax.nn.silu(c_ctx) @ w_ada[l] + b_ada[l]
        sh_c, sc_c, gt_c = jnp.split(mod_c, 3, axis=-1)
        h_l = _rmsnorm(x, g_pre[l]) * (1.0 + sc_l) + sh_l
        h_c = _rmsnorm(xc, g_pre[l]) * (1.0 + sc_c) + sh_c
        pl = _split_proj(h_l @ w_in[l])
        pc = _split_proj(h_c @ w_in[l])
        q_l, k_l, v_l = _attn_heads(pl[4], pl[5], pl[6], q_norm_g[l], k_norm_g[l], rope)
        q_c, k_c, v_c = _attn_heads(pc[4], pc[5], pc[6], q_norm_g[l], k_norm_g[l], None)
        keys = jnp.concatenate([k_l, k_c], axis=1)
        vals = jnp.concatenate([v_l, v_c], axis=1)
        att_l = _sdpa_blocks(q_l, keys, vals)
        dec = (w_decay_fwd[l], b_decay_fwd[l], w_decay_bwd[l], b_decay_bwd[l])
        gla_c_in = _gla_inputs(pc[8], pc[9], pc[10], pc[11], pc[12], *dec)
        gla_l_in = _gla_inputs(pl[8], pl[9], pl[10], pl[11], pl[12], *dec)
        gla_l, gla_c = _gla_bidirectional(gla_c_in, gla_l_in)
        shared = (conv_w[l], gla_norm_g[l], w_br_conv[l], w_br_attn[l], w_br_gla[l], b_gate[l], w_out[l])
        out_l = _mixer_output(pl, att_l, gla_l, *shared)
        if not last:
            att_c = _sdpa_blocks(q_c, k_c, v_c)
            out_c = _mixer_output(pc, att_c, gla_c, *shared)
            xc = xc + gt_c * _rmsnorm(out_c, g_post[l])
        x = x + gt_l * _rmsnorm(out_l, g_post[l])
    return x


def setup_inputs(seed=0):
    out = dict(first_inputs(seed))
    for name, value in second_inputs(seed + 1).items():
        if name != "x":
            out[name + "_2"] = value
    return out


def reference(
    x, p, positions, e_w_in, e_cq_norm, e_ckv_norm, e_w_uq, e_w_ukv, e_qn_nope, e_qn_rope,
    e_kn_nope, e_kn_rope, e_dil_qn, e_dil_kn, e_w_out, o_w_in, o_qn, o_kn, o_w_out, mix_norm,
    ff_norm, w_ff1, w_ff2, ple_norm, w_ple_gate, w_ple_proj, c_2, ctx_2, c_ctx_2, w_ada_2,
    b_ada_2, g_pre_2, g_post_2, w_in_2, conv_w_2, q_norm_g_2, k_norm_g_2, w_decay_fwd_2,
    b_decay_fwd_2, w_decay_bwd_2, b_decay_bwd_2, gla_norm_g_2, w_br_conv_2, w_br_attn_2,
    w_br_gla_2, b_gate_2, w_out_2,
):
    x = first_block(
        x, p, positions, e_w_in, e_cq_norm, e_ckv_norm, e_w_uq, e_w_ukv, e_qn_nope, e_qn_rope,
        e_kn_nope, e_kn_rope, e_dil_qn, e_dil_kn, e_w_out, o_w_in, o_qn, o_kn, o_w_out,
        mix_norm, ff_norm, w_ff1, w_ff2, ple_norm, w_ple_gate, w_ple_proj,
    )
    return second_block(
        x, c_2, ctx_2, c_ctx_2, w_ada_2, b_ada_2, g_pre_2, g_post_2, w_in_2, conv_w_2,
        q_norm_g_2, k_norm_g_2, w_decay_fwd_2, b_decay_fwd_2, w_decay_bwd_2, b_decay_bwd_2,
        gla_norm_g_2, w_br_conv_2, w_br_attn_2, w_br_gla_2, b_gate_2, w_out_2,
    )


_drawn_inputs = setup_inputs


def setup_inputs(seed=0):
    import zlib

    import numpy as np

    out = dict(_drawn_inputs(seed))
    spreads = {}
    factors = {'e_cq_norm': 8.0,
     'e_ckv_norm': 5.026,
     'e_qn_nope': 8.0,
     'e_qn_rope': 8.0,
     'e_kn_nope': 8.0,
     'e_kn_rope': 8.0,
     'e_dil_qn': 5.114,
     'e_dil_kn': 5.759,
     'o_qn': 7.651,
     'o_kn': 5.922,
     'ple_norm': 6.004,
     'g_pre_2': 3.747,
     'g_post_2': 7.265,
     'q_norm_g_2': 200.0,
     'k_norm_g_2': 200.0,
     'b_decay_fwd_2': 64.0,
     'b_decay_bwd_2': 64.0,
     'gla_norm_g_2': 200.0,
     'b_gate_2': 8.0}
    for name, (base, spread) in spreads.items():
        noise = np.random.default_rng([zlib.crc32(name.encode()), seed]).standard_normal(out[name].shape)
        drawn = base * np.exp(spread * noise) if base else spread * noise
        out[name] = jnp.asarray(drawn.astype(out[name].dtype))
    for name, factor in factors.items():
        out[name] = (out[name] * factor).astype(out[name].dtype)
    return out
```

```python
from contextlib import ExitStack, contextmanager

import concourse.bass as bass
from concourse import mybir

F32 = mybir.dt.float32
F32R = mybir.dt.float32r
I32 = mybir.dt.int32
ALU = mybir.AluOpType
ACT = mybir.ActivationFunctionType
AX = mybir.AxisListType.X

P = 128
D = 1024
KC = D // P
S = 256
NT = S // P
EPS = 1e-6
RSQRT_SEED = float(0x5F3759DF)
BLK = 512
SLOTS = 4
UNIT = 1024
STD = [(2, BLK)] * SLOTS

Q_LORA, KV_LORA, ROPE, NOPE, HD = 384, 256, 32, 64, 64
O_KV, O_ROPE, O_DIL = Q_LORA, Q_LORA + KV_LORA, Q_LORA + KV_LORA + ROPE
HEADS_E, HEADS_O = 8, 16
DIL_W = HEADS_E * HD
EVEN_IN = O_DIL + 3 * DIL_W
ODD_W = HEADS_O * HD
MLA_D = NOPE + ROPE
MLA_SCALE = MLA_D ** -0.5
HD_SCALE = HD ** -0.5
KEYS = P + S


class Tally:

    def __init__(self):
        self.base, self.i = {}, None

    def now(self, sem):
        v = self.base.get(sem.name, 0)
        return v if self.i is None or sem.name not in self.per else v + self.i * self.per[sem.name]

    def next(self, sem, n=1):
        self.base[sem.name] = self.base.get(sem.name, 0) + n
        assert self.i is None or sem.name in self.per, f"{sem.name} counts in a loop"
        return self.now(sem)

    @contextmanager
    def loop(self, eng, n, per):
        start = dict(self.base)
        with eng.Fori(0, n, 1) as i:
            self.i, self.per = i, {s.name: k for s, k in per.items()}
            yield i
        for name, k in self.per.items():
            got = self.base.get(name, 0) - start.get(name, 0)
            assert got == k, f"{name}: {got} per iteration, {k} stated"
            self.base[name] = start.get(name, 0) + n * k
        self.i = None


def layout(sizes):
    at, out = 0, {}
    for name, n in sizes:
        out[name] = (at, n)
        at += n
    return out, at


COLS, NCOLS = layout([
    ("mix_norm", 2 * KC), ("ff_norm", 2 * KC), ("ple_norm", 2 * KC), ("e_cq_norm", 3), ("e_ckv_norm", 2),
    ("e_qn_nope", 1), ("e_kn_nope", 1), ("e_dil_qn", 1), ("e_dil_kn", 1), ("o_qn", 1), ("o_kn", 1),
    ("g_pre_2", 2 * KC), ("g_post_2", 2 * KC), ("b_ada_2", 6 * KC), ("conv_w_2", 6 * KC), ("b_gate_2", 6 * KC),
    ("gla_norm_g_2", 4), ("q_norm_g_2", 2), ("k_norm_g_2", 2), ("cond", 2 * KC)])
CONST, NCONST = layout([("ident", P), ("tri_f", P), ("tri_b", P), ("rot", P), ("ones", P), ("cos", S), ("sin", S)])
FIRST, NFIRST = layout([
    ("dist", KEYS), ("lncount", KEYS), ("causal", KEYS), ("inv_freq", ROPE // 2), ("dil_slope", HEADS_E),
    ("moba_slope", HEADS_O), ("inv_n_z", 3 + 2 * HEADS_E), ("inv_n_q", 3 * HEADS_E), ("rope_gains", 2 * ROPE)])
NSTAT_Z, NSTAT_Q = 3 + 2 * HEADS_E, 3 * HEADS_E


def weight_plan(io):
    def std(w, row=lambda i: 0, col=lambda i: 0):
        return [(w, (lambda i, row=row, c=c: row(i) + 2 * c * P), col, 2, BLK) for c in range(SLOTS)]

    def cols(w, blocks, c0=0):
        return (blocks // 2, [std(w, col=lambda i, h=h: c0 + i * 2 * BLK + h * BLK) for h in range(2)])

    def fixed(v):
        return lambda i: v

    segments = []
    e_in = io["e_w_in"][0]
    segments.append(("e_in",) + cols(e_in, 4))
    segments.append(("e_tail", 1, [[(e_in, fixed(2 * c * P), fixed(4 * BLK), 2, EVEN_IN - 4 * BLK) for c in range(SLOTS)]]))
    uq, ukv = io["e_w_uq"][0], io["e_w_ukv"][0]
    segments.append(("uq", 1, [[(uq, fixed(0), fixed(0), 2, BLK), (uq, fixed(2 * P), fixed(0), 1, BLK),
                                (uq, fixed(0), fixed(BLK), 2, BLK // 2), (uq, fixed(2 * P), fixed(BLK), 1, BLK // 2)]]))
    segments.append(("ukv", 1, [[(ukv, fixed(c * P), fixed(b * BLK), 1, BLK) for b in range(2) for c in range(2)]]))
    for layer in range(2):
        if layer:
            segments.append(("o_in",) + cols(io["o_w_in"][0], 6))
        segments.append((f"mix_out{layer}",) + cols(io["o_w_out" if layer else "e_w_out"][0], 2))
        ff1, ff2, proj = io["w_ff1"][layer], io["w_ff2"][layer], io["w_ple_proj"][layer]
        segments.append((f"ff{layer}", 4, [std(ff1, col=lambda i, h=h: i * D + h * BLK) for h in range(2)]
                         + [std(ff2, row=lambda i: i * D, col=fixed(h * BLK)) for h in range(2)]))
        segments.append((f"gate{layer}",) + cols(io["w_ple_gate"][layer], 2))
        segments.append((f"proj{layer}", 1, [[(proj, fixed(c * P), fixed(b * BLK), 1, BLK) for b in range(2) for c in range(2)]]))
    return segments


C_CONV_B, C_CONV_C, C_CONV_X, C_CONV_Z = 0, D, 2 * D, 3 * D
C_Q = 4 * D
AH, AKV, AD = 8, 2, 128
C_K = C_Q + AH * AD
C_V = C_K + AKV * AD
C_ZA = C_V + AKV * AD
GH, GDK, GDV, RANK = 4, 128, 256, 16
C_GQ = C_ZA + AH * AD
C_GK = C_GQ + GH * GDK
C_GV = C_GK + GH * GDK
C_R = C_GV + GH * GDV
C_ZG = C_R + 2 * RANK
C_MG = C_ZG + D
ATTN_SCALE = AD ** -0.5
TOK = 2 * S
TT = TOK // P
LEVELS = [P >> (n + 1) for n in range(7)]
TILES = {0: [2, 3, 0, 1], 1: [3, 2, 1, 0]}
NMASK = 2 * len(LEVELS) * (P // 2) + P


def second_plan(io):
    def std(w, c0=0, per=0, width=BLK):
        return [(w, (lambda i, c=c: 2 * c * P), (lambda i: c0 + i * per), 2, width) for c in range(SLOTS)]

    out = []
    for layer in range(2):
        w, n = io["w_in_2"][layer], layer

        def gated(name, b, br):
            return (f"{name}{n}", 1, [q for half in range(2) for q in
                                      (std(w, C_MG + b * D + half * BLK), std(br, half * BLK))])

        out += [
            (f"ada{n}", 6, [std(io["w_ada_2"][layer], 0, BLK)]),
            (f"gq{n}", 1, [std(w, C_GQ)]), (f"gk{n}", 1, [std(w, C_GK)]), (f"gr{n}", 1, [std(w, C_R, width=P)]),
            (f"gv{n}", 2, [std(w, C_GV, BLK)]), (f"zg{n}", 2, [std(w, C_ZG, BLK)]),
            gated("mgc", 2, io["w_br_gla_2"][layer]),
            (f"q{n}", 2, [std(w, C_Q, BLK)]), (f"k{n}", 1, [std(w, C_K, width=AKV * AD)]),
            (f"v{n}", 1, [std(w, C_V, width=AKV * AD)]), (f"za{n}", 2, [std(w, C_ZA, BLK)]),
            gated("mgb", 1, io["w_br_attn_2"][layer]),
            (f"conv{n}", 2, [std(w, c, BLK) for c in (C_CONV_B, C_CONV_C, C_CONV_X, C_CONV_Z)]),
            gated("mga", 0, io["w_br_conv_2"][layer]),
            (f"out{n}", 2, [std(io["w_out_2"][layer], 0, BLK)]),
        ]
    return out


def sizes(quad):
    return [(k, w) for _, _, _, k, w in quad]


def mixer_kernel(nc, io, out):
    plan = weight_plan(io) + second_plan(io)
    quads = [(name, q) for name, n, qs in plan for q in qs]

    with ExitStack() as ctx:
        def sb(name, shape, dt=F32):
            return ctx.enter_context(nc.sbuf_tensor(name, shape, dt))

        def sem(name):
            return ctx.enter_context(nc.semaphore(name))

        RAW = sb("RAW", [P, SLOTS, UNIT])
        WHI = sb("WHI", [P, SLOTS, UNIT], F32R)
        WLO = sb("WLO", [P, SLOTS, UNIT], F32R)
        ATH = sb("ATH", [P, KC, 2 * S], F32R)
        ATL = sb("ATL", [P, KC, 2 * S], F32R)
        COL = sb("COL", [P, NCOLS])
        CST = sb("CST", [P, NCONST])
        STAT = sb("STAT", [P, 256])
        h = sb("h", [P, NT, D])
        ARENA = sb("ARENA", [P, 19 * 1024])
        bank = [ctx.enter_context(nc.psum_tensor(f"bank{b}", [P, BLK], F32)) for b in range(8)]

        def col(name, i=0, rows=P):
            return COL[0:rows, COLS[name][0] + i:COLS[name][0] + i + 1]

        def cst(name):
            return CST[:, CONST[name][0]:CONST[name][0] + CONST[name][1]]

        ident = cst("ident")
        top = [0]

        def view(n):
            top[0] += n
            return ARENA[:, top[0] - n:top[0]]

        Z = view(NT * 3 * ODD_W)
        ze = Z[:, 0:NT * EVEN_IN].rearrange("p (t n) -> p t n", t=NT)
        zo = Z.rearrange("p (t n) -> p t n", t=NT)
        Q = view(NT * HEADS_E * MLA_D).rearrange("p (t n) -> p t n", t=NT)
        KV = view(NT * HEADS_E * (NOPE + HD)).rearrange("p (t n) -> p t n", t=NT)
        mixed = view(NT * D).rearrange("p (t n) -> p t n", t=NT)
        scaled = mixed
        STAGE = view(2 * 2 * NT * MLA_D).rearrange("p (b g d) -> p b g d", b=2, g=2 * NT)
        QKT = view(2 * 2 * S).rearrange("p (b n) -> p b n", b=2)
        PROB = view(2 * KEYS).rearrange("p (b n) -> p b n", b=2)
        PROBT = view(2 * KEYS).rearrange("p (b n) -> p b n", b=2)
        FST = view(NFIRST)
        VAL = view(KC * S).rearrange("p (c n) -> p c n", c=KC)
        PIN = view(NT * 256).rearrange("p (t n) -> p t n", t=NT)
        assert top[0] <= 19 * 1024, top[0]
        GATE = Z[:, 0:NT * D].rearrange("p (t n) -> p t n", t=NT)
        RELU = Z[:, 2 * D:2 * D + 2 * S].rearrange("p (b n) -> p b n", b=2)
        PVAL = Z[:, 2 * D:2 * D + 2 * S]
        SQU = Z[:, 2 * D + 2 * S:2 * D + 4 * S].rearrange("p (b n) -> p b n", b=2)
        TMP = Z[:, 3 * D:3 * D + BLK]
        PTMP = Q

        def fst(name):
            return FST[:, FIRST[name][0]:FIRST[name][0] + FIRST[name][1]]

        ss, rs, nt1 = STAT[:, 0:48], STAT[:, 48:96], STAT[:, 96:144]
        rs_z = STAT[:, 144:144 + 2 * NSTAT_Z].rearrange("p (t n) -> p t n", t=NT)
        NMAX = STAT[:, 182:186].rearrange("p (b t) -> p b t", b=2)
        DEN = STAT[:, 186:190].rearrange("p (b t) -> p b t", b=2)
        RDEN = STAT[:, 190:194].rearrange("p (b t) -> p b t", b=2)
        GQK = STAT[:, 194:197]
        POSF = STAT[:, 197:199]
        RSZO = sb("RSZO", [P, 2, NT, 2 * HEADS_O])
        POS = sb("POS", [P, NT], I32)
        TRIG = sb("TRIG", [P, 5, NT, ROPE // 2])
        KROPE = sb("KROPE", [P, NT, ROPE])
        QROPE = VAL[:, 4:6, :].rearrange("p t (h n) -> p t h n", h=HEADS_E)
        ROT = VAL[:, 6:8, :].rearrange("p c (b h n) -> p (c b) h n", b=2, h=HEADS_E)
        ZERO = sb("ZERO", [P, BLK])

        inputs_in = sem("inputs_in")
        p_in, p_used = sem("p_in"), sem("p_used")
        raw_landed = [sem(f"raw_landed{s}") for s in range(SLOTS)]
        hi_split, lo_split = sem("hi_split"), sem("lo_split")
        gemm_step = sem("gemm_step")
        bank_free = [sem(f"bank_free{b}") for b in range(4)]
        rows_ready = sem("rows_ready")
        turned = sem("turned")
        chunk_val = sem("chunk_val")
        at_ready = sem("at_ready")
        u_ready = sem("u_ready")
        relu_done = sem("relu_done")
        trig_ready, trig_done = sem("trig_ready"), sem("trig_done")
        staged, qk_turned, qk_ready = sem("staged"), sem("qk_turned"), sem("qk_ready")
        scored, max_ready, probs_ready = sem("scored"), sem("max_ready"), sem("probs_ready")
        probs_turned, probs_t_ready, head_out = sem("probs_turned"), sem("probs_t_ready"), sem("head_out")
        acc_open = sem("acc_open")
        gated = sem("gated")
        zeroed = sem("zeroed")
        stored = sem("stored")

        BTH = sb("BTH", [P, KC, TOK], F32R)
        BTL = sb("BTL", [P, KC, TOK], F32R)
        CTH, CTL = sb("CTH", [P, KC, 2], F32R), sb("CTL", [P, KC, 2], F32R)
        MOD = sb("MOD", [P, 3 * KC, 2])
        EBL = sb("EBL", [P, TT])
        CTMP = sb("CTMP", [P, 2 * KC])[:, :]
        TMPA = sb("TMPA", [P, 1])[:, :]
        one = cst("ones")[:, 0:1]

        def at(base, n, pattern=None, **kw):
            a = ARENA[:, base:base + n]
            return a.rearrange(pattern, **kw) if pattern else a

        xT = at(6144, KC * TOK, "p (c n) -> p c n", c=KC)
        CTXIN = at(4096, NT * D, "p (t n) -> p t n", t=NT)
        SQ2 = at(10240, 2 * TOK, "p (b n) -> p b n", b=2)
        RB, VB, TB = at(11264, TOK), at(11776, TOK), at(12288, TOK)
        W0 = at(12800, 2 * TOK, "p (b n) -> p b n", b=2)
        W1 = at(13824, 2 * TOK, "p (b n) -> p b n", b=2)
        VG = at(0, TT * D, "p (t n) -> p t n", t=TT)
        GQ = at(4096, GH * TOK)
        GK = at(10240, GH * TOK)
        RA = ARENA[0:2 * RANK + 1, 12288:12288 + TOK]
        LOGS, LA = at(12800, TOK), at(13312, TOK)
        QB = LOGS
        ON = at(12800, TT * GDV, "p (t n) -> p t n", t=TT)
        CUM = at(13824, TOK)
        DE = at(14336, 2 * TOK, "p (b n) -> p b n", b=2)
        QE = at(15360, TOK, "p (b n) -> p b n", b=2)
        KE = at(15872, 2 * TOK, "p (b n) -> p b n", b=2)
        KDT = at(16896, TOK)
        ATT = at(17408, 2 * TOK, "p (b n) -> p b n", b=2)
        STATE = at(18432, 3 * GDV, "p (b n) -> p b n", b=3)
        hflat = h.rearrange("p t n -> p (t n)")
        MASK = hflat[:, 0:NMASK].bitcast(I32)
        WD = h[0:2 * RANK + 1, 1, :].rearrange("p (d n) -> p d n", d=2)
        assert NMASK <= D
        Y = at(0, KC * TOK, "p (c n) -> p c n", c=KC)
        SIGZ = at(14336, 4 * TOK, "p (c n) -> p c n", c=4)
        WZ = at(16384, TOK)
        G = at(10240, 4 * TOK, "p (c n) -> p c n", c=4)
        WG = at(12288, TOK)
        VA = at(4096, TT * AKV * AD, "p (t n) -> p t n", t=TT)
        K2 = at(5120, AKV * TOK, "p (k n) -> p k n", k=AKV)
        QG = at(10240, (AH + AKV) * TOK)
        QS = at(15360, TOK)
        PL = at(15872, NT * TOK, "p (t n) -> p t n", t=NT)
        PC = at(16896, NT * S, "p (t n) -> p t n", t=NT)
        PLT = at(17408, TT * S, "p (s n) -> p s n", s=TT)
        PCT = at(18432, NT * S, "p (s n) -> p s n", s=NT)
        WA = at(18944, TOK)
        SIGA = at(15872, 4 * TOK, "p (c n) -> p c n", c=4)
        SQH = at(15872, 2 * TOK, "p (b n) -> p b n", b=2)
        DIAG = at(17408, TT * P, "p (t n) -> p t n", t=TT)
        AB = at(4096, 4 * TOK, "p (c n) -> p c n", c=4)
        AC = at(10240, 4 * TOK, "p (c n) -> p c n", c=4)
        PX = at(12288, 4 * TOK, "p (c n) -> p c n", c=4)
        CV = at(14336, 4 * TOK, "p (c n) -> p c n", c=4)
        SIGC = at(16384, 4 * TOK, "p (c n) -> p c n", c=4)
        WC = at(18432, TOK)
        OUT = at(14848, KC * TOK, "p (c n) -> p c n", c=KC)
        RSQ = STAT[:, 0:AH * TT + AKV * TT]
        RSV, RSW = STAT[:, 48:48 + 40], STAT[:, 96:96 + 40]
        SCL, NM, DN, RD = (STAT[:, 144 + 4 * n:148 + 4 * n] for n in range(4))
        GS, GR, GT = (STAT[:, 160 + 4 * n:164 + 4 * n] for n in range(3))

        ctx_in, mask_in, wd_in = sem("ctx_in"), sem("mask_in"), sem("wd_in")
        cond_sig, cond_ready, x_turned, x_ready = sem("cond_sig"), sem("cond_ready"), sem("x_turned"), sem("x_ready")
        sq_ready, sq_used = sem("sq_ready"), sem("sq_used")
        sig_done, bt_ready, inputs_ready = sem("sig_done"), sem("bt_ready"), sem("inputs_ready")
        g_pre, g_logs, g_la, g_cum, g_diff, g_exp = (sem(n) for n in ("g_pre", "g_logs", "g_la", "g_cum", "g_diff", "g_exp"))
        g_keys, g_kturned, g_kready, g_pair, g_level = (sem(n) for n in ("g_keys", "g_kturned", "g_kready", "g_pair", "g_level"))
        g_outer, g_state, g_att, g_out, g_rows, g_turned = (sem(n) for n in ("g_outer", "g_state", "g_att", "g_out", "g_rows", "g_turned"))
        a_heads, a_diag, a_bc, a_gain, a_rot, a_q, a_score = (sem(n) for n in ("a_heads", "a_diag", "a_bc", "a_gain", "a_rot", "a_q", "a_score"))
        a_max, a_exp, a_norm, a_turned, a_pt, a_out = (sem(n) for n in ("a_max", "a_exp", "a_norm", "a_turned", "a_pt", "a_out"))
        out_rows, x_split = sem("out_rows"), sem("x_split")

        block = ctx.enter_context(nc.Block())

        @block.sync
        def _(sp):
            T = Tally()

            def load_quad(quad, i):
                for slot, (w, row, column, k, width) in enumerate(quad):
                    src = w[bass.ds(row(i), k * P), bass.ds(column(i), width)].rearrange("(c p) n -> p c n", p=P)
                    sp.wait_ge(lo_split, T.next(lo_split))
                    sp.dma_start(RAW[:, slot, 0:k * width].rearrange("p (c n) -> p c n", c=k), src) \
                        .then_inc(raw_landed[slot], 16)

            for name, n, qs in plan:
                if n == 1:
                    for q in qs:
                        load_quad(q, 0)
                else:
                    with T.loop(sp, n, {lo_split: SLOTS * len(qs)}) as i:
                        for q in qs:
                            load_quad(q, i)
            for t in range(NT):
                sp.wait_ge(out_rows, 2 * (t + 1))
                sp.dma_start(out[0][t * P:(t + 1) * P, :], h[:, t, :]).then_inc(stored, 16)
            sp.wait_ge(stored, 16 * NT)

        @block.gpsimd
        def _(pool):
            T = Tally()
            nc.gpsimd.memset(ZERO[:, :], 0.0).then_inc(zeroed, 1)
            pool.sem_inc(lo_split, SLOTS)

            def lo_quad(quad):
                for slot, (k, width) in enumerate(quad):
                    pool.wait_ge(hi_split, T.next(hi_split))
                    n = k * width
                    nc.gpsimd.tensor_tensor(WLO[:, slot, 0:n], RAW[:, slot, 0:n], WHI[:, slot, 0:n], ALU.subtract) \
                        .then_inc(lo_split, 1)

            for name, n, qs in plan:
                if n == 1:
                    for q in qs:
                        lo_quad(sizes(q))
                else:
                    with T.loop(pool, n, {hi_split: SLOTS * len(qs)}):
                        for q in qs:
                            lo_quad(sizes(q))

        @block.scalar
        def _(act):
            T = Tally()
            act.dma_start(h[:, :, :], io["x"][0].rearrange("(t p) n -> p t n", p=P)).then_inc(inputs_in, 16)
            act.dma_start(CST[:, :], io["const"]).then_inc(inputs_in, 16)
            act.dma_start(COL[:, :], io["cols"]).then_inc(inputs_in, 16)
            act.dma_start(FST[:, :], io["first"]).then_inc(inputs_in, 16)
            act.dma_start(POS[:, :], io["pos"]).then_inc(inputs_in, 16)
            act.dma_start(PIN[:, :, :], io["p"][0, 0].rearrange("(t p) n -> p t n", p=P)).then_inc(p_in, 16)

            def hi_unit(slot, k, width):
                act.wait_ge(raw_landed[slot], T.next(raw_landed[slot], 16))
                n = k * width
                nc.scalar.activation(WHI[:, slot, 0:n], RAW[:, slot, 0:n], ACT.Copy).then_inc(hi_split, 1)

            def hi_quad(quad, steps, groups):
                for slot, (k, width) in enumerate(quad):
                    act.wait_ge(gemm_step, steps + (slot + 1) * groups)
                    hi_unit(slot, k, width)

            order = [sizes(q) for _, q in quads] + [None]

            def segment(name, groups, work=lambda j, base: None, per=None):
                at = [n for n, _ in quads].index(name)
                n, qs = next((n, qs) for s, n, qs in plan if s == name)

                def step(j, nxt):
                    base = T.now(gemm_step)
                    if nxt is not None:
                        hi_quad(nxt, base, groups[j])
                    T.next(gemm_step, SLOTS * groups[j])
                    work(j, base)

                after = order[at + len(qs)]
                loops = n if after == STD else n - 1
                if loops > 0:
                    counts = {gemm_step: SLOTS * sum(groups)} | {r: 16 * len(qs) for r in raw_landed} | (per or {})
                    with T.loop(act, loops, counts):
                        for j in range(len(qs)):
                            step(j, STD)
                for _ in range(n - loops):
                    for j in range(len(qs)):
                        step(j, order[at + j + 1])

            def chunks_out(count, gain):
                for g in range((count + 1) // 2):
                    act.wait_ge(turned, T.next(turned))
                    for c in range(2 * g, min(2 * g + 2, count)):
                        o = (c % 2) * S
                        last = nc.scalar.activation(VAL[:, c, :], bank[4 + g % 4][:, o:o + S], ACT.Copy,
                                                    scale=gain(c))
                    last.then_inc(chunk_val, 1)

            def heads(n, d, kind):
                def operands(par):
                    act.wait_ge(qk_turned, T.next(qk_turned))
                    nc.scalar.activation(QKT[0:d, par, 0:S], bank[par][0:d, 0:S], ACT.Copy)
                    nc.scalar.activation(QKT[0:d, par, S:2 * S], bank[par][0:d, S:2 * S], ACT.Copy,
                                         scale=GQK[0:d, kind:kind + 1]).then_inc(qk_ready, 1)

                def pair(ahead):
                    for par in range(2):
                        act.wait_ge(max_ready, T.next(max_ready))
                        for t in range(NT):
                            part = PROB[:, par, 0:P] if t == 0 else PROB[:, par, P:KEYS]
                            last = nc.scalar.activation(part, part, ACT.Exp, bias=NMAX[:, par, t:t + 1],
                                                        accum_out=DEN[:, par, t:t + 1])
                        last.then_inc(probs_ready, 1)
                    if ahead:
                        for par in range(2):
                            operands(par)
                    for par in range(2):
                        act.wait_ge(probs_turned, T.next(probs_turned))
                        nc.scalar.activation(PROBT[:, par, :], bank[4 + par][:, 0:KEYS], ACT.Copy) \
                            .then_inc(probs_t_ready, 1)

                for par in range(2):
                    operands(par)
                with T.loop(act, n // 2 - 1, {qk_turned: 2, max_ready: 2, probs_turned: 2}):
                    pair(True)
                pair(False)

            for slot, (k, width) in enumerate(STD):
                hi_unit(slot, k, width)
            act.wait_ge(trig_ready, 1)
            nc.scalar.activation(TRIG[:, 4, :, :], TRIG[:, 2, :, :], ACT.Sin)
            nc.scalar.activation(TRIG[:, 3, :, :], TRIG[:, 2, :, :], ACT.Sin, scale=0.5).then_inc(trig_done, 1)
            for layer in range(2):
                chunks_out(KC, lambda c: col("mix_norm", layer * KC + c))
                if layer == 0:
                    segment("e_in", [2, 2])
                    segment("e_tail", [2])
                    chunks_out(5, lambda c: col("e_cq_norm", c) if c < 3 else col("e_ckv_norm", c - 3))
                    segment("uq", [2])
                    segment("ukv", [2])
                    heads(HEADS_E, MLA_D, 0)
                    heads(HEADS_E, HD, 1)
                else:
                    segment("o_in", [2, 2])
                    heads(HEADS_O, HD, 2)
                chunks_out(KC, lambda c: 1.0)
                if layer:
                    act.dma_start(CTXIN, io["ctx_2"][0].rearrange("(t p) n -> p t n", p=P)).then_inc(ctx_in, 16)
                segment(f"mix_out{layer}", [2, 2])
                chunks_out(KC, lambda c: col("ff_norm", layer * KC + c))

                def relu(j, base):
                    if j < 2:
                        for c in range(4):
                            act.wait_ge(u_ready, T.next(u_ready))
                            act.wait_ge(gemm_step, base + 4 * (SLOTS - 1) + c + 1)
                            nc.scalar.activation(RELU[:, c % 2, :], bank[c][:, 0:S], ACT.Relu).then_inc(bank_free[c], 1)

                segment(f"ff{layer}", [4, 4, 2, 2], relu, {u_ready: 8})
                act.wait_ge(turned, T.next(turned))
                nc.scalar.activation(PVAL, bank[0][:, :], ACT.Copy).then_inc(chunk_val, 1)
                chunks_out(KC, lambda c: col("ple_norm", layer * KC + c))

                def sigmoid(j, base):
                    for t in range(NT):
                        act.wait_ge(gemm_step, base + NT * (SLOTS - 1) + t + 1)
                        nc.scalar.activation(GATE[:, t, j * BLK:(j + 1) * BLK], bank[2 * j + t][:, :], ACT.Sigmoid) \
                            .then_inc(bank_free[2 * j + t], 1)

                segment(f"gate{layer}", [2, 2], sigmoid)
                if layer == 0:
                    act.dma_start(PIN[:, :, :], io["p"][1, 0].rearrange("(t p) n -> p t n", p=P)).then_inc(p_in, 16)
                segment(f"proj{layer}", [2])
            act.wait_ge(x_turned, T.next(x_turned, 8))
            act.dma_start(MASK, io["mask"]).then_inc(mask_in, 16)

            def load_decay(layer):
                for d, name in enumerate(("fwd", "bwd")):
                    act.dma_start(WD[d * RANK:(d + 1) * RANK, d, :], io[f"w_decay_{name}_2"][layer]).then_inc(wd_in, 16)
                    act.dma_start(WD[2 * RANK:2 * RANK + 1, d, :], io[f"b_decay_{name}_2"][layer:layer + 1, :]).then_inc(wd_in, 16)

            act.wait_ge(inputs_ready, 1)
            load_decay(0)
            nc.scalar.activation(CTMP, COL[:, COLS["cond"][0]:COLS["cond"][0] + 2 * KC], ACT.Sigmoid).then_inc(cond_sig, 1)

            def square_chunks(src, when=None):
                for c in range(KC):
                    if when is not None and c in when:
                        act.wait_ge(*when[c])
                    if T.next(sq_ready) > 2:
                        act.wait_ge(sq_used, T.now(sq_ready) - 2)
                    w = TOK if when is None else tq
                    nc.scalar.activation(SQ2[:, c % 2, 0:w], src[:, c, 0:w], ACT.Square).then_inc(sq_ready, 1)

            for layer in range(2):
                tq = TOK if layer == 0 else S
                nq = tq // P
                act.wait_ge(x_ready, T.next(x_ready))
                square_chunks(xT)
                segment(f"ada{layer}", [4])
                segment(f"gq{layer}", [4])
                segment(f"gk{layer}", [4])
                segment(f"gr{layer}", [1])
                segment(f"gv{layer}", [4])

                def sigmoid_z(room):
                    def work(j, base):
                        for c in range(4):
                            act.wait_ge(gemm_step, base + 4 * (SLOTS - 1) + c + 1)
                            nc.scalar.activation(room[:, c, 0:tq], bank[c][:, 0:tq], ACT.Sigmoid).then_inc(sig_done, 1)
                    return work

                segment(f"zg{layer}", [4], sigmoid_z(SIGZ))

                def gla_dir(d):
                    act.wait_ge(g_pre, T.next(g_pre))
                    nc.scalar.activation(LOGS, bank[4][:, :], ACT.Abs)
                    act.drain()
                    nc.scalar.activation(LOGS, LOGS, ACT.Exp, scale=-1.0)
                    act.drain()
                    nc.scalar.activation(LOGS, LOGS, ACT.Ln, bias=one).then_inc(g_logs, 1)
                    act.wait_ge(g_diff, T.next(g_diff))
                    nc.scalar.activation(DE[:, 0, :], DE[:, 0, :], ACT.Exp)
                    end = CUM.rearrange("p (t n) -> p t n", t=TT)[:, :, P - 1 if d == 0 else 0]
                    nc.scalar.activation(EBL[:, :], end, ACT.Exp)
                    nc.scalar.activation(DE[:, 1, 0:tq], CUM[:, 0:tq], ACT.Exp).then_inc(g_exp, 1)
                    act.wait_ge(g_kturned, T.next(g_kturned))
                    nc.scalar.activation(KDT, bank[4][:, :], ACT.Copy).then_inc(g_kready, 1)
                    for n in range(len(LEVELS)):
                        act.wait_ge(g_diff, T.next(g_diff))
                        nc.scalar.activation(DE[:, n % 2, 0:tq], DE[:, n % 2, 0:tq], ACT.Exp).then_inc(g_exp, 1)

                with T.loop(act, GH, {g_pre: 2, g_diff: 2 * (1 + len(LEVELS)), g_kturned: 2}):
                    for d in range(2):
                        gla_dir(d)
                if layer == 0:
                    load_decay(1)

                def sigmoid_g(b):
                    def work(j, base):
                        if j % 2 == 0:
                            for c in range(4):
                                act.wait_ge(gemm_step, base + 4 * (SLOTS - 1) + c + 1)
                                nc.scalar.activation(G[:, c, 0:tq], bank[c][:, 0:tq], ACT.Sigmoid,
                                                     bias=col("b_gate_2", (layer * 3 + b) * KC + j // 2 * 4 + c)).then_inc(bank_free[c], 1)
                    return work

                segment(f"mgc{layer}", [4] * 4, sigmoid_g(2))
                segment(f"q{layer}", [4])
                segment(f"k{layer}", [2])
                segment(f"v{layer}", [4])
                segment(f"za{layer}", [4], sigmoid_z(SIGA))
                def square_head(src, par, w):
                    act.wait_ge(sq_used, T.next(sq_used))
                    nc.scalar.activation(SQH[:, par, 0:w], src, ACT.Square).then_inc(sq_ready, 1)

                act.wait_ge(a_heads, T.next(a_heads))
                T.base[sq_used.name] = T.base[sq_ready.name] - 2
                with T.loop(act, AH // 2, {sq_used: 2}) as i:
                    for par in range(2):
                        square_head(QG[:, bass.ds((i * 2 + par) * TOK, tq)], par, tq)
                for k in range(AKV):
                    square_head(QG[:, (AH + k) * TOK:(AH + k + 1) * TOK], k, TOK)
                T.next(sq_ready, AH + AKV)

                def attend():
                    act.wait_ge(a_max, T.next(a_max))
                    for t in range(nq):
                        if t < NT:
                            last = nc.scalar.activation(PL[:, t, :], bank[1 + t][:, :], ACT.Exp, bias=NM[:, t:t + 1],
                                                        scale=SCL[:, t:t + 1], accum_out=DN[:, t:t + 1])
                        else:
                            o = (t - NT) * S
                            last = nc.scalar.activation(PC[:, t - NT, :], bank[3][:, o:o + S], ACT.Exp, bias=NM[:, t:t + 1],
                                                        scale=SCL[:, t:t + 1], accum_out=DN[:, t:t + 1])
                    last.then_inc(a_exp, 1)
                    act.wait_ge(a_turned, T.next(a_turned))
                    for t in range(NT):
                        last = nc.scalar.activation(PLT[:, :, t * P:(t + 1) * P], bank[4 + t][:, :].rearrange("p (s n) -> p s n", s=TT), ACT.Copy)
                    if nq > NT:
                        for t in range(NT):
                            last = nc.scalar.activation(PCT[:, :, t * P:(t + 1) * P],
                                                        bank[6][:, t * S:(t + 1) * S].rearrange("p (s n) -> p s n", s=NT), ACT.Copy)
                    last.then_inc(a_pt, 1)

                for kv in range(AKV):
                    with T.loop(act, AH // AKV, {a_max: 1, a_turned: 1}):
                        attend()
                segment(f"mgb{layer}", [4] * 4, sigmoid_g(1))

                def conv_z(j, base):
                    if j == 3:
                        sigmoid_z(SIGC)(j, base)

                segment(f"conv{layer}", [4] * 4, conv_z)
                segment(f"mga{layer}", [4] * 4, sigmoid_g(0))
                segment(f"out{layer}", [4])
                act.wait_ge(x_split, T.next(x_split))
                square_chunks(OUT, {})

        @block.vector
        def _(dve):
            T = Tally()
            V = nc.vector
            drain = dve.drain

            def rsqrt(y, v, t):
                V.tensor_scalar(y.bitcast(I32), v.bitcast(I32), -0.5, RSQRT_SEED, ALU.mult, ALU.add)
                for _ in range(3):
                    drain()
                    V.tensor_tensor(t, y, y, ALU.mult)
                    drain()
                    V.scalar_tensor_tensor(t, t, -0.5, v, ALU.mult, ALU.mult)
                    drain()
                    V.scalar_tensor_tensor(y, t, 1.5, y, ALU.add, ALU.mult)
                drain()

            def norm_rows():
                for t in range(NT):
                    V.tensor_tensor_reduce(scaled[:, t, :], h[:, t, :], h[:, t, :], 1.0 / D, 0.0, ALU.mult, ALU.add,
                                           ss[:, t:t + 1])
                drain()
                V.tensor_scalar(ss[:, 0:NT], ss[:, 0:NT], EPS, None, ALU.add)
                drain()
                rsqrt(rs[:, 0:NT], ss[:, 0:NT], nt1[:, 0:NT])
                for t in range(NT):
                    V.tensor_scalar(scaled[:, t, :], h[:, t, :], rs[:, t:t + 1], None, ALU.mult).then_inc(rows_ready, 1)

            def chunks_split(count, tok=0, val=VAL):
                for g in range((count + 1) // 2):
                    c, e = 2 * g, min(2 * g + 2, count)
                    dve.wait_ge(chunk_val, T.next(chunk_val))
                    V.tensor_copy(ATH[:, c:e, tok:tok + S], val[:, c:e, :])
                    drain()
                    V.tensor_tensor(ATL[:, c:e, tok:tok + S], val[:, c:e, :], ATH[:, c:e, tok:tok + S], ALU.subtract) \
                        .then_inc(at_ready, 1)

            def block_done(base, before, units, t):
                dve.wait_ge(gemm_step, base + NT * (before + units - 1) + t + 1)

            def rows_out(dst, base, before, units, b, width=BLK, banks=0):
                for t in range(NT):
                    block_done(base, before, units, t)
                    V.tensor_copy(dst(t), bank[banks + t][:, 0:width]).then_inc(bank_free[banks + t], 1)
                    T.next(bank_free[banks + t])

            def add_rows(base, before, units, cols, banks):
                for t in range(NT):
                    block_done(base, before, units, t)
                    V.tensor_tensor(h[:, t, cols], h[:, t, cols], bank[banks + t][:, :], ALU.add) \
                        .then_inc(bank_free[banks + t], 1)
                    T.next(bank_free[banks + t])

            def blocks(n, out_block):
                with T.loop(dve, n // 2, {gemm_step: 2 * NT * SLOTS} | {b: 1 for b in bank_free}) as i:
                    for j in range(2):
                        base = T.now(gemm_step)
                        out_block(i * 2 * BLK + j * BLK, base, 2 * j)
                        T.next(gemm_step, NT * SLOTS)

            def bc(ap, n):
                return ap.to_broadcast([P, ap.shape[1], n])

            def rope(dst, t, heads):
                half = ROPE // 2
                x1, x2 = dst[:, :, 0:half], dst[:, :, half:ROPE]
                c, s = (TRIG[:, i, t:t + 1, :].to_broadcast([P, heads, half]) for i in (3, 4))
                r = [ROT[:, i, 0:heads, :] for i in range(4)]
                for o, a, b in zip(r, (x1, x2, x1, x2), (c, s, s, c)):
                    V.tensor_tensor(o, a, b, ALU.mult)
                drain()
                V.tensor_tensor(x1, r[0], r[1], ALU.subtract)
                V.tensor_tensor(x2, r[2], r[3], ALU.add)
                drain()

            def squares(src, n):
                o = scaled.rearrange("p t n -> p (t n)")[:, 0:n]
                V.tensor_tensor(o, src, src, ALU.mult)
                drain()
                return o

            def head_sums(dst, sq, d):
                V.tensor_reduce(dst, sq.rearrange("p (g d) -> p g d", d=d), AX, ALU.add)

            def even_norms_z():
                sums = ss[:, 0:2 * NSTAT_Z].rearrange("p (t n) -> p t n", t=NT)
                for t in range(NT):
                    sq = squares(ze[:, t, 0:O_DIL + 2 * DIL_W], O_DIL + 2 * DIL_W)
                    head_sums(sums[:, t, 0:1], sq[:, 0:O_KV], Q_LORA)
                    head_sums(sums[:, t, 1:2], sq[:, O_KV:O_ROPE], KV_LORA)
                    head_sums(sums[:, t, 2:3], sq[:, O_ROPE:O_DIL], ROPE)
                    head_sums(sums[:, t, 3:NSTAT_Z], sq[:, O_DIL:O_DIL + 2 * DIL_W], HD)
                    drain()
                    V.tensor_tensor(sums[:, t, :], sums[:, t, :], fst("inv_n_z"), ALU.mult)
                drain()
                flat = ss[:, 0:2 * NSTAT_Z]
                V.tensor_scalar(flat, flat, EPS, None, ALU.add)
                drain()
                rsqrt(STAT[:, 144:144 + 2 * NSTAT_Z], flat, nt1[:, 0:2 * NSTAT_Z])
                for t in range(NT):
                    V.tensor_scalar(ze[:, t, 0:O_KV], ze[:, t, 0:O_KV], rs_z[:, t, 0:1], None, ALU.mult)
                    V.tensor_scalar(ze[:, t, O_KV:O_ROPE], ze[:, t, O_KV:O_ROPE], rs_z[:, t, 1:2], None, ALU.mult) \
                        .then_inc(rows_ready, 1)
                for t in range(NT):
                    V.scalar_tensor_tensor(KROPE[:, t, :], ze[:, t, O_ROPE:O_DIL], rs_z[:, t, 2:3],
                                           fst("rope_gains")[:, ROPE:2 * ROPE], ALU.mult, ALU.mult)
                drain()
                for t in range(NT):
                    rope(KROPE[:, t:t + 1, :], t, 1)

            def mla_norms():
                flat = RSZO[:, 0, :, 0:NSTAT_Q]
                for t in range(NT):
                    sq = squares(Q[:, t, :], HEADS_E * MLA_D).rearrange("p (g d) -> p g d", d=MLA_D)
                    V.tensor_reduce(flat[:, t, 0:HEADS_E], sq[:, :, 0:NOPE], AX, ALU.add)
                    V.tensor_reduce(flat[:, t, HEADS_E:2 * HEADS_E], sq[:, :, NOPE:MLA_D], AX, ALU.add)
                    drain()
                    sq = squares(KV[:, t, :], HEADS_E * (NOPE + HD)).rearrange("p (g d) -> p g d", d=NOPE + HD)
                    V.tensor_reduce(flat[:, t, 2 * HEADS_E:NSTAT_Q], sq[:, :, 0:NOPE], AX, ALU.add)
                    drain()
                    V.tensor_tensor(flat[:, t, :], flat[:, t, :], fst("inv_n_q"), ALU.mult)
                drain()
                V.tensor_scalar(flat, flat, EPS, None, ALU.add)
                drain()
                y = RSZO[:, 1, :, 0:NSTAT_Q]
                rsqrt(y, flat, nt1[:, 0:2 * NSTAT_Q].rearrange("p (t n) -> p t n", t=NT))
                for t in range(NT):
                    qr = Q[:, t, :].rearrange("p (g d) -> p g d", d=MLA_D)[:, :, NOPE:MLA_D]
                    r = y[:, t, HEADS_E:2 * HEADS_E].rearrange("p (g o) -> p g o", o=1)
                    V.tensor_tensor(QROPE[:, t, :, :], qr, bc(r, ROPE), ALU.mult)
                    drain()
                    gain = fst("rope_gains")[:, 0:ROPE].rearrange("p (o n) -> p o n", o=1)
                    V.tensor_tensor(QROPE[:, t, :, :], QROPE[:, t, :, :], gain.to_broadcast([P, HEADS_E, ROPE]), ALU.mult)
                    drain()
                    rope(QROPE[:, t, :, :], t, HEADS_E)

            def moba_norms():
                flat = RSZO[:, 0, :, :]
                for t in range(NT):
                    head_sums(flat[:, t, :], squares(zo[:, t, 0:2 * ODD_W], 2 * ODD_W), HD)
                    drain()
                V.tensor_scalar(flat, flat, 1.0 / HD, EPS, ALU.mult, ALU.add)
                drain()
                rsqrt(RSZO[:, 1, :, :], flat, scaled[:, :, 0:2 * HEADS_O])

            def stage_mla(par, e):
                r = RSZO[:, 1, :, :]
                V.tensor_tensor(STAGE[:, par, 0:NT, 0:NOPE], Q[:, :, bass.ds(e * MLA_D, NOPE)], bc(r[:, :, bass.ds(e, 1)], NOPE), ALU.mult)
                V.tensor_copy(STAGE[:, par, 0:NT, NOPE:MLA_D],
                              QROPE.rearrange("p t h n -> p t (h n)")[:, :, bass.ds(e * ROPE, ROPE)])
                V.tensor_copy(STAGE[:, par, NT:2 * NT, NOPE:MLA_D], KROPE[:, :, :])
                V.tensor_tensor(STAGE[:, par, NT:2 * NT, 0:NOPE], KV[:, :, bass.ds(e * (NOPE + HD), NOPE)],
                                bc(r[:, :, bass.ds(e + 2 * HEADS_E, 1)], NOPE), ALU.mult).then_inc(staged, 1)

            def stage_dil(par, e):
                for g in range(2):
                    last = V.tensor_tensor(STAGE[:, par, g * NT:(g + 1) * NT, 0:HD], ze[:, :, bass.ds(e * HD + O_DIL + g * DIL_W, HD)],
                                           bc(rs_z[:, :, bass.ds(e + 3 + g * HEADS_E, 1)], HD), ALU.mult)
                last.then_inc(staged, 1)

            def stage_moba(par, e):
                for g in range(2):
                    last = V.tensor_tensor(STAGE[:, par, g * NT:(g + 1) * NT, 0:HD], zo[:, :, bass.ds(e * HD + g * ODD_W, HD)],
                                           bc(RSZO[:, 1, :, bass.ds(e + g * HEADS_O, 1)], HD), ALU.mult)
                last.then_inc(staged, 1)

            def bias_mla(par, e):
                V.tensor_tensor(PROB[:, par, :], fst("causal"), bank[2 + par][:, 0:KEYS], ALU.add)

            def bias_dil(par, e):
                V.scalar_tensor_tensor(PROB[:, par, :], fst("dist"), fst("dil_slope")[:, bass.ds(e, 1)],
                                       bank[2 + par][:, 0:KEYS], ALU.mult, ALU.add)
                drain()
                V.tensor_tensor(PROB[:, par, :], PROB[:, par, :], fst("lncount"), ALU.add)

            def bias_moba(par, e):
                V.scalar_tensor_tensor(PROB[:, par, :], fst("dist"), fst("moba_slope")[:, bass.ds(e, 1)],
                                       bank[2 + par][:, 0:KEYS], ALU.mult, ALU.add)

            def heads(n, stage, bias, col0):
                def pair(e, ahead):
                    for par in range(2):
                        dve.wait_ge(scored, T.next(scored))
                        bias(par, e + par)
                        drain()
                        V.tensor_reduce(NMAX[:, par, 0:1], PROB[:, par, 0:P], AX, ALU.max, negate=True)
                        V.tensor_reduce(NMAX[:, par, 1:2], PROB[:, par, P:KEYS], AX, ALU.max, negate=True) \
                            .then_inc(max_ready, 1)
                    if ahead:
                        for par in range(2):
                            stage(par, e + 2 + par)
                    for par in range(2):
                        dve.wait_ge(probs_ready, T.next(probs_ready))
                        V.reciprocal(RDEN[:, par, :], DEN[:, par, :])
                    drain()
                    for par in range(2):
                        dve.wait_ge(head_out, T.next(head_out))
                        for t in range(NT):
                            last = V.tensor_scalar(mixed[:, t, bass.ds((e + par) * HD + col0, HD)],
                                                   bank[6 + par][:, t * HD:(t + 1) * HD], RDEN[:, par, t:t + 1], None, ALU.mult)
                    return last

                for par in range(2):
                    stage(par, par)
                with T.loop(dve, n // 2 - 1, {scored: 2, probs_ready: 2, head_out: 2}) as i:
                    pair(i * 2, True)
                return pair(n - 2, False)

            dve.sem_inc(u_ready, 2)
            dve.wait_ge(inputs_in, 16 * 5)
            V.memset(GQK, MLA_SCALE)
            drain()
            V.scalar_tensor_tensor(GQK[0:NOPE, 0:1], col("e_qn_nope", 0, NOPE), MLA_SCALE, col("e_kn_nope", 0, NOPE), ALU.mult, ALU.mult)
            V.scalar_tensor_tensor(GQK[0:HD, 1:2], col("e_dil_qn", 0, HD), HD_SCALE, col("e_dil_kn", 0, HD), ALU.mult, ALU.mult)
            V.scalar_tensor_tensor(GQK[0:HD, 2:3], col("o_qn", 0, HD), HD_SCALE, col("o_kn", 0, HD), ALU.mult, ALU.mult)
            V.tensor_copy(POSF, POS[:, :])
            drain()
            angle, turns, rest = TRIG[:, 0, :, :], TRIG[:, 1, :, :], TRIG[:, 2, :, :]
            for t in range(NT):
                V.tensor_scalar(angle[:, t, :], fst("inv_freq"), POSF[:, t:t + 1], None, ALU.mult)
            drain()
            V.tensor_scalar(turns, angle, INV_TURN, ROUND, ALU.mult, ALU.add)
            drain()
            V.tensor_scalar(turns, turns, ROUND, None, ALU.subtract)
            drain()
            src = angle
            for part in TURN_PARTS:
                V.scalar_tensor_tensor(rest, turns, -part, src, ALU.mult, ALU.add)
                drain()
                src = rest
            V.tensor_scalar(rest, rest, PI_IN, -PI_IN, ALU.min, ALU.max).then_inc(trig_ready, 1)

            for layer in range(2):
                norm_rows()
                chunks_split(KC)
                if layer == 0:
                    blocks(4, lambda c, base, b: rows_out(lambda t: ze[:, t, bass.ds(c, BLK)], base, 0, SLOTS, 0, BLK, b))
                    base = T.now(gemm_step)
                    rows_out(lambda t: ze[:, t, 4 * BLK:EVEN_IN], base, 0, SLOTS, 0, EVEN_IN - 4 * BLK, 0)
                    T.next(gemm_step, NT * SLOTS)
                    dve.wait_ge(trig_done, 1)
                    cos = TRIG[:, 3, :, :]
                    V.scalar_tensor_tensor(cos, cos, -2.0, cos, ALU.mult, ALU.mult)
                    drain()
                    V.tensor_scalar(cos, cos, 1.0, None, ALU.add)
                    drain()
                    even_norms_z()
                    chunks_split(5)
                    base = T.now(gemm_step)
                    rows_out(lambda t: Q[:, t, 0:BLK], base, 0, 2, 0, BLK, 0)
                    rows_out(lambda t: Q[:, t, BLK:BLK + BLK // 2], base, 2, 2, 0, BLK // 2, 2)
                    T.next(gemm_step, NT * SLOTS)
                    base = T.now(gemm_step)
                    for b in range(2):
                        rows_out(lambda t: KV[:, t, b * BLK:(b + 1) * BLK], base, 2 * b, 2, 0, BLK, 2 * b)
                    T.next(gemm_step, NT * SLOTS)
                    drain()
                    mla_norms()
                    heads(HEADS_E, stage_mla, bias_mla, 0)
                    last = heads(HEADS_E, stage_dil, bias_dil, HEADS_E * HD)
                else:
                    blocks(6, lambda c, base, b: rows_out(lambda t: zo[:, t, bass.ds(c, BLK)], base, 0, SLOTS, 0, BLK, b))
                    drain()
                    moba_norms()
                    last = heads(HEADS_O, stage_moba, bias_moba, 0)
                last.then_inc(rows_ready, NT)
                chunks_split(KC)
                blocks(2, lambda c, base, b: add_rows(base, 0, SLOTS, bass.ds(c, BLK), b))
                drain()
                norm_rows()
                chunks_split(KC)
                with T.loop(dve, 4, {gemm_step: SLOTS * 12} | {b: 2 for b in bank_free}):
                    for j in range(2):
                        for c in range(4):
                            dve.wait_ge(bank_free[c], T.next(bank_free[c]) + 1)
                            V.tensor_tensor(SQU[:, c % 2, :], RELU[:, c % 2, :], RELU[:, c % 2, :], ALU.mult)
                            drain()
                            V.tensor_copy(ATH[:, 4 * j + c, S:2 * S], SQU[:, c % 2, :])
                            drain()
                            V.tensor_tensor(ATL[:, 4 * j + c, S:2 * S], SQU[:, c % 2, :], ATH[:, 4 * j + c, S:2 * S], ALU.subtract) \
                                .then_inc(u_ready, 1)
                    T.next(gemm_step, SLOTS * 12)
                for b in range(2):
                    for t in range(NT):
                        dve.wait_ge(acc_open, T.next(acc_open))
                        V.tensor_tensor(h[:, t, b * BLK:(b + 1) * BLK], h[:, t, b * BLK:(b + 1) * BLK], bank[4 + 2 * b + t][:, :], ALU.add)
                drain()
                norm_rows()
                chunks_split(2, S, RELU)
                chunks_split(KC)
                T.next(gemm_step, 2 * NT * SLOTS)
                for b in bank_free:
                    T.next(b)
                base = T.now(gemm_step)
                for b in range(2):
                    for t in range(NT):
                        n = 2 * b + t
                        dve.wait_ge(bank_free[n], T.now(bank_free[n]) + 1)
                        block_done(base, 2 * b, 2, t)
                        V.tensor_tensor(TMP, GATE[:, t, b * BLK:(b + 1) * BLK], bank[n][:, :], ALU.mult).then_inc(bank_free[n], 1)
                        T.next(bank_free[n])
                        drain()
                        last = V.tensor_tensor(h[:, t, b * BLK:(b + 1) * BLK], h[:, t, b * BLK:(b + 1) * BLK], TMP, ALU.add)
                        drain()
                T.next(gemm_step, NT * SLOTS)
            V.tensor_copy(TMP[:, 0:1], h[:, 0, 0:1]).then_inc(rows_ready, 1)
            for src in range(2):
                for g in range(KC // 2):
                    dve.wait_ge(x_turned, T.next(x_turned))
                    V.tensor_copy(xT[:, 2 * g:2 * g + 2, src * S:(src + 1) * S],
                                  bank[4 + g][:, :].rearrange("p (c n) -> p c n", c=2)).then_inc(at_ready, 1)
            drain()
            V.memset(WD, 0.0).then_inc(inputs_ready, 1)
            cond = COL[:, COLS["cond"][0]:COLS["cond"][0] + 2 * KC]
            dve.wait_ge(cond_sig, 1)
            V.tensor_tensor(CTMP, CTMP, cond, ALU.mult)
            drain()
            cth, ctl = (a.rearrange("p c v -> p (c v)") for a in (CTH, CTL))
            V.tensor_copy(cth, CTMP)
            drain()
            V.tensor_tensor(ctl, CTMP, cth, ALU.subtract).then_inc(cond_ready, 1)
            V.tensor_copy(TB[:, 0:1], xT[:, 0, 0:1]).then_inc(x_ready, 1)

            def split(dst, val, done):
                hi, lo = dst
                drain()
                V.tensor_copy(hi, val)
                drain()
                return V.tensor_tensor(lo, val, hi, ALU.subtract).then_inc(done, 1)

            def wide_rms(w):
                dve.wait_ge(sq_used, T.next(sq_used, KC))
                V.tensor_scalar(VB[:, 0:w], bank[4][:, 0:w], 1.0 / D, EPS, ALU.mult, ALU.add)
                drain()
                rsqrt(RB[:, 0:w], VB[:, 0:w], TB[:, 0:w])

            def groups(n, body, count=4, per=None):
                base = T.now(gemm_step)
                for c in range(count):
                    dve.wait_ge(gemm_step, base + count * (SLOTS - 1) + c + 1)
                    body(n, c)
                T.next(gemm_step, SLOTS * count)

            def group_blocks(n, body):
                with T.loop(dve, n, {gemm_step: 4 * SLOTS} | {b: 1 for b in bank_free}) as i:
                    groups(i, body)

            def freed(ins, c):
                ins.then_inc(bank_free[c], 1)
                T.next(bank_free[c])

            for layer in range(2):
                tq = TOK if layer == 0 else S
                nq = tq // P
                sides = ((0, slice(0, S)), (1, slice(S, TOK)))

                def ada(i, c):
                    freed(V.tensor_scalar(MOD.rearrange("p c v -> p (c v)")[:, bass.ds(i * 8 + 2 * c, 2)], bank[c][:, 0:2],
                                          COL[:, bass.ds(i * 4 + (COLS["b_ada_2"][0] + layer * 3 * KC + c), 1)], None, ALU.add), c)

                group_blocks(6, ada)
                drain()
                for v in range(2):
                    g0, g1 = (COL[:, COLS[n][0] + layer * KC:COLS[n][0] + (layer + 1) * KC] for n in ("g_pre_2", "g_post_2"))
                    V.scalar_tensor_tensor(MOD[:, KC:2 * KC, v], MOD[:, KC:2 * KC, v], 1.0, g0, ALU.add, ALU.mult)
                    V.tensor_tensor(MOD[:, 2 * KC:3 * KC, v], MOD[:, 2 * KC:3 * KC, v], g1, ALU.mult)
                wide_rms(TOK)
                for g in range(KC // 2):
                    V.tensor_tensor(W0, xT[:, 2 * g:2 * g + 2, :],
                                    RB.rearrange("p (o n) -> p o n", o=1).to_broadcast([P, 2, TOK]), ALU.mult)
                    drain()
                    for c in range(2):
                        for v, side in sides:
                            V.tensor_scalar(W1[:, c, side], W0[:, c, side], MOD[:, KC + 2 * g + c, v:v + 1],
                                            MOD[:, 2 * g + c, v:v + 1], ALU.mult, ALU.add)
                    split((ATH[:, 2 * g:2 * g + 2, :], ATL[:, 2 * g:2 * g + 2, :]), W1, at_ready)

                V.memset(RA[2 * RANK:2 * RANK + 1, :], 1.0)
                groups(0, lambda n, c: freed(V.tensor_scalar(GQ[:, c * TOK:c * TOK + tq], bank[c][:, 0:tq], GDK ** -0.5, None, ALU.mult), c))
                groups(0, lambda n, c: freed(V.tensor_copy(GK[:, c * TOK:(c + 1) * TOK], bank[c][:, :]), c))
                groups(0, lambda n, c: freed(V.tensor_copy(RA[0:2 * RANK, :], bank[c][0:2 * RANK, :]), c), 1)
                group_blocks(2, lambda i, c: freed(V.tensor_copy(VG[:, c, bass.ds(i * BLK, BLK)], bank[c][:, :]), c))

                def silu_z(room, tmp):
                    def body(i, c):
                        dve.wait_ge(sig_done, T.next(sig_done))
                        freed(V.tensor_tensor(tmp[:, 0:tq], room[:, c, 0:tq], bank[c][:, 0:tq], ALU.mult), c)
                        drain()
                        hi, lo = (a.rearrange("p c n -> p (c n)")[:, bass.ds(i * 4 * TOK + c * TOK, tq)] for a in (BTH, BTL))
                        V.tensor_copy(hi, tmp[:, 0:tq])
                        drain()
                        V.tensor_tensor(lo, tmp[:, 0:tq], hi, ALU.subtract)
                        drain()
                    return body

                def z_blocks():
                    with T.loop(dve, 2, {gemm_step: 4 * SLOTS, sig_done: 4} | {b: 1 for b in bank_free}) as i:
                        groups(i, silu_z(SIGZ, WZ))

                z_blocks()

                def gate_rows(chunk, part, tmp):
                    hi, lo = (a.rearrange("p c n -> p (c n)")[:, bass.ds(chunk * TOK, tq)] for a in (BTH, BTL))
                    V.tensor_tensor(tmp[:, 0:tq], hi, lo, ALU.add)
                    drain()
                    part(tmp[:, 0:tq])
                    split((hi, lo), tmp[:, 0:tq], bt_ready)

                drain()
                V.memset(ATT, 0.0)
                V.memset(KE, 0.0)
                dve.wait_ge(mask_in, 16)

                def halves(a, half):
                    return a.rearrange("p (b two x) -> p b two x", two=2, x=half)

                def gla_dir(hd, d):
                    dve.wait_ge(g_logs, T.next(g_logs))
                    V.scalar_tensor_tensor(LA, bank[4][:, :], 0.0, LOGS, ALU.min, ALU.subtract).then_inc(g_la, 1)
                    dve.wait_ge(g_cum, T.next(g_cum))
                    V.tensor_copy(CUM, bank[5][:, :])
                    drain()
                    cum = CUM.rearrange("p (t n) -> p t n", t=TT)
                    e = P - 1 if d == 0 else 0
                    V.tensor_tensor(DE[:, 0, :].rearrange("p (t n) -> p t n", t=TT),
                                    cum[:, :, e:e + 1].to_broadcast([P, TT, P]), cum, ALU.subtract).then_inc(g_diff, 1)
                    dve.wait_ge(g_exp, T.next(g_exp))
                    k = GK[:, bass.ds(hd * TOK, TOK)]
                    q = GQ[:, bass.ds(hd * TOK, tq)]
                    V.tensor_tensor(KE[:, 0, :], k, DE[:, 0, :], ALU.mult).then_inc(g_keys, 1)
                    V.tensor_tensor(QB[:, 0:tq], q, DE[:, 1, 0:tq], ALU.mult)
                    drain()

                    def diff(n):
                        half = LEVELS[n]
                        b, o = halves(CUM[:, 0:tq], half), halves(DE[:, n % 2, 0:tq], half)
                        ref = b[:, :, 0, half - 1:half] if d == 0 else b[:, :, 1, 0:1]
                        ref = ref.to_broadcast([P, tq // (2 * half), half])
                        V.tensor_tensor(o[:, :, 1 - d, :], b[:, :, 1 - d, :], ref, ALU.subtract)
                        V.tensor_tensor(o[:, :, d, :], ref, b[:, :, d, :], ALU.subtract).then_inc(g_diff, 1)

                    def decayed(n):
                        half, b = LEVELS[n], n % 2
                        dve.wait_ge(g_exp, T.next(g_exp))
                        o = halves(DE[:, b, 0:tq], half)
                        qo = QE[:, b, 0:tq // 2].rearrange("p (b x) -> p b x", x=half)
                        V.tensor_tensor(qo, halves(q, half)[:, :, 1 - d, :], o[:, :, 1 - d, :], ALU.mult)
                        V.tensor_tensor(halves(KE[:, 1 - b, 0:tq], half)[:, :, d, :],
                                        halves(GK[:, bass.ds(hd * TOK, tq)], half)[:, :, d, :], o[:, :, d, :], ALU.mult).then_inc(g_pair, 1)
                        drain()

                    def placed(n):
                        dve.wait_ge(g_level, T.next(g_level))
                        V.memset(TMPA, 0.0)
                        lv = bank[5 - n % 2]
                        if n == len(LEVELS):
                            m = MASK[:, 0:P].rearrange("p (o n) -> p o n", o=1).to_broadcast([P, nq, P])
                            return V.copy_predicated(ATT[:, d, 0:tq].rearrange("p (t n) -> p t n", t=nq), m,
                                                     lv[:, 0:tq].rearrange("p (t n) -> p t n", t=nq))
                        half = LEVELS[n]
                        m0 = P + (d * len(LEVELS) + n) * (P // 2)
                        nb = P // (2 * half)
                        m = MASK[:, m0:m0 + P // 2].rearrange("p (o b x) -> p o b x", o=1, x=half).to_broadcast([P, nq, nb, half])
                        o = ATT[:, d, 0:tq].rearrange("p (t b two x) -> p t b two x", t=nq, two=2, x=half)[:, :, :, 1 - d, :]
                        return V.copy_predicated(o, m, lv[:, 0:tq // 2].rearrange("p (t b x) -> p t b x", t=nq, x=half))

                    diff(0)
                    diff(1)
                    dve.wait_ge(g_outer, T.next(g_outer))
                    V.tensor_copy(STATE[:, 0, :], bank[5][:, 0:GDV])
                    drain()
                    order = TILES[d]
                    V.scalar_tensor_tensor(STATE[:, 1, :], STATE[:, 0, :], EBL[:, order[1]:order[1] + 1], bank[5][:, GDV:2 * GDV], ALU.mult, ALU.add)
                    drain()
                    V.scalar_tensor_tensor(STATE[:, 2, :], STATE[:, 1, :], EBL[:, order[2]:order[2] + 1], bank[4][:, 0:GDV], ALU.mult, ALU.add) \
                        .then_inc(g_state, 1)
                    drain()
                    for n in range(len(LEVELS)):
                        decayed(n)
                        if n + 2 < len(LEVELS):
                            diff(n + 2)
                        if n > 0:
                            placed(n - 1)
                    drain()
                    V.tensor_copy(KE[:, 0, 0:tq], GK[:, bass.ds(hd * TOK, tq)]).then_inc(g_pair, 1)
                    placed(len(LEVELS) - 1)
                    drain()
                    placed(len(LEVELS)).then_inc(g_att, 1)

                per = {g_logs: 2, g_cum: 2, g_exp: 2 * (1 + len(LEVELS)), g_level: 2 * (1 + len(LEVELS)), g_outer: 2, g_out: 1, g_turned: 2}
                with T.loop(dve, GH, per) as i:
                    for d in range(2):
                        gla_dir(i, d)
                    dve.wait_ge(g_out, T.next(g_out))
                    for b in range(nq // 2):
                        V.tensor_copy(ON[:, 2 * b:2 * b + 2, :], bank[6 + b][:, :].rearrange("p (t n) -> p t n", t=2))
                    drain()
                    for t in range(nq):
                        V.tensor_tensor_reduce(DE[:, 0, 0:GDV], ON[:, t, :], ON[:, t, :], 1.0 / GDV, 0.0, ALU.mult, ALU.add, GS[:, t:t + 1])
                        drain()
                    V.tensor_scalar(GS[:, 0:nq], GS[:, 0:nq], EPS, None, ALU.add)
                    drain()
                    rsqrt(GR[:, 0:nq], GS[:, 0:nq], GT[:, 0:nq])
                    for t in range(nq):
                        last = V.tensor_scalar(ON[:, t, :], ON[:, t, :], GR[:, t:t + 1], None, ALU.mult)
                    last.then_inc(g_rows, 1)
                    for c in range(2):
                        dve.wait_ge(g_turned, T.next(g_turned))
                        gate_rows(i * 2 + c, lambda w: V.scalar_tensor_tensor(w, bank[4 + c][:, 0:tq], col("gla_norm_g_2", layer * 2 + c), w,
                                                                              ALU.mult, ALU.mult), DE[:, c, :])

                def gated(first):
                    def gate(n, c):
                        T.next(bank_free[c])

                    def branch(n, c):
                        dve.wait_ge(bank_free[c], T.now(bank_free[c]) + 1)
                        y, o, g = Y[:, n * 4 + c, 0:tq], bank[c][:, 0:tq], G[:, c, 0:tq]
                        if first:
                            freed(V.tensor_tensor(y, g, o, ALU.mult), c)
                        else:
                            freed(V.tensor_tensor(WG[:, 0:tq], g, o, ALU.mult), c)
                            drain()
                            V.tensor_tensor(y, y, WG[:, 0:tq], ALU.add)
                            drain()
                    for n in range(2):
                        for c in range(4):
                            gate(n, c)
                        T.next(gemm_step, 4 * SLOTS)
                        groups(n, branch)
                    drain()

                gated(True)

                group_blocks(2, lambda i, c: freed(V.tensor_copy(QG[:, bass.ds(i * 4 * TOK + c * TOK, tq)], bank[c][:, 0:tq]), c))
                groups(0, lambda n, c: freed(V.tensor_copy(QG[:, (AH + c) * TOK:(AH + c + 1) * TOK], bank[c][:, :]), c), AKV)
                groups(0, lambda n, c: freed(V.tensor_copy(VA[:, c, :], bank[c][:, 0:AKV * AD]), c), TT)
                drain()
                with T.loop(dve, 2, {gemm_step: 4 * SLOTS, sig_done: 4} | {b: 1 for b in bank_free}) as i:
                    groups(i, silu_z(SIGA, WA))
                V.tensor_copy(TMPA, QG[:, 0:1]).then_inc(a_heads, 1)
                drain()
                nstat = AH * nq + AKV * TT
                dve.wait_ge(sq_used, T.next(sq_used, AH + AKV))
                V.tensor_scalar(RSV[:, 0:nstat], bank[4][:, 0:nstat], 1.0 / AD, EPS, ALU.mult, ALU.add)
                drain()
                rsqrt(RSQ[:, 0:nstat], RSV[:, 0:nstat], RSW[:, 0:nstat])
                V.tensor_scalar(RSQ[:, 0:AH * nq], RSQ[:, 0:AH * nq], ATTN_SCALE, None, ALU.mult)
                rsk = RSQ[:, AH * nq:nstat]
                for k in range(AKV):
                    if k:
                        dve.wait_ge(a_bc, T.now(a_bc))
                    for t in range(TT):
                        n = k * TT + t
                        last = V.tensor_scalar(DIAG[:, t, :], ident, rsk[:, n:n + 1], None, ALU.mult)
                    last.then_inc(a_diag, 1)
                    kr = QG[:, (AH + k) * TOK:(AH + k + 1) * TOK]
                    V.tensor_scalar(K2[:, k, :], kr, col("k_norm_g_2", layer), None, ALU.mult).then_inc(a_gain, 1)
                    drain()
                    dve.wait_ge(a_rot, T.next(a_rot))
                    V.tensor_tensor(QS[:, 0:S], cst("sin"), bank[6][:, 0:S], ALU.mult)
                    V.tensor_tensor(K2[:, k, 0:S], K2[:, k, 0:S], cst("cos"), ALU.mult)
                    drain()
                    V.tensor_tensor(K2[:, k, 0:S], K2[:, k, 0:S], QS[:, 0:S], ALU.add)
                    drain()
                    dve.wait_ge(a_bc, T.next(a_bc))
                    V.tensor_tensor(K2[:, k, :], K2[:, k, :], bank[5][:, :], ALU.mult)
                drain()

                def attend(hd):
                    V.tensor_scalar(QS[:, 0:tq], QG[:, bass.ds(hd * TOK, tq)], col("q_norm_g_2", layer), None, ALU.mult).then_inc(a_gain, 1)
                    V.tensor_copy(SCL[:, 0:nq], RSQ[:, bass.ds(hd * nq, nq)])
                    drain()
                    dve.wait_ge(a_rot, T.next(a_rot))
                    V.tensor_tensor(WA[:, 0:S], cst("sin"), bank[0][:, 0:S], ALU.mult)
                    V.tensor_tensor(QS[:, 0:S], QS[:, 0:S], cst("cos"), ALU.mult)
                    drain()
                    V.tensor_tensor(QS[:, 0:S], QS[:, 0:S], WA[:, 0:S], ALU.add).then_inc(a_q, 1)
                    dve.wait_ge(a_score, T.next(a_score))
                    for t in range(nq):
                        sc = bank[1 + t][:, :] if t < NT else bank[3][:, (t - NT) * S:(t - NT + 1) * S]
                        V.tensor_reduce(NM[:, t:t + 1], sc, AX, ALU.max, negate=True)
                    drain()
                    V.tensor_tensor(NM[:, 0:nq], NM[:, 0:nq], SCL[:, 0:nq], ALU.mult).then_inc(a_max, 1)
                    dve.wait_ge(a_exp, T.next(a_exp))
                    V.reciprocal(RD[:, 0:nq], DN[:, 0:nq])
                    drain()
                    for t in range(nq):
                        pr = PL[:, t, :] if t < NT else PC[:, t - NT, :]
                        last = V.tensor_scalar(pr, pr, RD[:, t:t + 1], None, ALU.mult)
                    last.then_inc(a_norm, 1)
                    dve.wait_ge(a_out, T.next(a_out))
                    gate_rows(hd, lambda w: V.tensor_tensor(w, w, bank[7][:, 0:tq], ALU.mult), WA)
                    drain()

                for kv in range(AKV):
                    with T.loop(dve, AH // AKV, {a_rot: 1, a_score: 1, a_exp: 1, a_out: 1}) as i:
                        attend(i + kv * (AH // AKV))
                gated(False)

                def tokens(a):
                    return a.rearrange("p (s n) -> p s n", n=S)

                with T.loop(dve, 2, {gemm_step: 16 * SLOTS, sig_done: 4} | {b: 4 for b in bank_free}) as i:
                    groups(i, lambda n, c: freed(V.tensor_copy(AB[:, c, 0:tq], bank[c][:, 0:tq]), c))
                    groups(i, lambda n, c: freed(V.tensor_copy(AC[:, c, 0:tq], bank[c][:, 0:tq]), c))
                    drain()
                    groups(i, lambda n, c: freed(V.tensor_tensor(PX[:, c, 0:tq], AC[:, c, 0:tq], bank[c][:, 0:tq], ALU.mult), c))
                    drain()

                    def tap(k, c):
                        return COL[:, bass.ds(i * 4 + (COLS["conv_w_2"][0] + (layer * 3 + k) * KC + c), 1)]

                    for c in range(4):
                        V.tensor_scalar(CV[:, c, 0:tq], PX[:, c, 0:tq], tap(1, c), None, ALU.mult)
                    drain()
                    for c in range(4):
                        p, o = tokens(PX[:, c, 0:tq]), tokens(CV[:, c, 0:tq])
                        V.scalar_tensor_tensor(o[:, :, 1:S], p[:, :, 0:S - 1], tap(0, c), o[:, :, 1:S], ALU.mult, ALU.add)
                    drain()
                    for c in range(4):
                        p, o = tokens(PX[:, c, 0:tq]), tokens(CV[:, c, 0:tq])
                        V.scalar_tensor_tensor(o[:, :, 0:S - 1], p[:, :, 1:S], tap(2, c), o[:, :, 0:S - 1], ALU.mult, ALU.add)
                    drain()
                    V.tensor_tensor(CV[:, :, 0:tq], CV[:, :, 0:tq], AB[:, :, 0:tq], ALU.mult)
                    drain()

                    def conv_out(n, c):
                        dve.wait_ge(sig_done, T.next(sig_done))
                        freed(V.tensor_tensor(WC[:, 0:tq], SIGC[:, c, 0:tq], bank[c][:, 0:tq], ALU.mult), c)
                        drain()
                        V.tensor_tensor(WC[:, 0:tq], WC[:, 0:tq], CV[:, c, 0:tq], ALU.mult)
                        hi, lo = (a.rearrange("p c n -> p (c n)")[:, bass.ds(i * 4 * TOK + c * TOK, tq)] for a in (BTH, BTL))
                        split((hi, lo), WC[:, 0:tq], bt_ready)
                        drain()

                    groups(i, conv_out)
                gated(False)

                for g in range(KC // 2):
                    split((BTH[:, 2 * g:2 * g + 2, 0:tq], BTL[:, 2 * g:2 * g + 2, 0:tq]), Y[:, 2 * g:2 * g + 2, 0:tq], bt_ready)
                group_blocks(2, lambda i, c: freed(V.tensor_copy(OUT.rearrange("p c n -> p (c n)")[:, bass.ds(i * 4 * TOK + c * TOK, tq)], bank[c][:, 0:tq]), c))
                drain()
                V.tensor_copy(TMPA, OUT[:, 0, 0:1]).then_inc(x_split, 1)
                wide_rms(tq)
                for c in range(KC):
                    V.tensor_tensor(OUT[:, c, 0:tq], OUT[:, c, 0:tq], RB[:, 0:tq], ALU.mult)
                drain()
                for c in range(KC):
                    for v, side in sides[0:nq // 2]:
                        last = V.scalar_tensor_tensor(xT[:, c, side], OUT[:, c, side], MOD[:, 2 * KC + c, v:v + 1], xT[:, c, side], ALU.mult, ALU.add)
                last.then_inc(x_ready, 1)
                drain()
            for t in range(NT):
                for g in range(2):
                    dve.wait_ge(x_turned, T.next(x_turned))
                    V.tensor_copy(h[:, t, g * BLK:(g + 1) * BLK], bank[4 + 2 * t + g][:, :]).then_inc(out_rows, 1)

        @block.tensor
        def _(pe):
            T = Tally()
            mm, turn = nc.tensor.matmul, nc.tensor.transpose
            for b in bank_free:
                pe.sem_inc(b, 1)

            def product(o, ah, al, bh, bl, start, stop, free=False):
                mm(o, ah, bh, start=start, stop=False, skip_group_check=free)
                mm(o, ah, bl, start=False, stop=False, skip_group_check=free)
                return mm(o, al, bh, start=False, stop=stop, skip_group_check=free)

            def unit(slot, ready=None):
                pe.wait_ge(lo_split, T.next(lo_split) + SLOTS)
                if ready is not None:
                    pe.wait_ge(*ready)

            def rows_block(units, width, b0, chunk0=0, tok=0, ready=None, acc=False):
                c0 = chunk0
                for u, (slot, k) in enumerate(units):
                    unit(slot, ready and ready[u])
                    for t in range(NT):
                        if u == 0 and not acc:
                            pe.wait_ge(bank_free[b0 + t], T.next(bank_free[b0 + t]))
                        for c in range(k):
                            tk = slice(tok + t * P, tok + (t + 1) * P)
                            w = slice(c * width, (c + 1) * width)
                            last = product(bank[b0 + t][:, 0:width], ATH[:, c0 + c, tk], ATL[:, c0 + c, tk],
                                           WHI[:, slot, w], WLO[:, slot, w], not acc and u == 0 and c == 0,
                                           not acc and u == len(units) - 1 and c == k - 1, acc)
                        last.then_inc(gemm_step, 1)
                    c0 += k

            def cols_block(ready=None, tok=0, width=S):
                for slot in range(SLOTS):
                    unit(slot, ready and ready[slot])
                    for j in range(BLK // P):
                        if slot == 0:
                            pe.wait_ge(bank_free[j], T.next(bank_free[j]))
                        for c in range(2):
                            w = slice(c * BLK + j * P, c * BLK + (j + 1) * P)
                            last = product(bank[j][:, 0:width], WHI[:, slot, w], WLO[:, slot, w],
                                           ATH[:, 2 * slot + c, tok:tok + width], ATL[:, 2 * slot + c, tok:tok + width],
                                           slot == 0 and c == 0, slot == SLOTS - 1 and c == 1)
                        last.then_inc(gemm_step, 1)

            std_units = [(s, 2) for s in range(SLOTS)]

            def rows_blocks(n, ready):
                with T.loop(pe, n // 2, {lo_split: 2 * SLOTS} | {b: 1 for b in bank_free}):
                    for j in range(2):
                        rows_block(std_units, BLK, 2 * j, ready=ready)

            def turn_rows(count, src):
                pe.wait_ge(rows_ready, T.next(rows_ready, NT))
                if T.now(turned):
                    pe.wait_ge(chunk_val, T.now(turned))
                base = T.now(turned)
                for g in range((count + 1) // 2):
                    for c in range(2 * g, min(2 * g + 2, count)):
                        for t in range(NT):
                            o = (c % 2) * S + t * P
                            last = turn(bank[4 + g % 4][:, o:o + P], src(t, c), ident)
                    last.then_inc(turned, 1)
                    T.next(turned)
                return [(at_ready, base + g + 1) for g in range((count + 1) // 2)]

            def heads(n, d, value):
                def operands(par):
                    pe.wait_ge(staged, T.next(staged))
                    for g in range(2 * NT):
                        last = turn(bank[par][0:MLA_D, g * P:(g + 1) * P], STAGE[:, par, g, :], ident)
                    last.then_inc(qk_turned, 1)

                def pair(e, ahead):
                    for par in range(2):
                        pe.wait_ge(qk_ready, T.next(qk_ready))
                        q, k = QKT[0:d, par, 0:S], QKT[0:d, par, S:2 * S]
                        mm(bank[2 + par][:, 0:P], q[:, 0:P], k[:, 0:P], start=True, stop=True)
                        mm(bank[2 + par][:, P:KEYS], q[:, P:S], k, start=True, stop=True).then_inc(scored, 1)
                    if ahead:
                        for par in range(2):
                            operands(par)
                    for par in range(2):
                        pe.wait_ge(probs_ready, T.next(probs_ready))
                        for g in range(KEYS // P):
                            last = turn(bank[4 + par][:, g * P:(g + 1) * P], PROB[:, par, g * P:(g + 1) * P], ident)
                        last.then_inc(probs_turned, 1)
                    for par in range(2):
                        pe.wait_ge(probs_t_ready, T.next(probs_t_ready))
                        o, p = bank[6 + par], PROBT[:, par, :]
                        mm(o[:, 0:HD], p[:, 0:P], value(0, e + par), start=True, stop=True)
                        mm(o[:, HD:2 * HD], p[:, P:2 * P], value(0, e + par), start=True, stop=False)
                        mm(o[:, HD:2 * HD], p[:, 2 * P:KEYS], value(1, e + par), start=False, stop=True).then_inc(head_out, 1)

                for par in range(2):
                    operands(par)
                with T.loop(pe, n // 2 - 1, {staged: 2, qk_ready: 2, probs_ready: 2, probs_t_ready: 2}) as i:
                    pair(i * 2, True)
                pair(n - 2, False)

            pe.wait_ge(inputs_in, 16 * 5)
            pe.wait_ge(zeroed, 1)
            for layer in range(2):
                ready = turn_rows(KC, lambda t, c: scaled[:, t, c * P:(c + 1) * P])
                if layer == 0:
                    rows_blocks(4, ready)
                    rows_block(std_units, EVEN_IN - 4 * BLK, 0)
                    ready = turn_rows(5, lambda t, c: ze[:, t, c * P:(c + 1) * P])
                    rows_block([(0, 2), (1, 1)], BLK, 0, ready=ready[0:2])
                    rows_block([(2, 2), (3, 1)], BLK // 2, 2)
                    rows_block([(0, 1), (1, 1)], BLK, 0, 3, ready=ready[1:3])
                    rows_block([(2, 1), (3, 1)], BLK, 2, 3)
                    heads(HEADS_E, MLA_D, lambda t, e: KV[:, t, bass.ds(e * (NOPE + HD) + NOPE, HD)])
                    heads(HEADS_E, HD, lambda t, e: ze[:, t, bass.ds(e * HD + O_DIL + 2 * DIL_W, HD)])
                else:
                    rows_blocks(6, ready)
                    heads(HEADS_O, HD, lambda t, e: zo[:, t, bass.ds(e * HD + 2 * ODD_W, HD)])
                ready = turn_rows(KC, lambda t, c: mixed[:, t, c * P:(c + 1) * P])
                rows_blocks(2, ready)
                ready = turn_rows(KC, lambda t, c: scaled[:, t, c * P:(c + 1) * P])
                pe.wait_ge(*ready[-1])
                for b in range(4, 8):
                    mm(bank[b][:, :], ZERO[0:1, 0:P], ZERO[0:1, :], start=True, stop=False, skip_group_check=True)
                with T.loop(pe, 4, {lo_split: 4 * SLOTS, u_ready: 8} | {b: 2 for b in bank_free}):
                    for j in range(2):
                        cols_block(ready)
                    hidden = [(u_ready, T.next(u_ready, 2) + 2) for _ in range(SLOTS)]
                    for j in range(2):
                        rows_block(std_units, BLK, 4 + 2 * j, tok=S, ready=hidden, acc=True)
                for b in range(4, 8):
                    mm(bank[b][:, :], ZERO[0:1, 0:P], ZERO[0:1, :], start=False, stop=True, skip_group_check=True) \
                        .then_inc(acc_open, 1)
                pe.wait_ge(p_in, 16 * (layer + 1))
                for c in range(2):
                    for t in range(NT):
                        last = turn(bank[0][:, c * S + t * P:c * S + (t + 1) * P], PIN[:, t, c * P:(c + 1) * P], ident)
                last.then_inc(turned, 1)
                T.next(turned)
                p_ready = (at_ready, T.now(turned))
                ready = turn_rows(KC, lambda t, c: scaled[:, t, c * P:(c + 1) * P])
                rows_blocks(2, ready)
                for b in range(2):
                    rows_block([(2 * b, 1), (2 * b + 1, 1)], BLK, 2 * b, tok=S, ready=[p_ready, p_ready])
            def cols_product(groups, rhs, width, b0=0, ready=None, wcols=BLK):
                rh, rl = rhs
                for slot in range(SLOTS):
                    unit(slot, ready and ready[slot])
                    for j in range(groups):
                        if slot == 0:
                            pe.wait_ge(bank_free[j], T.next(bank_free[j]))
                        for c in range(2):
                            w = slice(c * wcols + j * P, c * wcols + (j + 1) * P)
                            last = product(bank[j][:, 0:width], WHI[:, slot, w], WLO[:, slot, w], rh[:, 2 * slot + c, 0:width],
                                           rl[:, 2 * slot + c, 0:width], slot == 0 and c == 0, slot == SLOTS - 1 and c == 1)
                        last.then_inc(gemm_step, 1)

            def rows_product(width, ready=None):
                for slot in range(SLOTS):
                    unit(slot, ready and ready[slot])
                    for t in range(TT):
                        if slot == 0:
                            pe.wait_ge(bank_free[t], T.next(bank_free[t]))
                        for c in range(2):
                            w, tk = slice(c * width, (c + 1) * width), slice(t * P, (t + 1) * P)
                            last = product(bank[t][:, 0:width], ATH[:, 2 * slot + c, tk], ATL[:, 2 * slot + c, tk],
                                           WHI[:, slot, w], WLO[:, slot, w], slot == 0 and c == 0, slot == SLOTS - 1 and c == 1)
                        last.then_inc(gemm_step, 1)

            def loop_blocks(n, body):
                with T.loop(pe, n, {lo_split: SLOTS} | {b: 1 for b in bank_free}):
                    body()

            def sum_squares(w):
                for c in range(KC):
                    pe.wait_ge(sq_ready, T.next(sq_ready))
                    mm(bank[4][:, 0:w], cst("ones"), SQ2[:, c % 2, 0:w], start=c == 0, stop=c == KC - 1).then_inc(sq_used, 1)

            pe.wait_ge(rows_ready, T.next(rows_ready))
            pe.wait_ge(ctx_in, 16)
            base = T.now(at_ready) + T.now(turned)
            for s, src in enumerate((h, CTXIN)):
                for g in range(KC // 2):
                    if s:
                        pe.wait_ge(at_ready, base + g + 1)
                    for c in range(2 * g, 2 * g + 2):
                        for t in range(NT):
                            o = (c % 2) * S + t * P
                            last = turn(bank[4 + g][:, o:o + P], src[:, t, c * P:(c + 1) * P], ident)
                    last.then_inc(x_turned, 1)
            chunks = base + KC
            pe.wait_ge(cond_ready, 1)
            for layer in range(2):
                tq = TOK if layer == 0 else S
                nq = tq // P
                AT, BT = (ATH, ATL), (BTH, BTL)
                sum_squares(TOK)
                loop_blocks(6, lambda: cols_product(4, (CTH, CTL), 2))
                ready = [(at_ready, chunks + s + 1) for s in range(SLOTS)]
                chunks += SLOTS
                cols_product(4, AT, tq, ready=ready)
                cols_product(4, AT, TOK)
                cols_product(1, AT, TOK, wcols=P)
                loop_blocks(2, lambda: rows_product(BLK))
                loop_blocks(2, lambda: cols_product(4, AT, tq))

                pe.wait_ge(wd_in, 64 * (layer + 1))

                def gla_dir(hd, d):
                    v = [VG[:, t, bass.ds(hd * GDV, GDV)] for t in range(TT)]
                    for t in range(TT):
                        last = mm(bank[4][:, t * P:(t + 1) * P], RA[:, t * P:(t + 1) * P], WD[:, d, bass.ds(hd * GDK, GDK)], start=True, stop=True)
                    last.then_inc(g_pre, 1)
                    pe.wait_ge(g_la, T.next(g_la))
                    for t in range(TT):
                        last = mm(bank[5][:, t * P:(t + 1) * P], LA[:, t * P:(t + 1) * P], cst("tri_f" if d == 0 else "tri_b"), start=True, stop=True)
                    last.then_inc(g_cum, 1)
                    pe.wait_ge(g_keys, T.next(g_keys))
                    for t in range(TT):
                        last = turn(bank[4][:, t * P:(t + 1) * P], KE[:, 0, t * P:(t + 1) * P], ident)
                    last.then_inc(g_kturned, 1)
                    pe.wait_ge(g_kready, T.next(g_kready))
                    order = TILES[d]
                    for n, o in enumerate((bank[5][:, 0:GDV], bank[5][:, GDV:2 * GDV], bank[4][:, 0:GDV])):
                        t = order[n]
                        last = mm(o, KDT[:, t * P:(t + 1) * P], v[t], start=True, stop=True)
                    last.then_inc(g_outer, 1)
                    for n in range(len(LEVELS)):
                        pe.wait_ge(g_pair, T.next(g_pair))
                        for t in range(nq):
                            last = mm(bank[5 - n % 2][:, t * P // 2:(t + 1) * P // 2], KE[:, 1 - n % 2, t * P:(t + 1) * P],
                                      QE[:, n % 2, t * P // 2:(t + 1) * P // 2], start=True, stop=True)
                        last.then_inc(g_level, 1)
                    pe.wait_ge(g_pair, T.next(g_pair))
                    for t in range(nq):
                        last = mm(bank[4][:, t * P:(t + 1) * P], KE[:, 0, t * P:(t + 1) * P], GQ[:, bass.ds(hd * TOK + t * P, P)], start=True, stop=True)
                    last.then_inc(g_level, 1)
                    pe.wait_ge(g_state, T.next(g_state))
                    pe.wait_ge(g_att, T.next(g_att))
                    seen = set()
                    for n, t in enumerate(order):
                        if t >= nq:
                            continue
                        o = bank[6 + t // 2][:, t % 2 * GDV:(t % 2 + 1) * GDV]
                        end = d == 1
                        last = mm(o, ATT[:, d, t * P:(t + 1) * P], v[t], start=d == 0 and t // 2 not in seen, stop=end and n == 0, skip_group_check=True)
                        seen.add(t // 2)
                        if n:
                            last = mm(o, QB[:, t * P:(t + 1) * P], STATE[:, n - 1, :], start=False, stop=end, skip_group_check=True)
                    return last

                per = {g_la: 2, g_keys: 2, g_kready: 2, g_pair: 2 * (1 + len(LEVELS)), g_state: 2, g_att: 2, g_rows: 1, bt_ready: 2}
                with T.loop(pe, GH, per) as i:
                    gla_dir(i, 0)
                    gla_dir(i, 1).then_inc(g_out, 1)
                    pe.wait_ge(g_rows, T.next(g_rows))
                    for c in range(2):
                        for t in range(nq):
                            last = turn(bank[4 + c][:, t * P:(t + 1) * P], ON[:, t, c * P:(c + 1) * P], ident)
                        last.then_inc(g_turned, 1)
                    pe.wait_ge(bt_ready, T.next(bt_ready, 2))

                def gated(b):
                    for n in range(2):
                        cols_product(4, AT, tq)
                        cols_product(4, BT, tq, ready=b)

                gated(None)

                loop_blocks(2, lambda: cols_product(4, AT, tq))
                cols_product(AKV, AT, TOK, wcols=AKV * AD)
                rows_product(AKV * AD)
                loop_blocks(2, lambda: cols_product(4, AT, tq))
                one_col = cst("ones")[:, 0:1]
                with T.loop(pe, AH // 2, {sq_ready: 2}) as i:
                    for par in range(2):
                        pe.wait_ge(sq_ready, T.next(sq_ready))
                        for t in range(nq):
                            last = mm(bank[4][:, bass.ds(i * 2 * nq + par * nq + t, 1)], SQH[:, par, t * P:(t + 1) * P], one_col, start=True, stop=True)
                        last.then_inc(sq_used, 1)
                for k in range(AKV):
                    pe.wait_ge(sq_ready, T.next(sq_ready))
                    for t in range(TT):
                        n = AH * nq + k * TT + t
                        last = mm(bank[4][:, n:n + 1], SQH[:, k, t * P:(t + 1) * P], one_col, start=True, stop=True)
                    last.then_inc(sq_used, 1)
                for k in range(AKV):
                    pe.wait_ge(a_diag, T.next(a_diag))
                    if k:
                        pe.wait_ge(a_gain, T.now(a_gain) + 1)
                    for t in range(TT):
                        last = mm(bank[5][:, t * P:(t + 1) * P], cst("ones"), DIAG[:, t, :], start=True, stop=True)
                    last.then_inc(a_bc, 1)
                    pe.wait_ge(a_gain, T.next(a_gain))
                    mm(bank[6][:, 0:S], cst("rot"), K2[:, k, 0:S], start=True, stop=True).then_inc(a_rot, 1)

                def attend(kv):
                    pe.wait_ge(a_gain, T.next(a_gain))
                    mm(bank[0][:, 0:S], cst("rot"), QS[:, 0:S], start=True, stop=True).then_inc(a_rot, 1)
                    pe.wait_ge(a_q, T.next(a_q))
                    for t in range(nq):
                        q = QS[:, t * P:(t + 1) * P]
                        if t < NT:
                            last = mm(bank[1 + t][:, :], q, K2[:, kv, :], start=True, stop=True)
                        else:
                            last = mm(bank[3][:, (t - NT) * S:(t - NT + 1) * S], q, K2[:, kv, S:TOK], start=True, stop=True)
                    last.then_inc(a_score, 1)
                    pe.wait_ge(a_norm, T.next(a_norm))
                    for t in range(NT):
                        for s in range(TT):
                            last = turn(bank[4 + t][:, s * P:(s + 1) * P], PL[:, t, s * P:(s + 1) * P], ident)
                    for t in range(nq - NT):
                        for s in range(NT):
                            last = turn(bank[6][:, t * S + s * P:t * S + (s + 1) * P], PC[:, t, s * P:(s + 1) * P], ident)
                    last.then_inc(a_turned, 1)
                    pe.wait_ge(a_pt, T.next(a_pt))
                    v = [VA[:, s, kv * AD:(kv + 1) * AD] for s in range(TT)]
                    for s in range(TT):
                        last = mm(bank[7][:, 0:S], v[s], PLT[:, s, :], start=s == 0, stop=s == TT - 1)
                    if nq > NT:
                        for s in range(NT):
                            last = mm(bank[7][:, S:TOK], v[NT + s], PCT[:, s, :], start=s == 0, stop=s == NT - 1)
                    last.then_inc(a_out, 1)

                for kv in range(AKV):
                    with T.loop(pe, AH // AKV, {a_gain: 1, a_q: 1, a_norm: 1, a_pt: 1}):
                        attend(kv)
                gated([(bt_ready, T.next(bt_ready, 2)) for s in range(SLOTS)])
                with T.loop(pe, 2, {lo_split: 4 * SLOTS} | {b: 4 for b in bank_free}):
                    for _ in range(4):
                        cols_product(4, AT, tq)
                gated([(bt_ready, T.next(bt_ready, 2)) for s in range(SLOTS)])
                ready = [(bt_ready, T.next(bt_ready)) for s in range(SLOTS)]
                loop_blocks(2, lambda: cols_product(4, BT, tq, ready=ready))
                sum_squares(tq)
            pe.wait_ge(x_ready, 3)
            for t in range(NT):
                for g in range(2):
                    for c in range(4):
                        last = turn(bank[4 + 2 * t + g][:, c * P:(c + 1) * P], xT[:, 4 * g + c, t * P:(t + 1) * P], ident)
                    last.then_inc(x_turned, 1)


INV_TURN = float(1.0 / (2.0 * 3.141592653589793))
ROUND = 1.5 * 2.0 ** 23
TURN_PARTS = (6.25, 0.033203125, 2.0 * 3.141592653589793 - 6.283203125)
PI_IN = 3.1415925

_BIG = ["x", "p", "e_w_in", "e_w_uq", "e_w_ukv", "e_w_out", "o_w_in", "o_w_out", "w_ff1", "w_ff2", "w_ple_gate", "w_ple_proj",
        "ctx_2", "w_ada_2", "w_in_2", "w_decay_fwd_2", "b_decay_fwd_2", "w_decay_bwd_2", "b_decay_bwd_2", "w_br_conv_2",
        "w_br_attn_2", "w_br_gla_2", "w_out_2"]


def shape_constants():
    import numpy as np

    c, f = np.zeros((P, NCONST), np.float32), np.zeros((P, NFIRST), np.float32)

    def put(a, where, name, v):
        a[:, where[name][0]:where[name][0] + where[name][1]] = v

    i = np.arange(P)
    put(c, CONST, "ident", np.eye(P))
    put(c, CONST, "tri_f", (i[:, None] <= i[None, :]) / 16.0)
    put(c, CONST, "tri_b", (i[:, None] >= i[None, :]) / 16.0)
    rot = np.zeros((P, P))
    for m in range(P):
        rot[m + 32 if m // 32 % 2 == 0 else m - 32, m] = -1.0 if m // 32 % 2 == 0 else 1.0
    put(c, CONST, "rot", rot)
    put(c, CONST, "ones", 1.0)
    freqs = np.float32(10000.0) ** (-np.arange(32, dtype=np.float32) * np.float32(2.0) / np.float32(64))
    t = np.arange(S)
    place = np.where((i // 64 == 0)[:, None], (t // 64)[None, :], (t % 64)[None, :]).astype(np.float32)
    angle = (place * freqs[i % 32][:, None]).astype(np.float32).astype(np.float64)
    put(c, CONST, "cos", np.cos(angle))
    put(c, CONST, "sin", np.sin(angle))
    q = np.concatenate([np.repeat(i[:, None], P, 1), np.repeat(P + i[:, None], S, 1)], 1)
    k = np.concatenate([np.arange(P), np.arange(S)])[None, :]
    d = q - k
    put(f, FIRST, "dist", np.where(d >= 0, d, 1e30))
    put(f, FIRST, "causal", np.where(d >= 0, 0.0, -1e30))
    count = sum(((d >= 0) & (d <= w) & (d % g == 0)).astype(np.int64) for w, g in ((128, 1), (512, 4), (2048, 16)))
    put(f, FIRST, "lncount", np.where(d < 0, 0.0, np.where(count > 0, np.log(np.maximum(count, 1)), -1e30)))
    half = ROPE // 2
    put(f, FIRST, "inv_freq", np.float32(10000.0) ** (-np.arange(half, dtype=np.float32) / np.float32(half)))
    put(f, FIRST, "dil_slope", -(2.0 ** (-8.0 * np.arange(1, HEADS_E + 1) / HEADS_E)))
    put(f, FIRST, "moba_slope", -(2.0 ** (-8.0 * np.arange(1, HEADS_O + 1) / HEADS_O)))
    put(f, FIRST, "inv_n_z", [1.0 / Q_LORA, 1.0 / KV_LORA, 1.0 / ROPE] + [1.0 / HD] * 2 * HEADS_E)
    put(f, FIRST, "inv_n_q", [1.0 / NOPE] * HEADS_E + [1.0 / ROPE] * HEADS_E + [1.0 / NOPE] * HEADS_E)
    return c, f


def level_masks():
    import numpy as np

    m = np.zeros((P, NMASK), np.int32)
    m[:, 0:P] = np.eye(P)
    s = np.arange(P)[:, None]
    for d in range(2):
        for n, half in enumerate(LEVELS):
            own = s // (2 * half) == np.arange(P // 2)[None, :] // half
            side = s % (2 * half) < half if d == 0 else s % (2 * half) >= half
            at = P + (d * len(LEVELS) + n) * (P // 2)
            m[:, at:at + P // 2] = own & side
    return m


def packed(inputs):
    import numpy as np

    c, f = shape_constants()
    col = np.zeros((P, NCOLS), np.float32)
    for name, (at, n) in COLS.items():
        if name == "cond":
            v = np.stack([np.asarray(inputs["c_2"]).reshape(KC, P), np.asarray(inputs["c_ctx_2"]).reshape(KC, P)], 1).reshape(-1, P)
        else:
            v = np.asarray(inputs[name]).reshape(n, -1)
        col[0:v.shape[1], at:at + n] = v.T
    at = FIRST["rope_gains"][0]
    f[:, at:at + ROPE] = np.broadcast_to(np.asarray(inputs["e_qn_rope"]).reshape(1, ROPE), (P, ROPE))
    f[:, at + ROPE:at + 2 * ROPE] = np.broadcast_to(np.asarray(inputs["e_kn_rope"]).reshape(1, ROPE), (P, ROPE))
    return {"const": c, "first": f, "cols": col, "mask": level_masks(),
            "pos": np.ascontiguousarray(np.asarray(inputs["positions"]).reshape(NT, P).T.astype(np.int32))}


def kernel(**inputs):
    import numpy as np
    import concourse.bacc as bacc
    from concourse import mybir as _mybir
    from concourse.bass_utils import run_bass_kernel_spmd

    nc = bacc.Bacc("TRN2", target_bir_lowering=False, num_devices=1)
    arrays = {name: np.ascontiguousarray(inputs[name]) for name in _BIG} | packed(inputs)
    io = {name: nc.dram_tensor("in_" + name, a.shape, _mybir.dt.from_np(a.dtype), kind="ExternalInput").ap()
          for name, a in arrays.items()}
    out = nc.dram_tensor("out", (1, S, D), _mybir.dt.float32, kind="ExternalOutput").ap()
    mixer_kernel(nc, io, out)
    run = run_bass_kernel_spmd(nc, [{"in_" + name: a for name, a in arrays.items()}], core_ids=[0])
    return run.results[0]["out"]
```

```python
from contextlib import ExitStack, contextmanager

import concourse.bass as bass
from concourse import mybir

F32 = mybir.dt.float32
F32R = mybir.dt.float32r
I32 = mybir.dt.int32
ALU = mybir.AluOpType
ACT = mybir.ActivationFunctionType
AX = mybir.AxisListType.X

P = 128
D = 1024
KC = D // P
S = 256
NT = S // P
EPS = 1e-6
RSQRT_SEED = float(0x5F3759DF)
BLK = 512
SLOTS = 4
FF_STEPS = 4
ADA_AFTER = (4, 5, 7, 8, 10, 11, 13, 14)
ADA_W = 3 * D // (2 * FF_STEPS)
UNIT = 1024
STD = [(2, BLK)] * SLOTS

Q_LORA, KV_LORA, ROPE, NOPE, HD = 384, 256, 32, 64, 64
O_KV, O_ROPE, O_DIL = Q_LORA, Q_LORA + KV_LORA, Q_LORA + KV_LORA + ROPE
HEADS_E, HEADS_O = 8, 16
DIL_W = HEADS_E * HD
EVEN_IN = O_DIL + 3 * DIL_W
ODD_W = HEADS_O * HD
MLA_D = NOPE + ROPE
MLA_SCALE = MLA_D ** -0.5
HD_SCALE = HD ** -0.5
KEYS = P + S


class Tally:

    def __init__(self):
        self.base, self.i = {}, None

    def now(self, sem):
        v = self.base.get(sem.name, 0)
        return v if self.i is None or sem.name not in self.per else v + self.i * self.per[sem.name]

    def next(self, sem, n=1):
        self.base[sem.name] = self.base.get(sem.name, 0) + n
        assert self.i is None or sem.name in self.per, f"{sem.name} counts in a loop"
        return self.now(sem)

    @contextmanager
    def loop(self, eng, n, per):
        start = dict(self.base)
        with eng.Fori(0, n, 1) as i:
            self.i, self.per = i, {s.name: k for s, k in per.items()}
            yield i
        for name, k in self.per.items():
            got = self.base.get(name, 0) - start.get(name, 0)
            assert got == k, f"{name}: {got} per iteration, {k} stated"
            self.base[name] = start.get(name, 0) + n * k
        self.i = None


def layout(sizes):
    at, out = 0, {}
    for name, n in sizes:
        out[name] = (at, n)
        at += n
    return out, at


COLS, NCOLS = layout([
    ("mix_norm", 2 * KC), ("ff_norm", 2 * KC), ("ple_norm", 2 * KC), ("e_cq_norm", 3), ("e_ckv_norm", 2),
    ("e_qn_nope", 1), ("e_kn_nope", 1), ("e_dil_qn", 1), ("e_dil_kn", 1), ("o_qn", 1), ("o_kn", 1),
    ("g_pre_2", 2 * KC), ("g_post_2", 2 * KC), ("b_ada_2", 6 * KC), ("conv_w_2", 6 * KC), ("b_gate_2", 6 * KC),
    ("gla_norm_g_2", 4), ("q_norm_g_2", 2), ("k_norm_g_2", 2), ("cond", 2 * KC)])
CONST, NCONST = layout([("ident", P), ("tri_f", P), ("tri_b", P), ("rot", P), ("ones", P), ("cos", S), ("sin", S)])
FIRST, NFIRST = layout([
    ("dist", KEYS), ("lncount", KEYS), ("causal", KEYS), ("inv_freq", ROPE // 2), ("dil_slope", HEADS_E),
    ("moba_slope", HEADS_O), ("inv_n_z", 3 + 2 * HEADS_E), ("inv_n_q", 3 * HEADS_E), ("rope_gains", 2 * ROPE)])
NSTAT_Z, NSTAT_Q = 3 + 2 * HEADS_E, 3 * HEADS_E


def weight_plan(io):
    def std(w, row=lambda i: 0, col=lambda i: 0):
        return [(w, (lambda i, row=row, c=c: row(i) + 2 * c * P), col, 2, BLK) for c in range(SLOTS)]

    def cols(w, blocks, c0=0):
        return (blocks // 2, [std(w, col=lambda i, h=h: c0 + i * 2 * BLK + h * BLK) for h in range(2)])

    def fixed(v):
        return lambda i: v

    segments = []
    e_in = io["e_w_in"][0]
    segments.append(("e_in",) + cols(e_in, 4))
    segments.append(("e_tail", 1, [[(e_in, fixed(2 * c * P), fixed(4 * BLK), 2, EVEN_IN - 4 * BLK) for c in range(SLOTS)]]))
    uq, ukv = io["e_w_uq"][0], io["e_w_ukv"][0]
    segments.append(("uq", 1, [[(uq, fixed(0), fixed(0), 2, BLK), (uq, fixed(2 * P), fixed(0), 1, BLK),
                                (uq, fixed(0), fixed(BLK), 2, BLK // 2), (uq, fixed(2 * P), fixed(BLK), 1, BLK // 2)]]))
    segments.append(("ukv", 1, [[(ukv, fixed(c * P), fixed(b * BLK), 1, BLK) for b in range(2) for c in range(2)]]))
    for layer in range(2):
        if layer:
            segments.append(("o_in",) + cols(io["o_w_in"][0], 6))
        segments.append((f"mix_out{layer}",) + cols(io["o_w_out" if layer else "e_w_out"][0], 2))
        ff1, ff2, proj = io["w_ff1"][layer], io["w_ff2"][layer], io["w_ple_proj"][layer]
        a1, b1 = (std(ff1, col=lambda i, h=h: i * D + h * BLK) for h in range(2))
        a2, b2 = (std(ff2, row=lambda i: i * D, col=fixed(h * BLK)) for h in range(2))
        segments.append((f"ff{layer}", FF_STEPS, [a1, b1, a2, b2]))
        segments.append((f"gate{layer}",) + cols(io["w_ple_gate"][layer], 2))
        segments.append((f"proj{layer}", 1, [[(proj, fixed(c * P), fixed(b * BLK), 1, BLK) for b in range(2) for c in range(2)]]))
    return segments


C_CONV_B, C_CONV_C, C_CONV_X, C_CONV_Z = 0, D, 2 * D, 3 * D
C_Q = 4 * D
AH, AKV, AD = 8, 2, 128
C_K = C_Q + AH * AD
C_V = C_K + AKV * AD
C_ZA = C_V + AKV * AD
GH, GDK, GDV, RANK = 4, 128, 256, 16
C_GQ = C_ZA + AH * AD
C_GK = C_GQ + GH * GDK
C_GV = C_GK + GH * GDK
C_R = C_GV + GH * GDV
C_ZG = C_R + 2 * RANK
C_MG = C_ZG + D
ATTN_SCALE = AD ** -0.5
TOK = 2 * S
TT = TOK // P
LEVELS = [P >> (n + 1) for n in range(7)]
TILES = {0: [2, 3, 0, 1], 1: [3, 2, 1, 0]}
NMASK = (1 + len(LEVELS)) * P
TRI_TILE, TRI_LEVEL, TRI_LAST = 0, 4 * P, 4 * P + 2 * P * (len(LEVELS) - 1)
NTRI = TRI_LAST + P


def second_plan(io):
    def std(w, c0=0, per=0, width=BLK):
        return [(w, (lambda i, c=c: 2 * c * P), (lambda i: c0 + i * per), 2, width) for c in range(SLOTS)]

    out = []
    for layer in range(2):
        w, n = io["w_in_2"][layer], layer

        def gated(name, b, br):
            return (f"{name}{n}", 1, [std(w, C_MG + b * D + half * BLK) for half in range(2)] + [std(br, half * BLK) for half in range(2)])

        out += [
            (f"gq{n}", 1, [std(w, C_GQ)]), (f"gk{n}", 1, [std(w, C_GK)]), (f"gr{n}", 1, [std(w, C_R, width=P)]),
            (f"gv{n}", 2, [std(w, C_GV, BLK)]), (f"zg{n}", 2, [std(w, C_ZG, BLK)]),
            gated("mgc", 2, io["w_br_gla_2"][layer]),
            (f"q{n}", 2, [std(w, C_Q, BLK)]), (f"k{n}", 1, [std(w, C_K, width=AKV * AD)]),
            (f"v{n}", 1, [std(w, C_V, width=AKV * AD)]), (f"za{n}", 2, [std(w, C_ZA, BLK)]),
            gated("mgb", 1, io["w_br_attn_2"][layer]),
            (f"conv{n}", 2, [std(w, c, BLK) for c in (C_CONV_B, C_CONV_C, C_CONV_X, C_CONV_Z)]),
            gated("mga", 0, io["w_br_conv_2"][layer]),
            (f"out{n}", 2, [std(io["w_out_2"][layer], 0, BLK)]),
        ]
    return out


def sizes(quad):
    return [(k, w) for _, _, _, k, w in quad]


def mixer_kernel(nc, io, out):
    plan = weight_plan(io) + second_plan(io)
    quads = [(name, sizes(q)) for name, _, qs in plan for q in qs]

    with ExitStack() as ctx:
        def sb(name, shape, dt=F32):
            return ctx.enter_context(nc.sbuf_tensor(name, shape, dt))

        def sem(name):
            return ctx.enter_context(nc.semaphore(name))

        RAW = sb("RAW", [P, SLOTS, UNIT])
        WHI = sb("WHI", [P, SLOTS, UNIT], F32R)
        WLO = sb("WLO", [P, SLOTS, UNIT], F32R)
        ATH = sb("ATH", [P, KC, 2 * S], F32R)
        ATL = sb("ATL", [P, KC, 2 * S], F32R)
        COL = sb("COL", [P, NCOLS])
        CST = sb("CST", [P, NCONST])
        STAT = sb("STAT", [P, 256])
        h = sb("h", [P, NT, D])
        ARENA = sb("ARENA", [P, 19 * 1024])
        bank = [ctx.enter_context(nc.psum_tensor(f"bank{b}", [P, BLK], F32)) for b in range(8)]

        def col(name, i=0, rows=P):
            return COL[0:rows, COLS[name][0] + i:COLS[name][0] + i + 1]

        def cst(name):
            return CST[:, CONST[name][0]:CONST[name][0] + CONST[name][1]]

        ident = cst("ident")
        top = [0]

        def view(n):
            top[0] += n
            return ARENA[:, top[0] - n:top[0]]

        Z = view(NT * 3 * ODD_W)
        ze = Z[:, 0:NT * EVEN_IN].rearrange("p (t n) -> p t n", t=NT)
        zo = Z.rearrange("p (t n) -> p t n", t=NT)
        Q = view(NT * HEADS_E * MLA_D).rearrange("p (t n) -> p t n", t=NT)
        KV = view(NT * HEADS_E * (NOPE + HD)).rearrange("p (t n) -> p t n", t=NT)
        mixed = view(NT * D).rearrange("p (t n) -> p t n", t=NT)
        scaled = mixed
        STAGE = view(2 * 2 * NT * MLA_D).rearrange("p (b g d) -> p b g d", b=2, g=2 * NT)
        QKT = view(2 * 2 * S).rearrange("p (b n) -> p b n", b=2)
        PROB = view(2 * KEYS).rearrange("p (b n) -> p b n", b=2)
        PROBT = view(2 * KEYS).rearrange("p (b n) -> p b n", b=2)
        FST = view(NFIRST)
        VAL = view(KC * S).rearrange("p (c n) -> p c n", c=KC)
        PIN = view(NT * 256).rearrange("p (t n) -> p t n", t=NT)
        assert top[0] <= 19 * 1024, top[0]
        GATE = Z[:, 0:NT * D].rearrange("p (t n) -> p t n", t=NT)
        RELU = Z[:, 2 * D:2 * D + 4 * S].rearrange("p (b n) -> p b n", b=4)
        PVAL = Z[:, 2 * D:2 * D + 2 * S]
        TMP = Z[:, 3 * D:3 * D + BLK]
        SQU = Z[:, 3 * D + BLK:3 * D + BLK + 2 * S].rearrange("p (b n) -> p b n", b=2)
        PTMP = Q

        def fst(name):
            return FST[:, FIRST[name][0]:FIRST[name][0] + FIRST[name][1]]

        ss, rs, nt1 = STAT[:, 0:48], STAT[:, 48:96], STAT[:, 96:144]
        rs_z = STAT[:, 144:144 + 2 * NSTAT_Z].rearrange("p (t n) -> p t n", t=NT)
        NMAX = STAT[:, 182:186].rearrange("p (b t) -> p b t", b=2)
        DEN = STAT[:, 186:190].rearrange("p (b t) -> p b t", b=2)
        RDEN = STAT[:, 190:194].rearrange("p (b t) -> p b t", b=2)
        GQK = STAT[:, 194:197]
        POSF = STAT[:, 197:199]
        RSZO = sb("RSZO", [P, 2, NT, 2 * HEADS_O])
        POS = sb("POS", [P, NT], I32)
        TRIG = sb("TRIG", [P, 5, NT, ROPE // 2])
        KROPE = sb("KROPE", [P, NT, ROPE])
        QROPE = VAL[:, 4:6, :].rearrange("p t (h n) -> p t h n", h=HEADS_E)
        ROT = VAL[:, 6:8, :].rearrange("p c (b h n) -> p (c b) h n", b=2, h=HEADS_E)
        ZERO = sb("ZERO", [1, BLK], mybir.dt.bfloat16)
        SPARE = sb("SPARE", [P, BLK])

        MOD = sb("MOD", [P, 2, 3 * KC, 2])
        ACC = [ARENA[:, base:base + 3 * D] for base in (NT * 3 * ODD_W, NT * (3 * ODD_W + HEADS_E * (MLA_D + NOPE + HD) + D))]
        ADA = ARENA[:, NT * (3 * ODD_W + HEADS_E * (MLA_D + NOPE + HD)):][:, 0:4 * ADA_W].rearrange("p (b n) -> p b n", b=2)
        CTMP = sb("CTMP", [P, 2 * KC])[:, :]

        x_in, inputs_in = sem("x_in"), sem("inputs_in")
        cond_sig, ada_used, ada_acc, ada_sums = (sem(n) for n in ("cond_sig", "ada_used", "ada_acc", "ada_sums"))
        ada_landed = [sem(f"ada_landed{b}") for b in range(2)]
        p_in, p_used = sem("p_in"), sem("p_used")
        raw_landed = [sem(f"raw_landed{s}") for s in range(SLOTS)]
        hi_split, lo_split = sem("hi_split"), sem("lo_split")
        gemm_step = sem("gemm_step")
        bank_free = [sem(f"bank_free{b}") for b in range(4)]
        rows_ready = sem("rows_ready")
        turned = sem("turned")
        chunk_val = sem("chunk_val")
        at_ready = sem("at_ready")
        u_ready = sem("u_ready")
        relu_done = sem("relu_done")
        trig_ready, trig_done = sem("trig_ready"), sem("trig_done")
        staged, qk_turned, qk_ready = sem("staged"), sem("qk_turned"), sem("qk_ready")
        scored, max_ready, probs_ready = sem("scored"), sem("max_ready"), sem("probs_ready")
        probs_turned, probs_t_ready, head_out = sem("probs_turned"), sem("probs_t_ready"), sem("head_out")
        acc_open = sem("acc_open")
        gated = sem("gated")
        zeroed = sem("zeroed")
        stored = sem("stored")

        BTH = sb("BTH", [P, KC, TOK], F32R)
        BTL = sb("BTL", [P, KC, TOK], F32R)
        EBL = sb("EBL", [P, 2, TT])
        TMPA = sb("TMPA", [P, 1])[:, :]
        one = cst("ones")[:, 0:1]

        def at(base, n, pattern=None, **kw):
            a = ARENA[:, base:base + n]
            return a.rearrange(pattern, **kw) if pattern else a

        xT = at(6144, KC * TOK, "p (c n) -> p c n", c=KC)
        CTXIN = at(4096, NT * D, "p (t n) -> p t n", t=NT)
        SQX = at(0, KC * TOK)
        RB, VB, TB = at(11264, TOK), at(11776, TOK), at(12288, TOK)
        W0 = at(12800, 2 * TOK, "p (b n) -> p b n", b=2)
        W1 = at(13824, 2 * TOK, "p (b n) -> p b n", b=2)
        VG = at(0, TT * D, "p (t n) -> p t n", t=TT)
        GQ = at(4096, GH * TOK)
        GK = at(10240, GH * TOK)
        RA = SPARE[0:2 * RANK + 1, 0:TOK]
        P1 = at(12288, 4 * TOK, "p (k d n) -> p k d n", k=2, d=2)
        LOGS = P1[:, 0, :, :]
        P2 = at(14336, 4 * TOK, "p (l b k n) -> p l b k n", l=2, b=2, k=2)
        LASTE = at(14336, TOK)
        LAST = at(14336 + TOK, TOK)
        STATE = at(16384, 6 * GDV, "p (d s v) -> p d s v", d=2, s=3)
        ON = at(16384, TT * GDV, "p (t n) -> p t n", t=TT)
        ATT = at(17920, TOK)
        K2X = at(18432, TOK)
        TRI = BTH[:, :, :].rearrange("p c n -> p (c n)")[:, 0:NTRI]
        TRIRAW = at(14848, NTRI)
        LAS = BTL[:, 0:4, :].rearrange("p (s d) (t n) -> p s d t n", s=2, t=TT)
        hflat = h.rearrange("p t n -> p (t n)")
        MASK = hflat[:, 0:NMASK].bitcast(I32)
        WD = h[0:2 * RANK + 1, 1, :].rearrange("p (d n) -> p d n", d=2)
        assert NMASK <= D
        Y = at(0, KC * TOK, "p (c n) -> p c n", c=KC)
        SIGZ = at(14336, KC * TOK)
        G = [at(base, 4 * TOK, "p (c n) -> p c n", c=4) for base in (10240, 4096)]
        WG = at(18944, TOK)
        VA = at(4096, TT * AKV * AD, "p (t n) -> p t n", t=TT)
        K2 = at(5120, AKV * TOK, "p (k n) -> p k n", k=AKV)
        QG = at(10240, (AH + AKV) * TOK)
        KG = at(10240 + AH * TOK, AKV * TOK, "p (k n) -> p k n", k=AKV)
        SQQ = at(15360, AH * TOK)
        SQK = at(5120, AKV * TOK)
        DIAG = at(16384, AKV * TT * P, "p (k t n) -> p k t n", k=AKV, t=TT)
        QS = at(15360, 2 * TOK, "p (r n) -> p r n", r=2)
        PL = at(16384, 2 * NT * TOK, "p (r t n) -> p r t n", r=2, t=NT)
        PC = at(18432, 2 * NT * S, "p (r t n) -> p r t n", r=2, t=NT)
        PLT = at(16384, 2 * TT * S, "p (r s n) -> p r s n", r=2, s=TT)
        PCT = at(18432, 2 * NT * S, "p (r s n) -> p r s n", r=2, s=NT)
        ROTW = SPARE[:, :].rearrange("p (r n) -> p r n", r=2)
        SIGA = at(15360, KC * TOK)
        AB = at(4096, 4 * TOK, "p (c n) -> p c n", c=4)
        AC = at(10240, 4 * TOK, "p (c n) -> p c n", c=4)
        PX = at(12288, 4 * TOK, "p (c n) -> p c n", c=4)
        CV = at(14336, 4 * TOK, "p (c n) -> p c n", c=4)
        SIGC = at(16384, 4 * TOK)
        OUT = at(14848, KC * TOK, "p (c n) -> p c n", c=KC)
        RSQ = STAT[:, 0:AH * TT + AKV * TT]
        RSV, RSW = STAT[:, 48:48 + 40], STAT[:, 96:96 + 40]
        SCL, NM, DN, RD = (STAT[:, 144 + 8 * n:152 + 8 * n].rearrange("p (r t) -> p r t", r=2) for n in range(4))
        GS, GR, GT = (STAT[:, 176 + 4 * n:180 + 4 * n] for n in range(3))

        ctx_in, mask_in, wd_in = sem("ctx_in"), sem("mask_in"), sem("wd_in")
        out_sq, x_turned, x_ready = sem("out_sq"), sem("x_turned"), sem("x_ready")
        sq_ready, sq_sums = sem("sq_ready"), sem("sq_sums")
        sig_done, bt_ready, inputs_ready = sem("sig_done"), sem("bt_ready"), sem("inputs_ready")
        tri_in, tri_ready = sem("tri_in"), sem("tri_ready")
        g_pre, g_logs, g_la, g_qb, g_kc, g_diff, g_exp = (sem(n) for n in ("g_pre", "g_logs", "g_la", "g_qb", "g_kc", "g_diff", "g_exp"))
        g_keys, g_kturned, g_kready, g_pair, g_level = (sem(n) for n in ("g_keys", "g_kturned", "g_kready", "g_pair", "g_level"))
        g_outer, g_state, g_att, g_out, g_rows, g_turned = (sem(n) for n in ("g_outer", "g_state", "g_att", "g_out", "g_rows", "g_turned"))
        a_sq, a_sums, a_stored, a_diag, a_bc, a_gain, a_rot, a_q, a_score = (sem(n) for n in ("a_sq", "a_sums", "a_stored", "a_diag", "a_bc", "a_gain", "a_rot", "a_q", "a_score"))
        a_max, a_exp, a_norm, a_turned, a_pt, a_out = (sem(n) for n in ("a_max", "a_exp", "a_norm", "a_turned", "a_pt", "a_out"))
        out_rows = sem("out_rows")

        block = ctx.enter_context(nc.Block())

        @block.sync
        def _(sp):
            T = Tally()

            def load_modulation(layer, i, k):
                row, column = k % SLOTS * 2 * P, i * 2 * ADA_W + k // SLOTS * ADA_W
                src = io["w_ada_2"][layer][row:row + 2 * P, bass.ds(column, ADA_W)].rearrange("(c p) n -> p c n", p=P)
                sp.wait_ge(ada_used, T.next(ada_used))
                sp.dma_start(ADA[:, k % 2, :].rearrange("p (c n) -> p c n", c=2), src).then_inc(ada_landed[k % 2], 16)

            def load_quads(qs, i, modulation=None):
                for n, quad in enumerate(qs):
                    for slot, (w, row, column, k, width) in enumerate(quad):
                        src = w[bass.ds(row(i), k * P), bass.ds(column(i), width)].rearrange("(c p) n -> p c n", p=P)
                        sp.wait_ge(lo_split, T.next(lo_split))
                        sp.dma_start(RAW[:, slot, 0:k * width].rearrange("p (c n) -> p c n", c=k), src) \
                            .then_inc(raw_landed[slot], 16)
                        if modulation is not None and n * SLOTS + slot in ADA_AFTER:
                            load_modulation(modulation, i, ADA_AFTER.index(n * SLOTS + slot))

            for name, n, qs in plan:
                if n == 1:
                    load_quads(qs, 0)
                else:
                    modulation = int(name[-1]) if name in ("ff0", "ff1") else None
                    with T.loop(sp, n, {lo_split: SLOTS * len(qs), ada_used: 0 if modulation is None else 2 * SLOTS}) as i:
                        load_quads(qs, i, modulation)
                    if modulation is not None:
                        T.next(ada_used, 2)
            for t in range(NT):
                sp.wait_ge(out_rows, 2 * (t + 1))
                sp.dma_start(out[0][t * P:(t + 1) * P, :], h[:, t, :]).then_inc(stored, 16)
            sp.wait_ge(stored, 16 * NT)

        @block.gpsimd
        def _(pool):
            T = Tally()
            nc.gpsimd.memset(ZERO[:, :], 0.0).then_inc(zeroed, 1)
            pool.sem_inc(lo_split, SLOTS)

            def lo_quad(quad):
                for slot, (k, width) in enumerate(quad):
                    pool.wait_ge(hi_split, T.next(hi_split))
                    n = k * width
                    nc.gpsimd.tensor_tensor(WLO[:, slot, 0:n], RAW[:, slot, 0:n], WHI[:, slot, 0:n], ALU.subtract) \
                        .then_inc(lo_split, 1)

            def gla(layer):
                tq = TOK if layer == 0 else S
                steps = 4 + (len(LEVELS) - 1) * (tq // S) + 1
                with T.loop(pool, GH, {g_exp: steps}) as i:
                    k = GK[:, bass.ds(i * TOK, TOK)]
                    q = GQ[:, bass.ds(i * TOK, tq)].rearrange("p (o n) -> p o n", o=1).to_broadcast([P, 2, tq])
                    pool.wait_ge(g_exp, T.next(g_exp, 4))
                    nc.gpsimd.tensor_tensor(K2X, k, k, ALU.add).then_inc(g_kc, 1)
                    for d, end in enumerate((P - 1, 0)):
                        nc.gpsimd.tensor_copy(EBL[:, d, :], P1[:, 1, d, :].rearrange("p (t n) -> p t n", t=TT)[:, :, end])
                    pool.drain()
                    nc.gpsimd.tensor_tensor(P1[:, 1, :, 0:tq], P1[:, 1, :, 0:tq], q, ALU.mult).then_inc(g_qb, 1)
                    T.next(g_exp, steps - 4)

            for name, n, qs in plan:
                split = [sizes(q) for q in qs]
                if name.startswith("zg"):
                    gla(int(name[-1]))
                if n == 1:
                    for q in split:
                        lo_quad(q)
                else:
                    with T.loop(pool, n, {hi_split: SLOTS * len(split)}):
                        for q in split:
                            lo_quad(q)

        @block.scalar
        def _(act):
            T = Tally()
            for t in range(NT):
                act.dma_start(h[:, t, :], io["x"][0][t * P:(t + 1) * P, :]).then_inc(x_in, 16)
            act.dma_start(CST[:, :], io["const"]).then_inc(inputs_in, 16)
            act.dma_start(COL[:, :], io["cols"]).then_inc(inputs_in, 16)
            act.dma_start(FST[:, :], io["first"]).then_inc(inputs_in, 16)
            act.dma_start(POS[:, :], io["pos"]).then_inc(inputs_in, 16)
            act.dma_start(PIN[:, :, :], io["p"][0, 0].rearrange("(t p) n -> p t n", p=P)).then_inc(p_in, 16)

            def hi_unit(slot, k, width):
                act.wait_ge(raw_landed[slot], T.next(raw_landed[slot], 16))
                n = k * width
                nc.scalar.activation(WHI[:, slot, 0:n], RAW[:, slot, 0:n], ACT.Copy).then_inc(hi_split, 1)

            def hi_quad(quad, steps, groups):
                for slot, (k, width) in enumerate(quad):
                    act.wait_ge(gemm_step, steps + (slot + 1) * groups)
                    hi_unit(slot, k, width)

            order = [q for _, q in quads] + [None]

            def segment(name, groups, work=lambda j, base: None, per=None):
                at = [n for n, _ in quads].index(name)
                n, qs = next((n, qs) for s, n, qs in plan if s == name)
                own = [q for q in quads if q[0] == name]

                def step(j, nxt):
                    base = T.now(gemm_step)
                    if nxt is not None:
                        hi_quad(nxt, base, groups[j])
                    T.next(gemm_step, SLOTS * groups[j])
                    work(j, base)

                after = order[at + len(own)]
                loops = n if after == STD else n - 1
                if loops > 0:
                    counts = {gemm_step: SLOTS * sum(groups)} | {r: 16 * len(qs) for r in raw_landed} | (per or {})
                    with T.loop(act, loops, counts):
                        for j in range(len(own)):
                            step(j, STD)
                for _ in range(n - loops):
                    for j in range(len(own)):
                        step(j, order[at + j + 1])
            def chunks_out(count, gain):
                for g in range((count + 1) // 2):
                    act.wait_ge(turned, T.next(turned))
                    for c in range(2 * g, min(2 * g + 2, count)):
                        o = (c % 2) * S
                        last = nc.scalar.activation(VAL[:, c, :], bank[4 + g % 4][:, o:o + S], ACT.Copy,
                                                    scale=gain(c))
                    last.then_inc(chunk_val, 1)

            def heads(n, d, kind):
                def operands(par):
                    act.wait_ge(qk_turned, T.next(qk_turned))
                    nc.scalar.activation(QKT[0:d, par, 0:S], bank[par][0:d, 0:S], ACT.Copy)
                    nc.scalar.activation(QKT[0:d, par, S:2 * S], bank[par][0:d, S:2 * S], ACT.Copy,
                                         scale=GQK[0:d, kind:kind + 1]).then_inc(qk_ready, 1)

                def pair(ahead):
                    for par in range(2):
                        act.wait_ge(max_ready, T.next(max_ready))
                        for t in range(NT):
                            part = PROB[:, par, 0:P] if t == 0 else PROB[:, par, P:KEYS]
                            last = nc.scalar.activation(part, part, ACT.Exp, bias=NMAX[:, par, t:t + 1],
                                                        accum_out=DEN[:, par, t:t + 1])
                        last.then_inc(probs_ready, 1)
                    if ahead:
                        for par in range(2):
                            operands(par)
                    for par in range(2):
                        act.wait_ge(probs_turned, T.next(probs_turned))
                        nc.scalar.activation(PROBT[:, par, :], bank[4 + par][:, 0:KEYS], ACT.Copy) \
                            .then_inc(probs_t_ready, 1)

                for par in range(2):
                    operands(par)
                with T.loop(act, n // 2 - 1, {qk_turned: 2, max_ready: 2, probs_turned: 2}):
                    pair(True)
                pair(False)

            for slot, (k, width) in enumerate(STD):
                hi_unit(slot, k, width)
            for layer in range(2):
                chunks_out(KC, lambda c: col("mix_norm", layer * KC + c))
                if layer == 0:
                    act.wait_ge(trig_ready, 1)
                    nc.scalar.activation(TRIG[:, 4, :, :], TRIG[:, 2, :, :], ACT.Sin)
                    nc.scalar.activation(TRIG[:, 3, :, :], TRIG[:, 2, :, :], ACT.Sin, scale=0.5).then_inc(trig_done, 1)
                    nc.scalar.activation(CTMP, COL[:, COLS["cond"][0]:COLS["cond"][0] + 2 * KC], ACT.Sigmoid).then_inc(cond_sig, 1)
                    segment("e_in", [2, 2])
                    segment("e_tail", [2])
                    chunks_out(5, lambda c: col("e_cq_norm", c) if c < 3 else col("e_ckv_norm", c - 3))
                    segment("uq", [2])
                    segment("ukv", [2])
                    heads(HEADS_E, MLA_D, 0)
                    heads(HEADS_E, HD, 1)
                else:
                    segment("o_in", [2, 2])
                    heads(HEADS_O, HD, 2)
                chunks_out(KC, lambda c: 1.0)
                if layer:
                    act.dma_start(CTXIN, io["ctx_2"][0].rearrange("(t p) n -> p t n", p=P)).then_inc(ctx_in, 16)
                segment(f"mix_out{layer}", [2, 2])
                chunks_out(KC, lambda c: col("ff_norm", layer * KC + c))

                def relu(j, base):
                    if j < 2:
                        for c in range(4):
                            act.wait_ge(u_ready, T.next(u_ready))
                            act.wait_ge(gemm_step, base + 4 * (SLOTS - 1) + c + 1)
                            nc.scalar.activation(RELU[:, c, :], bank[c][:, 0:S], ACT.Relu).then_inc(bank_free[c], 1)

                segment(f"ff{layer}", [4, 4, 2, 2], relu, {u_ready: 8})
                act.wait_ge(turned, T.next(turned))
                nc.scalar.activation(PVAL, bank[0][:, :], ACT.Copy).then_inc(chunk_val, 1)
                chunks_out(KC, lambda c: col("ple_norm", layer * KC + c))

                def sigmoid(j, base):
                    for t in range(NT):
                        act.wait_ge(gemm_step, base + NT * (SLOTS - 1) + t + 1)
                        nc.scalar.activation(GATE[:, t, j * BLK:(j + 1) * BLK], bank[2 * j + t][:, :], ACT.Sigmoid) \
                            .then_inc(bank_free[2 * j + t], 1)

                segment(f"gate{layer}", [2, 2], sigmoid)
                if layer == 0:
                    act.dma_start(PIN[:, :, :], io["p"][1, 0].rearrange("(t p) n -> p t n", p=P)).then_inc(p_in, 16)
                segment(f"proj{layer}", [2])
            act.wait_ge(x_turned, T.next(x_turned, 8))
            act.dma_start(MASK, io["mask"]).then_inc(mask_in, 16)

            def load_decay(layer):
                for d, name in enumerate(("fwd", "bwd")):
                    act.dma_start(WD[d * RANK:(d + 1) * RANK, d, :], io[f"w_decay_{name}_2"][layer]).then_inc(wd_in, 16)
                    act.dma_start(WD[2 * RANK:2 * RANK + 1, d, :], io[f"b_decay_{name}_2"][layer:layer + 1, :]).then_inc(wd_in, 16)

            act.wait_ge(inputs_ready, 1)
            load_decay(0)

            for layer in range(2):
                tq = TOK if layer == 0 else S
                nq = tq // P
                for c in range(KC):
                    act.wait_ge(x_ready, T.next(x_ready))
                    nc.scalar.activation(SQX[:, c * TOK:(c + 1) * TOK], xT[:, c, :], ACT.Square).then_inc(sq_ready, 1)
                act.dma_start(TRIRAW, io["tri"]).then_inc(tri_in, 16)
                act.wait_ge(tri_in, 16 * (layer + 1))
                nc.scalar.activation(TRI, TRIRAW, ACT.Copy).then_inc(tri_ready, 1)
                segment(f"gq{layer}", [4])
                segment(f"gk{layer}", [4])
                segment(f"gr{layer}", [1])
                segment(f"gv{layer}", [4])

                def sigmoid_z(room, halves=2):
                    def work(j, base):
                        half = T.i if halves == 2 else 0
                        for c in range(4):
                            act.wait_ge(gemm_step, base + 4 * (SLOTS - 1) + c + 1)
                            nc.scalar.activation(room[:, bass.ds(half * 4 * TOK + c * TOK, tq)], bank[c][:, 0:tq], ACT.Sigmoid) \
                                .then_inc(sig_done, 1)
                    return work

                nb = tq // S

                def gla_logs():
                    act.wait_ge(g_pre, T.next(g_pre))
                    for d in range(2):
                        nc.scalar.activation(LOGS[:, d, :], bank[2 + d][:, :], ACT.Abs)
                    act.drain()
                    nc.scalar.activation(LOGS, LOGS, ACT.Exp, scale=-1.0)
                    act.drain()
                    nc.scalar.activation(LOGS, LOGS, ACT.Ln, bias=one).then_inc(g_logs, 1)

                def exps(dst, src):
                    act.wait_ge(g_diff, T.next(g_diff))
                    nc.scalar.activation(dst, src, ACT.Exp).then_inc(g_exp, 1)

                def two(b):
                    return bank[b][:, :].rearrange("p (k n) -> p k n", k=2)

                def gla_tiles():
                    for b in range(4):
                        exps(P1[:, :, b // 2, b % 2 * S:(b % 2 + 1) * S], two(b))

                def gla_head(ahead):
                    act.wait_ge(g_kturned, T.next(g_kturned))
                    for d in range(2):
                        last = nc.scalar.activation(P1[:, 0, d, :], bank[4 + d][:, :], ACT.Copy)
                    last.then_inc(g_kready, 1)
                    for n in range(len(LEVELS)):
                        if n >= 2:
                            act.wait_ge(g_level, T.now(g_level) + n)
                        if n == len(LEVELS) - 1:
                            exps(LASTE[:, 0:tq], bank[0][:, 0:tq])
                        else:
                            for b in range(nb):
                                exps(P2[:, n % 2, b, :, :], two(2 * n % 4 + b))
                    T.next(g_level, 1 + len(LEVELS))
                    if ahead:
                        gla_logs()
                        gla_tiles()

                gla_logs()
                gla_tiles()
                with T.loop(act, GH - 1, {g_kturned: 1, g_diff: 4 + (len(LEVELS) - 1) * nb + 1, g_level: 1 + len(LEVELS), g_pre: 1}):
                    gla_head(True)
                gla_head(False)
                if layer == 0:
                    load_decay(1)
                segment(f"zg{layer}", [4], sigmoid_z(SIGZ))

                def sigmoid_g(b):
                    def work(j, base):
                        if j < 2:
                            for c in range(4):
                                act.wait_ge(gemm_step, base + 4 * (SLOTS - 1) + c + 1)
                                nc.scalar.activation(G[j][:, c, 0:tq], bank[c][:, 0:tq], ACT.Sigmoid,
                                                     bias=col("b_gate_2", (layer * 3 + b) * KC + j * 4 + c)).then_inc(bank_free[c], 1)
                    return work

                segment(f"mgc{layer}", [4] * 4, sigmoid_g(2))
                def square_heads(room, count, w):
                    def work(j, base):
                        block = 0 if count < 4 else T.i if T.i is not None else 1
                        for c in range(count):
                            act.wait_ge(gemm_step, base + count * (SLOTS - 1) + c + 1)
                            nc.scalar.activation(room[:, bass.ds(block * 4 * TOK + c * TOK, w)], bank[c][:, 0:w], ACT.Square).then_inc(a_sq, 1)
                    return work

                segment(f"q{layer}", [4], square_heads(SQQ, 4, tq))
                segment(f"k{layer}", [AKV], square_heads(SQK, AKV, TOK))
                segment(f"v{layer}", [4])

                def attend():
                    for r in range(2):
                        act.wait_ge(a_max, T.next(a_max))
                        for t in range(nq):
                            dst, src = (PL[:, r, t, :], bank[3 * r + t][:, :]) if t < NT else \
                                (PC[:, r, t - NT, :], bank[3 * r + 2][:, (t - NT) * S:(t - NT + 1) * S])
                            last = nc.scalar.activation(dst, src, ACT.Exp, bias=NM[:, r, t:t + 1], scale=SCL[:, r, t:t + 1],
                                                        accum_out=DN[:, r, t:t + 1])
                        last.then_inc(a_exp, 1)
                    for r in range(2):
                        act.wait_ge(a_turned, T.next(a_turned))
                        for t in range(NT):
                            last = nc.scalar.activation(PLT[:, r, :, t * P:(t + 1) * P],
                                                        bank[3 * r + t][:, :].rearrange("p (s n) -> p s n", s=TT), ACT.Copy)
                        if nq > NT:
                            last = nc.scalar.activation(PCT[:, r, :, :].rearrange("p s (t n) -> p s t n", t=NT),
                                                        bank[3 * r + 2][:, :].rearrange("p (t s n) -> p s t n", t=NT, s=NT), ACT.Copy)
                        last.then_inc(a_pt, 1)

                with T.loop(act, AH // 2, {a_max: 2, a_turned: 2}):
                    attend()
                segment(f"za{layer}", [4], sigmoid_z(SIGA))
                segment(f"mgb{layer}", [4] * 4, sigmoid_g(1))

                def conv_z(j, base):
                    if j == 3:
                        sigmoid_z(SIGC, 1)(j, base)

                segment(f"conv{layer}", [4] * 4, conv_z)
                segment(f"mga{layer}", [4] * 4, sigmoid_g(0))

                def square_out(j, base):
                    half = T.i if T.i is not None else 1
                    for c in range(4):
                        act.wait_ge(gemm_step, base + 4 * (SLOTS - 1) + c + 1)
                        nc.scalar.activation(SQX[:, bass.ds(half * 4 * TOK + c * TOK, tq)], bank[c][:, 0:tq], ACT.Square).then_inc(out_sq, 1)

                segment(f"out{layer}", [4], square_out)

        @block.vector
        def _(dve):
            T = Tally()
            V = nc.vector
            drain = dve.drain

            def rsqrt(y, v, t):
                V.tensor_scalar(y.bitcast(I32), v.bitcast(I32), -0.5, RSQRT_SEED, ALU.mult, ALU.add)
                for _ in range(3):
                    drain()
                    V.tensor_tensor(t, y, y, ALU.mult)
                    drain()
                    V.scalar_tensor_tensor(t, t, -0.5, v, ALU.mult, ALU.mult)
                    drain()
                    V.scalar_tensor_tensor(y, t, 1.5, y, ALU.add, ALU.mult)
                drain()

            def norm_rows():
                for t in range(NT):
                    V.tensor_tensor_reduce(scaled[:, t, :], h[:, t, :], h[:, t, :], 1.0 / D, 0.0, ALU.mult, ALU.add,
                                           ss[:, t:t + 1])
                drain()
                V.tensor_scalar(ss[:, 0:NT], ss[:, 0:NT], EPS, None, ALU.add)
                drain()
                rsqrt(rs[:, 0:NT], ss[:, 0:NT], nt1[:, 0:NT])
                for t in range(NT):
                    V.tensor_scalar(scaled[:, t, :], h[:, t, :], rs[:, t:t + 1], None, ALU.mult).then_inc(rows_ready, 1)

            def chunks_split(count, tok=0, val=VAL):
                for g in range((count + 1) // 2):
                    c, e = 2 * g, min(2 * g + 2, count)
                    dve.wait_ge(chunk_val, T.next(chunk_val))
                    V.tensor_copy(ATH[:, c:e, tok:tok + S], val[:, c:e, :])
                    drain()
                    V.tensor_tensor(ATL[:, c:e, tok:tok + S], val[:, c:e, :], ATH[:, c:e, tok:tok + S], ALU.subtract) \
                        .then_inc(at_ready, 1)

            def block_done(base, before, units, t):
                dve.wait_ge(gemm_step, base + NT * (before + units - 1) + t + 1)

            def rows_out(dst, base, before, units, b, width=BLK, banks=0):
                for t in range(NT):
                    block_done(base, before, units, t)
                    V.tensor_copy(dst(t), bank[banks + t][:, 0:width]).then_inc(bank_free[banks + t], 1)
                    T.next(bank_free[banks + t])

            def add_rows(base, before, units, cols, banks):
                for t in range(NT):
                    block_done(base, before, units, t)
                    V.tensor_tensor(h[:, t, cols], h[:, t, cols], bank[banks + t][:, :], ALU.add) \
                        .then_inc(bank_free[banks + t], 1)
                    T.next(bank_free[banks + t])

            def blocks(n, out_block):
                with T.loop(dve, n // 2, {gemm_step: 2 * NT * SLOTS} | {b: 1 for b in bank_free}) as i:
                    for j in range(2):
                        base = T.now(gemm_step)
                        out_block(i * 2 * BLK + j * BLK, base, 2 * j)
                        T.next(gemm_step, NT * SLOTS)

            def bc(ap, n):
                return ap.to_broadcast([P, ap.shape[1], n])

            def rope(dst, t, heads):
                half = ROPE // 2
                x1, x2 = dst[:, :, 0:half], dst[:, :, half:ROPE]
                c, s = (TRIG[:, i, t:t + 1, :].to_broadcast([P, heads, half]) for i in (3, 4))
                r = [ROT[:, i, 0:heads, :] for i in range(4)]
                for o, a, b in zip(r, (x1, x2, x1, x2), (c, s, s, c)):
                    V.tensor_tensor(o, a, b, ALU.mult)
                drain()
                V.tensor_tensor(x1, r[0], r[1], ALU.subtract)
                V.tensor_tensor(x2, r[2], r[3], ALU.add)
                drain()

            def squares(src, n):
                o = scaled.rearrange("p t n -> p (t n)")[:, 0:n]
                V.tensor_tensor(o, src, src, ALU.mult)
                drain()
                return o

            def head_sums(dst, sq, d):
                V.tensor_reduce(dst, sq.rearrange("p (g d) -> p g d", d=d), AX, ALU.add)

            def even_norms_z():
                sums = ss[:, 0:2 * NSTAT_Z].rearrange("p (t n) -> p t n", t=NT)
                for t in range(NT):
                    sq = squares(ze[:, t, 0:O_DIL + 2 * DIL_W], O_DIL + 2 * DIL_W)
                    head_sums(sums[:, t, 0:1], sq[:, 0:O_KV], Q_LORA)
                    head_sums(sums[:, t, 1:2], sq[:, O_KV:O_ROPE], KV_LORA)
                    head_sums(sums[:, t, 2:3], sq[:, O_ROPE:O_DIL], ROPE)
                    head_sums(sums[:, t, 3:NSTAT_Z], sq[:, O_DIL:O_DIL + 2 * DIL_W], HD)
                    drain()
                    V.tensor_tensor(sums[:, t, :], sums[:, t, :], fst("inv_n_z"), ALU.mult)
                drain()
                flat = ss[:, 0:2 * NSTAT_Z]
                V.tensor_scalar(flat, flat, EPS, None, ALU.add)
                drain()
                rsqrt(STAT[:, 144:144 + 2 * NSTAT_Z], flat, nt1[:, 0:2 * NSTAT_Z])
                for t in range(NT):
                    V.tensor_scalar(ze[:, t, 0:O_KV], ze[:, t, 0:O_KV], rs_z[:, t, 0:1], None, ALU.mult)
                    V.tensor_scalar(ze[:, t, O_KV:O_ROPE], ze[:, t, O_KV:O_ROPE], rs_z[:, t, 1:2], None, ALU.mult) \
                        .then_inc(rows_ready, 1)
                for t in range(NT):
                    V.scalar_tensor_tensor(KROPE[:, t, :], ze[:, t, O_ROPE:O_DIL], rs_z[:, t, 2:3],
                                           fst("rope_gains")[:, ROPE:2 * ROPE], ALU.mult, ALU.mult)
                drain()
                for t in range(NT):
                    rope(KROPE[:, t:t + 1, :], t, 1)

            def mla_norms():
                flat = RSZO[:, 0, :, 0:NSTAT_Q]
                for t in range(NT):
                    sq = squares(Q[:, t, :], HEADS_E * MLA_D).rearrange("p (g d) -> p g d", d=MLA_D)
                    V.tensor_reduce(flat[:, t, 0:HEADS_E], sq[:, :, 0:NOPE], AX, ALU.add)
                    V.tensor_reduce(flat[:, t, HEADS_E:2 * HEADS_E], sq[:, :, NOPE:MLA_D], AX, ALU.add)
                    drain()
                    sq = squares(KV[:, t, :], HEADS_E * (NOPE + HD)).rearrange("p (g d) -> p g d", d=NOPE + HD)
                    V.tensor_reduce(flat[:, t, 2 * HEADS_E:NSTAT_Q], sq[:, :, 0:NOPE], AX, ALU.add)
                    drain()
                    V.tensor_tensor(flat[:, t, :], flat[:, t, :], fst("inv_n_q"), ALU.mult)
                drain()
                V.tensor_scalar(flat, flat, EPS, None, ALU.add)
                drain()
                y = RSZO[:, 1, :, 0:NSTAT_Q]
                rsqrt(y, flat, nt1[:, 0:2 * NSTAT_Q].rearrange("p (t n) -> p t n", t=NT))
                for t in range(NT):
                    qr = Q[:, t, :].rearrange("p (g d) -> p g d", d=MLA_D)[:, :, NOPE:MLA_D]
                    r = y[:, t, HEADS_E:2 * HEADS_E].rearrange("p (g o) -> p g o", o=1)
                    V.tensor_tensor(QROPE[:, t, :, :], qr, bc(r, ROPE), ALU.mult)
                    drain()
                    gain = fst("rope_gains")[:, 0:ROPE].rearrange("p (o n) -> p o n", o=1)
                    V.tensor_tensor(QROPE[:, t, :, :], QROPE[:, t, :, :], gain.to_broadcast([P, HEADS_E, ROPE]), ALU.mult)
                    drain()
                    rope(QROPE[:, t, :, :], t, HEADS_E)

            def moba_norms():
                flat = RSZO[:, 0, :, :]
                for t in range(NT):
                    head_sums(flat[:, t, :], squares(zo[:, t, 0:2 * ODD_W], 2 * ODD_W), HD)
                    drain()
                V.tensor_scalar(flat, flat, 1.0 / HD, EPS, ALU.mult, ALU.add)
                drain()
                rsqrt(RSZO[:, 1, :, :], flat, scaled[:, :, 0:2 * HEADS_O])

            def stage_mla(par, e):
                r = RSZO[:, 1, :, :]
                V.tensor_tensor(STAGE[:, par, 0:NT, 0:NOPE], Q[:, :, bass.ds(e * MLA_D, NOPE)], bc(r[:, :, bass.ds(e, 1)], NOPE), ALU.mult)
                V.tensor_copy(STAGE[:, par, 0:NT, NOPE:MLA_D],
                              QROPE.rearrange("p t h n -> p t (h n)")[:, :, bass.ds(e * ROPE, ROPE)])
                V.tensor_copy(STAGE[:, par, NT:2 * NT, NOPE:MLA_D], KROPE[:, :, :])
                V.tensor_tensor(STAGE[:, par, NT:2 * NT, 0:NOPE], KV[:, :, bass.ds(e * (NOPE + HD), NOPE)],
                                bc(r[:, :, bass.ds(e + 2 * HEADS_E, 1)], NOPE), ALU.mult).then_inc(staged, 1)

            def stage_dil(par, e):
                for g in range(2):
                    last = V.tensor_tensor(STAGE[:, par, g * NT:(g + 1) * NT, 0:HD], ze[:, :, bass.ds(e * HD + O_DIL + g * DIL_W, HD)],
                                           bc(rs_z[:, :, bass.ds(e + 3 + g * HEADS_E, 1)], HD), ALU.mult)
                last.then_inc(staged, 1)

            def stage_moba(par, e):
                for g in range(2):
                    last = V.tensor_tensor(STAGE[:, par, g * NT:(g + 1) * NT, 0:HD], zo[:, :, bass.ds(e * HD + g * ODD_W, HD)],
                                           bc(RSZO[:, 1, :, bass.ds(e + g * HEADS_O, 1)], HD), ALU.mult)
                last.then_inc(staged, 1)

            def bias_mla(par, e):
                V.tensor_tensor(PROB[:, par, :], fst("causal"), bank[2 + par][:, 0:KEYS], ALU.add)

            def bias_dil(par, e):
                V.scalar_tensor_tensor(PROB[:, par, :], fst("dist"), fst("dil_slope")[:, bass.ds(e, 1)],
                                       bank[2 + par][:, 0:KEYS], ALU.mult, ALU.add)
                drain()
                V.tensor_tensor(PROB[:, par, :], PROB[:, par, :], fst("lncount"), ALU.add)

            def bias_moba(par, e):
                V.scalar_tensor_tensor(PROB[:, par, :], fst("dist"), fst("moba_slope")[:, bass.ds(e, 1)],
                                       bank[2 + par][:, 0:KEYS], ALU.mult, ALU.add)

            def heads(n, stage, bias, col0):
                def pair(e, ahead):
                    for par in range(2):
                        dve.wait_ge(scored, T.next(scored))
                        bias(par, e + par)
                        drain()
                        V.tensor_reduce(NMAX[:, par, 0:1], PROB[:, par, 0:P], AX, ALU.max, negate=True)
                        V.tensor_reduce(NMAX[:, par, 1:2], PROB[:, par, P:KEYS], AX, ALU.max, negate=True) \
                            .then_inc(max_ready, 1)
                    if ahead:
                        for par in range(2):
                            stage(par, e + 2 + par)
                    for par in range(2):
                        dve.wait_ge(probs_ready, T.next(probs_ready))
                        V.reciprocal(RDEN[:, par, :], DEN[:, par, :])
                    drain()
                    for par in range(2):
                        dve.wait_ge(head_out, T.next(head_out))
                        for t in range(NT):
                            last = V.tensor_scalar(mixed[:, t, bass.ds((e + par) * HD + col0, HD)],
                                                   bank[6 + par][:, t * HD:(t + 1) * HD], RDEN[:, par, t:t + 1], None, ALU.mult)
                    return last

                for par in range(2):
                    stage(par, par)
                with T.loop(dve, n // 2 - 1, {scored: 2, probs_ready: 2, head_out: 2}) as i:
                    pair(i * 2, True)
                return pair(n - 2, False)

            dve.sem_inc(u_ready, 4)
            dve.wait_ge(x_in, 16 * NT)
            for layer in range(2):
                norm_rows()
                chunks_split(KC)
                if layer == 0:
                    dve.wait_ge(inputs_in, 16 * 4)
                    V.memset(GQK, MLA_SCALE)
                    drain()
                    V.scalar_tensor_tensor(GQK[0:NOPE, 0:1], col("e_qn_nope", 0, NOPE), MLA_SCALE, col("e_kn_nope", 0, NOPE), ALU.mult, ALU.mult)
                    V.scalar_tensor_tensor(GQK[0:HD, 1:2], col("e_dil_qn", 0, HD), HD_SCALE, col("e_dil_kn", 0, HD), ALU.mult, ALU.mult)
                    V.scalar_tensor_tensor(GQK[0:HD, 2:3], col("o_qn", 0, HD), HD_SCALE, col("o_kn", 0, HD), ALU.mult, ALU.mult)
                    V.tensor_copy(POSF, POS[:, :])
                    drain()
                    angle, turns, rest = TRIG[:, 0, :, :], TRIG[:, 1, :, :], TRIG[:, 2, :, :]
                    for t in range(NT):
                        V.tensor_scalar(angle[:, t, :], fst("inv_freq"), POSF[:, t:t + 1], None, ALU.mult)
                    drain()
                    V.tensor_scalar(turns, angle, INV_TURN, ROUND, ALU.mult, ALU.add)
                    drain()
                    V.tensor_scalar(turns, turns, ROUND, None, ALU.subtract)
                    drain()
                    src = angle
                    for part in TURN_PARTS:
                        V.scalar_tensor_tensor(rest, turns, -part, src, ALU.mult, ALU.add)
                        drain()
                        src = rest
                    V.tensor_scalar(rest, rest, PI_IN, -PI_IN, ALU.min, ALU.max).then_inc(trig_ready, 1)

                    dve.wait_ge(cond_sig, 1)
                    V.tensor_tensor(CTMP, CTMP, COL[:, COLS["cond"][0]:COLS["cond"][0] + 2 * KC], ALU.mult)
                    blocks(4, lambda c, base, b: rows_out(lambda t: ze[:, t, bass.ds(c, BLK)], base, 0, SLOTS, 0, BLK, b))
                    base = T.now(gemm_step)
                    rows_out(lambda t: ze[:, t, 4 * BLK:EVEN_IN], base, 0, SLOTS, 0, EVEN_IN - 4 * BLK, 0)
                    T.next(gemm_step, NT * SLOTS)
                    dve.wait_ge(trig_done, 1)
                    cos = TRIG[:, 3, :, :]
                    V.scalar_tensor_tensor(cos, cos, -2.0, cos, ALU.mult, ALU.mult)
                    drain()
                    V.tensor_scalar(cos, cos, 1.0, None, ALU.add)
                    drain()
                    even_norms_z()
                    chunks_split(5)
                    base = T.now(gemm_step)
                    rows_out(lambda t: Q[:, t, 0:BLK], base, 0, 2, 0, BLK, 0)
                    rows_out(lambda t: Q[:, t, BLK:BLK + BLK // 2], base, 2, 2, 0, BLK // 2, 2)
                    T.next(gemm_step, NT * SLOTS)
                    base = T.now(gemm_step)
                    for b in range(2):
                        rows_out(lambda t: KV[:, t, b * BLK:(b + 1) * BLK], base, 2 * b, 2, 0, BLK, 2 * b)
                    T.next(gemm_step, NT * SLOTS)
                    drain()
                    mla_norms()
                    heads(HEADS_E, stage_mla, bias_mla, 0)
                    last = heads(HEADS_E, stage_dil, bias_dil, HEADS_E * HD)
                else:
                    blocks(6, lambda c, base, b: rows_out(lambda t: zo[:, t, bass.ds(c, BLK)], base, 0, SLOTS, 0, BLK, b))
                    drain()
                    moba_norms()
                    last = heads(HEADS_O, stage_moba, bias_moba, 0)
                last.then_inc(rows_ready, NT)
                chunks_split(KC)
                blocks(2, lambda c, base, b: add_rows(base, 0, SLOTS, bass.ds(c, BLK), b))
                drain()
                norm_rows()
                chunks_split(KC)
                dve.sem_inc(ada_used, 2)

                def modulation(i, k):
                    dve.wait_ge(ada_landed[k % 2], T.next(ada_landed[k % 2], 16))
                    for c in range(2):
                        n = 2 * (k % SLOTS) + c
                        w = ADA[:, k % 2, c * ADA_W:(c + 1) * ADA_W]
                        for v in range(2):
                            a, s = ACC[v][:, bass.ds(i * 2 * ADA_W + k // SLOTS * ADA_W, ADA_W)], CTMP[:, 2 * n + v:2 * n + v + 1]
                            last = V.tensor_scalar(a, w, s, None, ALU.mult) if n == 0 else \
                                V.scalar_tensor_tensor(a, w, s, a, ALU.mult, ALU.add)
                        if c:
                            last.then_inc(ada_used, 1)
                        drain()

                def relu_squares(j):
                    for c in range(4):
                        dve.wait_ge(bank_free[c], T.next(bank_free[c]) + 1)
                        V.tensor_tensor(SQU[:, c % 2, :], RELU[:, c, :], RELU[:, c, :], ALU.mult)
                        drain()
                        V.tensor_copy(ATH[:, 4 * j + c, S:2 * S], SQU[:, c % 2, :])
                        drain()
                        V.tensor_tensor(ATL[:, 4 * j + c, S:2 * S], SQU[:, c % 2, :], ATH[:, 4 * j + c, S:2 * S], ALU.subtract) \
                            .then_inc(u_ready, 1)

                with T.loop(dve, FF_STEPS, {gemm_step: SLOTS * 12} | {b: 2 for b in bank_free} | {r: 16 * SLOTS for r in ada_landed}) as i:
                    for k in range(4):
                        modulation(i, k)
                    relu_squares(0)
                    for k in range(4, 6):
                        modulation(i, k)
                    relu_squares(1)
                    for k in range(6, 8):
                        modulation(i, k)
                    T.next(gemm_step, SLOTS * 12)
                dve.drain().then_inc(ada_acc, 1)
                for b in range(2):
                    for t in range(NT):
                        dve.wait_ge(acc_open, T.next(acc_open))
                        V.tensor_tensor(h[:, t, b * BLK:(b + 1) * BLK], h[:, t, b * BLK:(b + 1) * BLK], bank[4 + 2 * b + t][:, :], ALU.add)
                drain()
                norm_rows()
                chunks_split(2, S, RELU[:, 0:2, :])
                chunks_split(KC)
                dve.wait_ge(ada_sums, T.next(ada_sums))
                b_ada = COL[:, COLS["b_ada_2"][0] + layer * 3 * KC:COLS["b_ada_2"][0] + (layer + 1) * 3 * KC].rearrange("p (c o) -> p c o", o=1)
                V.tensor_tensor(MOD[:, layer, :, :], bank[1][:, 0:6 * KC].rearrange("p (c v) -> p c v", v=2),
                                b_ada.to_broadcast([P, 3 * KC, 2]), ALU.add).then_inc(bank_free[1], 1)
                T.next(bank_free[1])
                T.next(gemm_step, 2 * NT * SLOTS)
                for b in bank_free:
                    T.next(b)
                base = T.now(gemm_step)
                for b in range(2):
                    for t in range(NT):
                        n = 2 * b + t
                        dve.wait_ge(bank_free[n], T.now(bank_free[n]) + 1)
                        block_done(base, 2 * b, 2, t)
                        V.tensor_tensor(TMP, GATE[:, t, b * BLK:(b + 1) * BLK], bank[n][:, :], ALU.mult).then_inc(bank_free[n], 1)
                        T.next(bank_free[n])
                        drain()
                        last = V.tensor_tensor(h[:, t, b * BLK:(b + 1) * BLK], h[:, t, b * BLK:(b + 1) * BLK], TMP, ALU.add)
                        drain()
                T.next(gemm_step, NT * SLOTS)
            V.tensor_copy(TMP[:, 0:1], h[:, 0, 0:1]).then_inc(rows_ready, 1)
            for src in range(2):
                for g in range(KC // 2):
                    dve.wait_ge(x_turned, T.next(x_turned))
                    V.tensor_copy(xT[:, 2 * g:2 * g + 2, src * S:(src + 1) * S],
                                  bank[4 + g][:, :].rearrange("p (c n) -> p c n", c=2)).then_inc(at_ready, 1)
            drain()
            V.memset(WD, 0.0).then_inc(inputs_ready, 1)
            V.tensor_copy(TB[:, 0:1], xT[:, 0, 0:1]).then_inc(x_ready, KC)

            def split(dst, val, done):
                hi, lo = dst
                drain()
                V.tensor_copy(hi, val)
                drain()
                return V.tensor_tensor(lo, val, hi, ALU.subtract).then_inc(done, 1)

            def wide_rms(w):
                dve.wait_ge(sq_sums, T.next(sq_sums))
                V.tensor_scalar(VB[:, 0:w], bank[4][:, 0:w], 1.0 / D, EPS, ALU.mult, ALU.add)
                drain()
                rsqrt(RB[:, 0:w], VB[:, 0:w], TB[:, 0:w])

            def groups(n, body, count=4, per=None):
                base = T.now(gemm_step)
                for c in range(count):
                    dve.wait_ge(gemm_step, base + count * (SLOTS - 1) + c + 1)
                    body(n, c)
                T.next(gemm_step, SLOTS * count)

            def group_blocks(n, body):
                with T.loop(dve, n, {gemm_step: 4 * SLOTS} | {b: 1 for b in bank_free}) as i:
                    groups(i, body)

            def freed(ins, c):
                ins.then_inc(bank_free[c], 1)
                T.next(bank_free[c])

            for layer in range(2):
                tq = TOK if layer == 0 else S
                nq = tq // P
                sides = ((0, slice(0, S)), (1, slice(S, TOK)))

                mod = MOD[:, layer, :, :]
                for v in range(2):
                    g0, g1 = (COL[:, COLS[n][0] + layer * KC:COLS[n][0] + (layer + 1) * KC] for n in ("g_pre_2", "g_post_2"))
                    V.scalar_tensor_tensor(mod[:, KC:2 * KC, v], mod[:, KC:2 * KC, v], 1.0, g0, ALU.add, ALU.mult)
                    V.tensor_tensor(mod[:, 2 * KC:3 * KC, v], mod[:, 2 * KC:3 * KC, v], g1, ALU.mult)
                wide_rms(TOK)
                for g in range(KC // 2):
                    V.tensor_tensor(W0, xT[:, 2 * g:2 * g + 2, :],
                                    RB.rearrange("p (o n) -> p o n", o=1).to_broadcast([P, 2, TOK]), ALU.mult)
                    drain()
                    for c in range(2):
                        for v, side in sides:
                            V.tensor_scalar(W1[:, c, side], W0[:, c, side], mod[:, KC + 2 * g + c, v:v + 1],
                                            mod[:, 2 * g + c, v:v + 1], ALU.mult, ALU.add)
                    split((ATH[:, 2 * g:2 * g + 2, :], ATL[:, 2 * g:2 * g + 2, :]), W1, at_ready)

                V.memset(RA[2 * RANK:2 * RANK + 1, :], 1.0)
                groups(0, lambda n, c: freed(V.tensor_scalar(GQ[:, c * TOK:c * TOK + tq], bank[c][:, 0:tq], GDK ** -0.5, None, ALU.mult), c))
                groups(0, lambda n, c: freed(V.tensor_copy(GK[:, c * TOK:(c + 1) * TOK], bank[c][:, :]), c))
                groups(0, lambda n, c: freed(V.tensor_copy(RA[0:2 * RANK, :], bank[c][0:2 * RANK, :]), c), 1)
                group_blocks(2, lambda i, c: freed(V.tensor_copy(VG[:, c, bass.ds(i * BLK, BLK)], bank[c][:, :]), c))

                def gate_block(i, room, times):
                    def silu(n, c):
                        dve.wait_ge(sig_done, T.next(sig_done))
                        z = room[:, bass.ds(n * 4 * TOK + c * TOK, tq)] if n is not None else room[:, c * TOK:c * TOK + tq]
                        freed(V.tensor_tensor(z, z, bank[c][:, 0:tq], ALU.mult), c)

                    whole = room[:, 0:4 * TOK] if room is SIGC else room[:, bass.ds(i * 4 * TOK, 4 * TOK)]
                    groups(None if room is SIGC else i, silu)
                    drain()
                    w = whole.rearrange("p (c n) -> p c n", c=4)[:, :, 0:tq]
                    times(w)
                    split((BTH[:, bass.ds(i * 4, 4), 0:tq], BTL[:, bass.ds(i * 4, 4), 0:tq]), w, bt_ready)
                    drain()

                def gate_blocks(room, times):
                    with T.loop(dve, 2, {gemm_step: 4 * SLOTS, sig_done: 4} | {b: 1 for b in bank_free}) as i:
                        gate_block(i, room, lambda w: times(i, w))

                dve.wait_ge(mask_in, 16)
                drain()
                nb = tq // S
                orders = [TILES[d] for d in range(2)]

                def gla_decays():
                    dve.wait_ge(g_logs, T.next(g_logs))
                    for d in range(2):
                        V.scalar_tensor_tensor(LOGS[:, d, :], bank[2 + d][:, :], 0.0, LOGS[:, d, :], ALU.min, ALU.subtract)
                    drain()
                    la = LOGS.rearrange("p d (t n) -> p d t n", t=TT)
                    V.tensor_copy(LAS[:, 0, :, :, :], la)
                    drain()
                    V.tensor_tensor(LAS[:, 1, :, :, :], la, LAS[:, 0, :, :, :], ALU.subtract).then_inc(g_la, 1)

                def gla_keys(i):
                    dve.wait_ge(g_exp, T.next(g_exp, 4))
                    key = GK[:, bass.ds(i * TOK, TOK)].rearrange("p (o n) -> p o n", o=1).to_broadcast([P, 2, TOK])
                    return V.tensor_tensor(LOGS, LOGS, key, ALU.mult)

                def gla_level(n, i):
                    q, key = (a[:, bass.ds(i * TOK, tq)] for a in (GQ, GK))
                    if n == len(LEVELS) - 1:
                        dve.wait_ge(g_exp, T.next(g_exp))
                        for d in range(2):
                            o, x = (a.rearrange("p (t x two) -> p t x two", t=nq, two=2)[:, :, :, 1 - d] for a in (LAST[:, 0:tq], q))
                            e = LASTE[:, 0:tq].rearrange("p (t d x) -> p t d x", t=nq, d=2)[:, :, d, :]
                            last = V.scalar_tensor_tensor(o, e, 0.5, x, ALU.mult, ALU.mult)
                        last.then_inc(g_pair, 1)
                        return
                    dve.wait_ge(g_exp, T.next(g_exp, nb))
                    e = P2[:, n % 2, 0:nb, :, :]
                    V.tensor_tensor(e[:, :, 0, :], e[:, :, 0, :], q.rearrange("p (b n) -> p b n", b=nb), ALU.mult)
                    V.tensor_tensor(e[:, :, 1, :], e[:, :, 1, :], key.rearrange("p (b n) -> p b n", b=nb), ALU.mult).then_inc(g_pair, 1)

                def gla_place(m):
                    drain()
                    dve.wait_ge(g_level, T.next(g_level))
                    V.memset(TMPA, 0.0)
                    mask = MASK[:, m * P:(m + 1) * P].rearrange("p (o n) -> p o n", o=1).to_broadcast([P, nq, P])
                    return V.copy_predicated(ATT[:, 0:tq].rearrange("p (t n) -> p t n", t=nq), mask,
                                             bank[4 + m % 2][:, 0:tq].rearrange("p (t n) -> p t n", t=nq))

                def gla_states():
                    dve.wait_ge(g_qb, T.next(g_qb))
                    dve.wait_ge(g_outer, T.next(g_outer))
                    for d in range(2):
                        V.tensor_copy(STATE[:, d, 0, :], bank[4 + d][:, 0:GDV])
                    drain()
                    for d, o in enumerate(orders):
                        V.scalar_tensor_tensor(STATE[:, d, 1, :], STATE[:, d, 0, :], EBL[:, d, o[1]:o[1] + 1], bank[4 + d][:, GDV:2 * GDV], ALU.mult, ALU.add)
                    drain()
                    for d, o in enumerate(orders):
                        last = V.scalar_tensor_tensor(STATE[:, d, 2, :], STATE[:, d, 1, :], EBL[:, d, o[2]:o[2] + 1],
                                                      bank[6][:, d * GDV:(d + 1) * GDV], ALU.mult, ALU.add)
                    last.then_inc(g_state, 1)

                def gla_head(i, ahead):
                    gla_level(0, i)
                    gla_states()
                    gla_place(0)
                    for n in range(1, len(LEVELS)):
                        gla_level(n, i)
                        gla_place(n)
                    gla_place(len(LEVELS)).then_inc(g_att, 1)
                    if ahead:
                        gla_decays()
                    dve.wait_ge(g_out, T.next(g_out))
                    o = [bank[6 + t // 2][:, t % 2 * GDV:(t % 2 + 1) * GDV] for t in range(nq)]
                    for b in range(nb):
                        V.tensor_copy(ON[:, 2 * b:2 * b + 2, :], bank[6 + b][:, :].rearrange("p (t n) -> p t n", t=2))
                    drain()
                    for t in range(nq):
                        V.tensor_tensor_reduce(ON[:, t, :], ON[:, t, :], o[t], 1.0 / GDV, 0.0, ALU.mult, ALU.add, GS[:, t:t + 1])
                    drain()
                    V.tensor_scalar(GS[:, 0:nq], GS[:, 0:nq], EPS, None, ALU.add)
                    drain()
                    rsqrt(GR[:, 0:nq], GS[:, 0:nq], GT[:, 0:nq])
                    for t in range(nq):
                        last = V.tensor_scalar(ON[:, t, :], o[t], GR[:, t:t + 1], None, ALU.mult)
                    last.then_inc(g_rows, 1)
                    if ahead:
                        gla_keys(i + 1)
                    for c in range(2):
                        dve.wait_ge(g_turned, T.next(g_turned))
                        last = V.tensor_scalar(VG[:, 0:nq, bass.ds(i * GDV + c * P, P)], bank[4 + c][:, 0:tq].rearrange("p (t n) -> p t n", t=nq),
                                               col("gla_norm_g_2", layer * 2 + c), None, ALU.mult)
                    if ahead:
                        last.then_inc(g_keys, 1)
                    drain()

                gla_decays()
                gla_keys(0).then_inc(g_keys, 1)
                per = {g_logs: 1, g_exp: 4 + (len(LEVELS) - 1) * nb + 1, g_level: 1 + len(LEVELS), g_qb: 1, g_outer: 1, g_out: 1, g_turned: 2}
                with T.loop(dve, GH - 1, per) as i:
                    gla_head(i, True)
                gla_head(GH - 1, False)
                def gla_times(i, w):
                    o = VG[:, 0:nq, bass.ds(i * 4 * P, 4 * P)]
                    for c in range(4):
                        V.tensor_tensor(w[:, c, :].rearrange("p (t n) -> p t n", n=P), w[:, c, :].rearrange("p (t n) -> p t n", n=P),
                                        o[:, :, c * P:(c + 1) * P], ALU.mult)

                gate_blocks(SIGZ, gla_times)

                def gated(first):
                    def branch(n, c):
                        dve.wait_ge(bank_free[c], T.now(bank_free[c]) + 1)
                        y, o, g = Y[:, n * 4 + c, 0:tq], bank[c][:, 0:tq], G[n][:, c, 0:tq]
                        if first:
                            freed(V.tensor_tensor(y, g, o, ALU.mult), c)
                        else:
                            freed(V.tensor_tensor(WG[:, 0:tq], g, o, ALU.mult), c)
                            drain()
                            V.tensor_tensor(y, y, WG[:, 0:tq], ALU.add)
                            drain()
                    for n in range(2):
                        for c in range(4):
                            T.next(bank_free[c])
                        T.next(gemm_step, 4 * SLOTS)
                    for n in range(2):
                        groups(n, branch)
                    drain()

                gated(True)

                def head_in(dst, c, w):
                    dve.wait_ge(a_sq, T.next(a_sq))
                    freed(V.tensor_copy(dst, bank[c][:, 0:w]), c)

                with T.loop(dve, 2, {gemm_step: 4 * SLOTS, a_sq: 4} | {b: 1 for b in bank_free}) as i:
                    groups(i, lambda n, c: head_in(QG[:, bass.ds(n * 4 * TOK + c * TOK, tq)], c, tq))
                groups(0, lambda n, c: head_in(KG[:, c, :], c, TOK), AKV)
                groups(0, lambda n, c: freed(V.tensor_copy(VA[:, c, :], bank[c][:, 0:AKV * AD]), c), TT)
                drain()

                def gain(r, hd):
                    V.tensor_scalar(QS[:, r, 0:tq], QG[:, bass.ds(hd * TOK, tq)], col("q_norm_g_2", layer), None, ALU.mult).then_inc(a_gain, 1)

                def rotate(r):
                    dve.wait_ge(a_rot, T.next(a_rot))
                    V.tensor_tensor(ROTW[:, r, :], cst("sin"), bank[6 + r][:, 0:S], ALU.mult)
                    V.tensor_tensor(QS[:, r, 0:S], QS[:, r, 0:S], cst("cos"), ALU.mult)
                    drain()
                    V.tensor_tensor(QS[:, r, 0:S], QS[:, r, 0:S], ROTW[:, r, :], ALU.add).then_inc(a_q, 1)

                V.tensor_scalar(KG, KG, col("k_norm_g_2", layer), None, ALU.mult).then_inc(a_gain, 1)
                nstat = AH * nq + AKV * TT
                dve.wait_ge(a_sums, T.next(a_sums))
                V.tensor_scalar(RSV[:, 0:nstat], bank[4][:, 0:nstat], 1.0 / AD, EPS, ALU.mult, ALU.add)
                for r in range(2):
                    gain(r, r)
                drain()
                rsqrt(RSQ[:, 0:nstat], RSV[:, 0:nstat], RSW[:, 0:nstat])
                V.tensor_scalar(RSQ[:, 0:AH * nq], RSQ[:, 0:AH * nq], ATTN_SCALE, None, ALU.mult)
                dve.wait_ge(a_rot, T.next(a_rot))
                both = lambda name: cst(name).rearrange("p (o n) -> p o n", o=1).to_broadcast([P, AKV, S])
                V.tensor_tensor(ROTW, both("sin"), bank[5][:, :].rearrange("p (k n) -> p k n", k=AKV), ALU.mult)
                V.tensor_tensor(KG[:, :, 0:S], KG[:, :, 0:S], both("cos"), ALU.mult)
                for kv in range(AKV):
                    for t in range(TT):
                        n = AH * nq + kv * TT + t
                        last = V.tensor_scalar(DIAG[:, kv, t, :], ident, RSQ[:, n:n + 1], None, ALU.mult)
                last.then_inc(a_diag, 1)
                drain()
                V.tensor_tensor(KG[:, :, 0:S], KG[:, :, 0:S], ROTW, ALU.add)
                drain()
                dve.wait_ge(a_bc, T.next(a_bc))
                for kv in range(AKV):
                    V.tensor_tensor(K2[:, kv, :], KG[:, kv, :], bank[5 - kv][:, :], ALU.mult)
                drain()
                for r in range(2):
                    rotate(r)

                def attend(hd, ahead):
                    for r in range(2):
                        dve.wait_ge(a_score, T.next(a_score))
                        for t in range(nq):
                            sc = bank[3 * r + t][:, :] if t < NT else bank[3 * r + 2][:, (t - NT) * S:(t - NT + 1) * S]
                            V.tensor_reduce(NM[:, r, t:t + 1], sc, AX, ALU.max, negate=True)
                        V.tensor_copy(SCL[:, r, 0:nq], RSQ[:, bass.ds((hd + r) * nq, nq)])
                        drain()
                        V.tensor_tensor(NM[:, r, 0:nq], NM[:, r, 0:nq], SCL[:, r, 0:nq], ALU.mult).then_inc(a_max, 1)
                    if ahead:
                        for r in range(2):
                            gain(r, hd + 2 + r)
                    for r in range(2):
                        dve.wait_ge(a_exp, T.next(a_exp))
                        V.reciprocal(RD[:, r, 0:nq], DN[:, r, 0:nq])
                        drain()
                        for t in range(nq):
                            pr = PL[:, r, t, :] if t < NT else PC[:, r, t - NT, :]
                            last = V.tensor_scalar(pr, pr, RD[:, r, t:t + 1], None, ALU.mult)
                        last.then_inc(a_norm, 1)
                    if ahead:
                        for r in range(2):
                            rotate(r)
                    for r in range(2):
                        dve.wait_ge(a_out, T.next(a_out))
                        V.tensor_copy(QG[:, bass.ds((hd + r) * TOK, tq)], bank[3 * r][:, 0:tq]).then_inc(a_stored, 1)

                with T.loop(dve, AH // 2 - 1, {a_score: 2, a_exp: 2, a_rot: 2, a_out: 2}) as i:
                    attend(i * 2, True)
                attend(AH - 2, False)
                drain()
                gate_blocks(SIGA, lambda i, w: V.tensor_tensor(
                    w, w, QG[:, bass.ds(i * 4 * TOK, 4 * TOK)].rearrange("p (c n) -> p c n", c=4)[:, :, 0:tq], ALU.mult))
                gated(False)

                def tokens(a):
                    return a.rearrange("p (s n) -> p s n", n=S)

                with T.loop(dve, 2, {gemm_step: 16 * SLOTS, sig_done: 4} | {b: 4 for b in bank_free}) as i:
                    groups(i, lambda n, c: freed(V.tensor_copy(AB[:, c, 0:tq], bank[c][:, 0:tq]), c))
                    groups(i, lambda n, c: freed(V.tensor_copy(AC[:, c, 0:tq], bank[c][:, 0:tq]), c))
                    drain()
                    groups(i, lambda n, c: freed(V.tensor_tensor(PX[:, c, 0:tq], AC[:, c, 0:tq], bank[c][:, 0:tq], ALU.mult), c))
                    drain()

                    def tap(k, c):
                        return COL[:, bass.ds(i * 4 + (COLS["conv_w_2"][0] + (layer * 3 + k) * KC + c), 1)]

                    for c in range(4):
                        V.tensor_scalar(CV[:, c, 0:tq], PX[:, c, 0:tq], tap(1, c), None, ALU.mult)
                    drain()
                    for c in range(4):
                        p, o = tokens(PX[:, c, 0:tq]), tokens(CV[:, c, 0:tq])
                        V.scalar_tensor_tensor(o[:, :, 1:S], p[:, :, 0:S - 1], tap(0, c), o[:, :, 1:S], ALU.mult, ALU.add)
                    drain()
                    for c in range(4):
                        p, o = tokens(PX[:, c, 0:tq]), tokens(CV[:, c, 0:tq])
                        V.scalar_tensor_tensor(o[:, :, 0:S - 1], p[:, :, 1:S], tap(2, c), o[:, :, 0:S - 1], ALU.mult, ALU.add)
                    drain()
                    V.tensor_tensor(CV[:, :, 0:tq], CV[:, :, 0:tq], AB[:, :, 0:tq], ALU.mult)
                    drain()

                    gate_block(i, SIGC, lambda w: V.tensor_tensor(w, w, CV[:, :, 0:tq], ALU.mult))
                gated(False)

                for g in range(KC // 2):
                    split((BTH[:, 2 * g:2 * g + 2, 0:tq], BTL[:, 2 * g:2 * g + 2, 0:tq]), Y[:, 2 * g:2 * g + 2, 0:tq], bt_ready)
                def out_in(i, c):
                    dve.wait_ge(out_sq, T.next(out_sq))
                    freed(V.tensor_copy(OUT.rearrange("p c n -> p (c n)")[:, bass.ds(i * 4 * TOK + c * TOK, tq)], bank[c][:, 0:tq]), c)

                with T.loop(dve, 2, {gemm_step: 4 * SLOTS, out_sq: 4} | {b: 1 for b in bank_free}) as i:
                    groups(i, out_in)
                drain()
                wide_rms(tq)
                for c in range(KC):
                    V.tensor_tensor(OUT[:, c, 0:tq], OUT[:, c, 0:tq], RB[:, 0:tq], ALU.mult)
                drain()
                for c in range(KC):
                    for v, side in sides[0:nq // 2]:
                        last = V.scalar_tensor_tensor(xT[:, c, side], OUT[:, c, side], mod[:, 2 * KC + c, v:v + 1], xT[:, c, side], ALU.mult, ALU.add)
                    last.then_inc(x_ready, 1)
                drain()
            for t in range(NT):
                for g in range(2):
                    dve.wait_ge(x_turned, T.next(x_turned))
                    V.tensor_copy(h[:, t, g * BLK:(g + 1) * BLK], bank[4 + 2 * t + g][:, :]).then_inc(out_rows, 1)

        @block.tensor
        def _(pe):
            T = Tally()
            mm, turn = nc.tensor.matmul, nc.tensor.transpose
            for b in bank_free:
                pe.sem_inc(b, 1)

            def product(o, ah, al, bh, bl, start, stop, free=False):
                mm(o, ah, bh, start=start, stop=False, skip_group_check=free)
                mm(o, ah, bl, start=False, stop=False, skip_group_check=free)
                return mm(o, al, bh, start=False, stop=stop, skip_group_check=free)

            def unit(slot, ready=None):
                pe.wait_ge(lo_split, T.next(lo_split) + SLOTS)
                if ready is not None:
                    pe.wait_ge(*ready)

            def rows_block(units, width, b0, chunk0=0, tok=0, ready=None, acc=False):
                c0 = chunk0
                for u, (slot, k) in enumerate(units):
                    unit(slot, ready and ready[u])
                    for t in range(NT):
                        if u == 0 and not acc:
                            pe.wait_ge(bank_free[b0 + t], T.next(bank_free[b0 + t]))
                        for c in range(k):
                            tk = slice(tok + t * P, tok + (t + 1) * P)
                            w = slice(c * width, (c + 1) * width)
                            last = product(bank[b0 + t][:, 0:width], ATH[:, c0 + c, tk], ATL[:, c0 + c, tk],
                                           WHI[:, slot, w], WLO[:, slot, w], not acc and u == 0 and c == 0,
                                           not acc and u == len(units) - 1 and c == k - 1, acc)
                        last.then_inc(gemm_step, 1)
                    c0 += k

            def cols_block(ready=None, tok=0, width=S):
                for slot in range(SLOTS):
                    unit(slot, ready and ready[slot])
                    for j in range(BLK // P):
                        if slot == 0:
                            pe.wait_ge(bank_free[j], T.next(bank_free[j]))
                        for c in range(2):
                            w = slice(c * BLK + j * P, c * BLK + (j + 1) * P)
                            last = product(bank[j][:, 0:width], WHI[:, slot, w], WLO[:, slot, w],
                                           ATH[:, 2 * slot + c, tok:tok + width], ATL[:, 2 * slot + c, tok:tok + width],
                                           slot == 0 and c == 0, slot == SLOTS - 1 and c == 1)
                        last.then_inc(gemm_step, 1)

            std_units = [(s, 2) for s in range(SLOTS)]

            def rows_blocks(n, ready):
                with T.loop(pe, n // 2, {lo_split: 2 * SLOTS} | {b: 1 for b in bank_free}):
                    for j in range(2):
                        rows_block(std_units, BLK, 2 * j, ready=ready)

            def turn_rows(count, src):
                pe.wait_ge(rows_ready, T.next(rows_ready, NT))
                if T.now(turned):
                    pe.wait_ge(chunk_val, T.now(turned))
                base = T.now(turned)
                for g in range((count + 1) // 2):
                    for c in range(2 * g, min(2 * g + 2, count)):
                        for t in range(NT):
                            o = (c % 2) * S + t * P
                            last = turn(bank[4 + g % 4][:, o:o + P], src(t, c), ident)
                    last.then_inc(turned, 1)
                    T.next(turned)
                return [(at_ready, base + g + 1) for g in range((count + 1) // 2)]

            def heads(n, d, value):
                def operands(par):
                    pe.wait_ge(staged, T.next(staged))
                    for g in range(2 * NT):
                        last = turn(bank[par][0:MLA_D, g * P:(g + 1) * P], STAGE[:, par, g, :], ident)
                    last.then_inc(qk_turned, 1)

                def pair(e, ahead):
                    for par in range(2):
                        pe.wait_ge(qk_ready, T.next(qk_ready))
                        q, k = QKT[0:d, par, 0:S], QKT[0:d, par, S:2 * S]
                        mm(bank[2 + par][:, 0:P], q[:, 0:P], k[:, 0:P], start=True, stop=True)
                        mm(bank[2 + par][:, P:KEYS], q[:, P:S], k, start=True, stop=True).then_inc(scored, 1)
                    if ahead:
                        for par in range(2):
                            operands(par)
                    for par in range(2):
                        pe.wait_ge(probs_ready, T.next(probs_ready))
                        for g in range(KEYS // P):
                            last = turn(bank[4 + par][:, g * P:(g + 1) * P], PROB[:, par, g * P:(g + 1) * P], ident)
                        last.then_inc(probs_turned, 1)
                    for par in range(2):
                        pe.wait_ge(probs_t_ready, T.next(probs_t_ready))
                        o, p = bank[6 + par], PROBT[:, par, :]
                        mm(o[:, 0:HD], p[:, 0:P], value(0, e + par), start=True, stop=True)
                        mm(o[:, HD:2 * HD], p[:, P:2 * P], value(0, e + par), start=True, stop=False)
                        mm(o[:, HD:2 * HD], p[:, 2 * P:KEYS], value(1, e + par), start=False, stop=True).then_inc(head_out, 1)

                for par in range(2):
                    operands(par)
                with T.loop(pe, n // 2 - 1, {staged: 2, qk_ready: 2, probs_ready: 2, probs_t_ready: 2}) as i:
                    pair(i * 2, True)
                pair(n - 2, False)

            pe.wait_ge(inputs_in, 16 * 4)
            pe.wait_ge(zeroed, 1)
            for layer in range(2):
                ready = turn_rows(KC, lambda t, c: scaled[:, t, c * P:(c + 1) * P])
                if layer == 0:
                    rows_blocks(4, ready)
                    rows_block(std_units, EVEN_IN - 4 * BLK, 0)
                    ready = turn_rows(5, lambda t, c: ze[:, t, c * P:(c + 1) * P])
                    rows_block([(0, 2), (1, 1)], BLK, 0, ready=ready[0:2])
                    rows_block([(2, 2), (3, 1)], BLK // 2, 2)
                    rows_block([(0, 1), (1, 1)], BLK, 0, 3, ready=ready[1:3])
                    rows_block([(2, 1), (3, 1)], BLK, 2, 3)
                    heads(HEADS_E, MLA_D, lambda t, e: KV[:, t, bass.ds(e * (NOPE + HD) + NOPE, HD)])
                    heads(HEADS_E, HD, lambda t, e: ze[:, t, bass.ds(e * HD + O_DIL + 2 * DIL_W, HD)])
                else:
                    rows_blocks(6, ready)
                    heads(HEADS_O, HD, lambda t, e: zo[:, t, bass.ds(e * HD + 2 * ODD_W, HD)])
                ready = turn_rows(KC, lambda t, c: mixed[:, t, c * P:(c + 1) * P])
                rows_blocks(2, ready)
                ready = turn_rows(KC, lambda t, c: scaled[:, t, c * P:(c + 1) * P])
                pe.wait_ge(*ready[-1])
                for b in range(4, 8):
                    mm(bank[b][:, :], ZERO[0:1, 0:P], ZERO[0:1, :], start=True, stop=False, skip_group_check=True)
                with T.loop(pe, FF_STEPS, {lo_split: 4 * SLOTS, u_ready: 8} | {b: 2 for b in bank_free}):
                    for j in range(2):
                        cols_block(ready)
                    hidden = [(u_ready, T.next(u_ready, 2) + 4) for _ in range(SLOTS)]
                    for j in range(2):
                        rows_block(std_units, BLK, 4 + 2 * j, tok=S, ready=hidden, acc=True)
                for b in range(4, 8):
                    mm(bank[b][:, :], ZERO[0:1, 0:P], ZERO[0:1, :], start=False, stop=True, skip_group_check=True) \
                        .then_inc(acc_open, 1)
                pe.wait_ge(p_in, 16 * (layer + 1))
                for c in range(2):
                    for t in range(NT):
                        last = turn(bank[0][:, c * S + t * P:c * S + (t + 1) * P], PIN[:, t, c * P:(c + 1) * P], ident)
                last.then_inc(turned, 1)
                T.next(turned)
                p_ready = (at_ready, T.now(turned))

                def modulation(v):
                    for n in range(3 * KC):
                        last = mm(bank[1][:, 2 * n + v:2 * n + v + 1], ACC[v][:, n * P:(n + 1) * P], cst("ones")[:, 0:1], start=True, stop=True)
                    return last

                pe.wait_ge(ada_acc, T.next(ada_acc))
                pe.wait_ge(bank_free[1], T.next(bank_free[1]))
                modulation(0)
                ready = turn_rows(KC, lambda t, c: scaled[:, t, c * P:(c + 1) * P])
                modulation(1).then_inc(ada_sums, 1)
                rows_blocks(2, ready)
                for b in range(2):
                    rows_block([(2 * b, 1), (2 * b + 1, 1)], BLK, 2 * b, tok=S, ready=[p_ready, p_ready])
            def cols_product(groups, rhs, width, b0=0, ready=None, wcols=BLK):
                rh, rl = rhs
                for slot in range(SLOTS):
                    unit(slot, ready and ready[slot])
                    for j in range(groups):
                        if slot == 0:
                            pe.wait_ge(bank_free[j], T.next(bank_free[j]))
                        for c in range(2):
                            w = slice(c * wcols + j * P, c * wcols + (j + 1) * P)
                            last = product(bank[j][:, 0:width], WHI[:, slot, w], WLO[:, slot, w], rh[:, 2 * slot + c, 0:width],
                                           rl[:, 2 * slot + c, 0:width], slot == 0 and c == 0, slot == SLOTS - 1 and c == 1)
                        last.then_inc(gemm_step, 1)

            def rows_product(width, ready=None):
                for slot in range(SLOTS):
                    unit(slot, ready and ready[slot])
                    for t in range(TT):
                        if slot == 0:
                            pe.wait_ge(bank_free[t], T.next(bank_free[t]))
                        for c in range(2):
                            w, tk = slice(c * width, (c + 1) * width), slice(t * P, (t + 1) * P)
                            last = product(bank[t][:, 0:width], ATH[:, 2 * slot + c, tk], ATL[:, 2 * slot + c, tk],
                                           WHI[:, slot, w], WLO[:, slot, w], slot == 0 and c == 0, slot == SLOTS - 1 and c == 1)
                        last.then_inc(gemm_step, 1)

            def loop_blocks(n, body):
                with T.loop(pe, n, {lo_split: SLOTS} | {b: 1 for b in bank_free}):
                    body()

            def sum_squares(w, squared):
                for c in range(KC):
                    pe.wait_ge(squared, T.next(squared))
                    last = mm(bank[4][:, 0:w], cst("ones"), SQX[:, c * TOK:c * TOK + w], start=c == 0, stop=c == KC - 1)
                last.then_inc(sq_sums, 1)

            pe.wait_ge(rows_ready, T.next(rows_ready))
            pe.wait_ge(ctx_in, 16)
            base = T.now(at_ready) + T.now(turned)
            for s, src in enumerate((h, CTXIN)):
                for g in range(KC // 2):
                    if s:
                        pe.wait_ge(at_ready, base + g + 1)
                    for c in range(2 * g, 2 * g + 2):
                        for t in range(NT):
                            o = (c % 2) * S + t * P
                            last = turn(bank[4 + g][:, o:o + P], src[:, t, c * P:(c + 1) * P], ident)
                    last.then_inc(x_turned, 1)
            chunks = base + KC
            for layer in range(2):
                tq = TOK if layer == 0 else S
                nq = tq // P
                AT, BT = (ATH, ATL), (BTH, BTL)
                sum_squares(TOK, sq_ready)
                ready = [(at_ready, chunks + s + 1) for s in range(SLOTS)]
                chunks += SLOTS
                cols_product(4, AT, tq, ready=ready)
                cols_product(4, AT, TOK)
                cols_product(1, AT, TOK, wcols=P)
                loop_blocks(2, lambda: rows_product(BLK))

                nb = tq // S
                pe.wait_ge(wd_in, 64 * (layer + 1))
                pe.wait_ge(tri_ready, layer + 1)
                for b in bank_free:
                    pe.wait_ge(b, T.now(b) + 1)

                def gla_sums(o, d, t, columns):
                    mm(o, LAS[:, 0, d, t, :], columns, start=True, stop=False)
                    return mm(o, LAS[:, 1, d, t, :], columns, start=False, stop=True)

                def gla_pre(i):
                    for d in range(2):
                        for t in range(TT):
                            last = mm(bank[2 + d][:, t * P:(t + 1) * P], RA[:, t * P:(t + 1) * P], WD[:, d, bass.ds(i * GDK, GDK)], start=True, stop=True)
                    last.then_inc(g_pre, 1)

                def gla_tiles(first=False):
                    pe.wait_ge(g_la, T.next(g_la))
                    if not first:
                        pe.wait_ge(g_exp, T.next(g_exp))
                    for b in range(4):
                        d = b // 2
                        columns = TRI[:, TRI_TILE + d * 2 * P:TRI_TILE + (d + 1) * 2 * P].rearrange("p (k n) -> p k n", k=2)
                        for j in range(2):
                            o = bank[b][:, :].rearrange("p (k n) -> p k n", k=2)[:, :, j * P:(j + 1) * P]
                            last = gla_sums(o, d, b % 2 * 2 + j, columns)
                        last.then_inc(g_diff, 1)

                def gla_level(n):
                    half = LEVELS[n]
                    pe.wait_ge(g_exp, T.next(g_exp, 2 if n < 2 else nb))
                    if n == len(LEVELS) - 1:
                        for t in range(nq):
                            for d in range(2):
                                o = bank[0][:, t * P + d * P // 2:t * P + (d + 1) * P // 2]
                                last = gla_sums(o, d, t, TRI[:, TRI_LAST + d * P // 2:TRI_LAST + (d + 1) * P // 2])
                        last.then_inc(g_diff, 1)
                        return
                    for b in range(nb):
                        whole = bank[2 * n % 4 + b][:, :]
                        for j in range(2):
                            for d in range(2):
                                at0 = TRI_LEVEL + (2 * n + d) * P
                                columns = TRI[:, at0:at0 + P].rearrange("p (k b x) -> p k b x", k=2, x=half)
                                q0, k0 = j * P + (1 - d) * half, S + j * P + d * half
                                o = bass.AP(whole.tensor, whole.offset + q0, [list(whole.ap[0]), [k0 - q0, 2], [2 * half, P // (2 * half)], [1, half]])
                                last = gla_sums(o, d, 2 * b + j, columns)
                        last.then_inc(g_diff, 1)

                def gla_scores(m, i):
                    n = m - 1
                    for t in range(nq):
                        tk, side = slice(t * P, (t + 1) * P), slice(t % 2 * P, (t % 2 + 1) * P)
                        if m == 0:
                            key, q = K2X[:, tk], GQ[:, bass.ds(i * TOK + t * P, P)]
                        elif n == len(LEVELS) - 1:
                            key, q = K2X[:, tk], LAST[:, tk]
                        else:
                            key, q = P2[:, n % 2, t // 2, 1, side], P2[:, n % 2, t // 2, 0, side]
                        last = mm(bank[4 + m % 2][:, tk], key, q, start=True, stop=True)
                    last.then_inc(g_level, 1)

                def gla_head(i, ahead):
                    v = [VG[:, t, bass.ds(i * GDV, GDV)] for t in range(TT)]
                    o = [bank[6 + t // 2][:, t % 2 * GDV:(t % 2 + 1) * GDV] for t in range(nq)]
                    pe.wait_ge(g_keys, T.next(g_keys))
                    for d in range(2):
                        for t in range(TT):
                            last = turn(bank[4 + d][:, t * P:(t + 1) * P], P1[:, 0, d, t * P:(t + 1) * P], ident)
                    last.then_inc(g_kturned, 1)
                    gla_level(0)
                    gla_level(1)
                    pe.wait_ge(g_kready, T.next(g_kready))
                    for d in range(2):
                        for n, room in enumerate((bank[4 + d][:, 0:GDV], bank[4 + d][:, GDV:2 * GDV], bank[6][:, d * GDV:(d + 1) * GDV])):
                            t = TILES[d][n]
                            last = mm(room, P1[:, 0, d, t * P:(t + 1) * P], v[t], start=True, stop=True)
                    last.then_inc(g_outer, 1)
                    pe.wait_ge(g_state, T.next(g_state))
                    pe.wait_ge(g_qb, T.next(g_qb))
                    opened = set()
                    for d in range(2):
                        for n in range(1, TT):
                            t = TILES[d][n]
                            if t < nq:
                                mm(o[t], P1[:, 1, d, t * P:(t + 1) * P], STATE[:, d, n - 1, :], start=t // 2 not in opened, stop=False, skip_group_check=True)
                                opened.add(t // 2)
                    pe.wait_ge(g_kc, T.next(g_kc))
                    gla_scores(0, i)
                    for n in range(len(LEVELS)):
                        if 0 < n < len(LEVELS) - 1:
                            gla_level(n + 1)
                        if n == len(LEVELS) - 1:
                            T.next(g_exp, nb)
                            if ahead:
                                gla_pre(i + 1)
                        pe.wait_ge(g_pair, T.next(g_pair))
                        gla_scores(n + 1, i)
                    pe.wait_ge(g_att, T.next(g_att))
                    for t in range(nq):
                        last = mm(o[t], ATT[:, t * P:(t + 1) * P], v[t], start=False, stop=True, skip_group_check=True)
                    last.then_inc(g_out, 1)
                    if ahead:
                        gla_tiles()
                    else:
                        T.next(g_exp)
                    pe.wait_ge(g_rows, T.next(g_rows))
                    for c in range(2):
                        for t in range(nq):
                            last = turn(bank[4 + c][:, t * P:(t + 1) * P], ON[:, t, c * P:(c + 1) * P], ident)
                        last.then_inc(g_turned, 1)

                gla_pre(0)
                gla_tiles(True)
                per = {g_keys: 1, g_kready: 1, g_state: 1, g_qb: 1, g_kc: 1, g_pair: len(LEVELS), g_att: 1, g_rows: 1, g_la: 1,
                       g_exp: 4 + (len(LEVELS) - 1) * nb + 1}
                with T.loop(pe, GH - 1, per) as i:
                    gla_head(i, True)
                gla_head(GH - 1, False)
                loop_blocks(2, lambda: cols_product(4, AT, tq))

                def branch_ready():
                    first = T.next(bt_ready)
                    second = T.next(bt_ready)
                    return [(bt_ready, first)] * 2 + [(bt_ready, second)] * 2

                def gated(b):
                    for n in range(2):
                        cols_product(4, AT, tq)
                    for n in range(2):
                        cols_product(4, BT, tq, ready=b)

                gated(branch_ready())

                loop_blocks(2, lambda: cols_product(4, AT, tq))
                cols_product(AKV, AT, TOK, wcols=AKV * AD)
                rows_product(AKV * AD)
                one_col = cst("ones")[:, 0:1]
                pe.wait_ge(a_sq, T.next(a_sq, AH + AKV))
                for hd in range(AH):
                    for t in range(nq):
                        mm(bank[4][:, hd * nq + t:hd * nq + t + 1], SQQ[:, hd * TOK + t * P:hd * TOK + (t + 1) * P], one_col, start=True, stop=True)
                for n in range(AKV * TT):
                    last = mm(bank[4][:, AH * nq + n:AH * nq + n + 1], SQK[:, n * P:(n + 1) * P], one_col, start=True, stop=True)
                last.then_inc(a_sums, 1)

                def rotated(o, q):
                    pe.wait_ge(a_gain, T.next(a_gain))
                    mm(o, cst("rot"), q, start=True, stop=True).then_inc(a_rot, 1)

                rotated(bank[5][:, :], KG[:, :, 0:S])
                for r in range(2):
                    rotated(bank[6 + r][:, 0:S], QS[:, r, 0:S])
                pe.wait_ge(a_diag, T.next(a_diag))
                for kv in range(AKV):
                    for t in range(TT):
                        last = mm(bank[5 - kv][:, t * P:(t + 1) * P], cst("ones"), DIAG[:, kv, t, :], start=True, stop=True)
                last.then_inc(a_bc, 1)

                def attend(kv, ahead):
                    for r in range(2):
                        pe.wait_ge(a_q, T.next(a_q))
                        for t in range(nq):
                            q = QS[:, r, t * P:(t + 1) * P]
                            if t < NT:
                                last = mm(bank[3 * r + t][:, :], q, K2[:, kv, :], start=True, stop=True)
                            else:
                                last = mm(bank[3 * r + 2][:, (t - NT) * S:(t - NT + 1) * S], q, K2[:, kv, S:TOK], start=True, stop=True)
                        last.then_inc(a_score, 1)
                    if ahead:
                        for r in range(2):
                            rotated(bank[6 + r][:, 0:S], QS[:, r, 0:S])
                    for r in range(2):
                        pe.wait_ge(a_norm, T.next(a_norm))
                        for t in range(NT):
                            for s in range(TT):
                                last = turn(bank[3 * r + t][:, s * P:(s + 1) * P], PL[:, r, t, s * P:(s + 1) * P], ident)
                        for t in range(nq - NT):
                            for s in range(NT):
                                last = turn(bank[3 * r + 2][:, t * S + s * P:t * S + (s + 1) * P], PC[:, r, t, s * P:(s + 1) * P], ident)
                        last.then_inc(a_turned, 1)
                    v = [VA[:, s, kv * AD:(kv + 1) * AD] for s in range(TT)]
                    for r in range(2):
                        pe.wait_ge(a_pt, T.next(a_pt))
                        for s in range(TT):
                            last = mm(bank[3 * r][:, 0:S], v[s], PLT[:, r, s, :], start=s == 0, stop=s == TT - 1)
                        if nq > NT:
                            for s in range(NT):
                                last = mm(bank[3 * r][:, S:TOK], v[NT + s], PCT[:, r, s, :], start=s == 0, stop=s == NT - 1)
                        last.then_inc(a_out, 1)
                    for r in range(2):
                        pe.wait_ge(a_stored, T.next(a_stored))

                per = {a_gain: 2, a_q: 2, a_norm: 2, a_pt: 2, a_stored: 2}
                with T.loop(pe, AH // 2 // AKV, per):
                    attend(0, True)
                attend(1, True)
                attend(1, False)
                loop_blocks(2, lambda: cols_product(4, AT, tq))
                gated(branch_ready())
                with T.loop(pe, 2, {lo_split: 4 * SLOTS} | {b: 4 for b in bank_free}):
                    for _ in range(4):
                        cols_product(4, AT, tq)
                gated(branch_ready())
                ready = [(bt_ready, T.next(bt_ready)) for s in range(SLOTS)]
                loop_blocks(2, lambda: cols_product(4, BT, tq, ready=ready))
                sum_squares(tq, out_sq)
            pe.wait_ge(x_ready, 3 * KC)
            for t in range(NT):
                for g in range(2):
                    for c in range(4):
                        last = turn(bank[4 + 2 * t + g][:, c * P:(c + 1) * P], xT[:, 4 * g + c, t * P:(t + 1) * P], ident)
                    last.then_inc(x_turned, 1)


INV_TURN = float(1.0 / (2.0 * 3.141592653589793))
ROUND = 1.5 * 2.0 ** 23
TURN_PARTS = (6.25, 0.033203125, 2.0 * 3.141592653589793 - 6.283203125)
PI_IN = 3.1415925

_BIG = ["x", "p", "e_w_in", "e_w_uq", "e_w_ukv", "e_w_out", "o_w_in", "o_w_out", "w_ff1", "w_ff2", "w_ple_gate", "w_ple_proj",
        "ctx_2", "w_ada_2", "w_in_2", "w_decay_fwd_2", "b_decay_fwd_2", "w_decay_bwd_2", "b_decay_bwd_2", "w_br_conv_2",
        "w_br_attn_2", "w_br_gla_2", "w_out_2"]


def shape_constants():
    import numpy as np

    c, f = np.zeros((P, NCONST), np.float32), np.zeros((P, NFIRST), np.float32)

    def put(a, where, name, v):
        a[:, where[name][0]:where[name][0] + where[name][1]] = v

    i = np.arange(P)
    put(c, CONST, "ident", np.eye(P))
    put(c, CONST, "tri_f", (i[:, None] <= i[None, :]) / 16.0)
    put(c, CONST, "tri_b", (i[:, None] >= i[None, :]) / 16.0)
    rot = np.zeros((P, P))
    for m in range(P):
        rot[m + 32 if m // 32 % 2 == 0 else m - 32, m] = -1.0 if m // 32 % 2 == 0 else 1.0
    put(c, CONST, "rot", rot)
    put(c, CONST, "ones", 1.0)
    freqs = np.float32(10000.0) ** (-np.arange(32, dtype=np.float32) * np.float32(2.0) / np.float32(64))
    t = np.arange(S)
    place = np.where((i // 64 == 0)[:, None], (t // 64)[None, :], (t % 64)[None, :]).astype(np.float32)
    angle = (place * freqs[i % 32][:, None]).astype(np.float32).astype(np.float64)
    put(c, CONST, "cos", np.cos(angle))
    put(c, CONST, "sin", np.sin(angle))
    q = np.concatenate([np.repeat(i[:, None], P, 1), np.repeat(P + i[:, None], S, 1)], 1)
    k = np.concatenate([np.arange(P), np.arange(S)])[None, :]
    d = q - k
    put(f, FIRST, "dist", np.where(d >= 0, d, 1e30))
    put(f, FIRST, "causal", np.where(d >= 0, 0.0, -1e30))
    count = sum(((d >= 0) & (d <= w) & (d % g == 0)).astype(np.int64) for w, g in ((128, 1), (512, 4), (2048, 16)))
    put(f, FIRST, "lncount", np.where(d < 0, 0.0, np.where(count > 0, np.log(np.maximum(count, 1)), -1e30)))
    half = ROPE // 2
    put(f, FIRST, "inv_freq", np.float32(10000.0) ** (-np.arange(half, dtype=np.float32) / np.float32(half)))
    put(f, FIRST, "dil_slope", -(2.0 ** (-8.0 * np.arange(1, HEADS_E + 1) / HEADS_E)))
    put(f, FIRST, "moba_slope", -(2.0 ** (-8.0 * np.arange(1, HEADS_O + 1) / HEADS_O)))
    put(f, FIRST, "inv_n_z", [1.0 / Q_LORA, 1.0 / KV_LORA, 1.0 / ROPE] + [1.0 / HD] * 2 * HEADS_E)
    put(f, FIRST, "inv_n_q", [1.0 / NOPE] * HEADS_E + [1.0 / ROPE] * HEADS_E + [1.0 / NOPE] * HEADS_E)
    return c, f


def level_masks():
    import numpy as np

    k, q = np.arange(P)[:, None], np.arange(P)[None, :]
    return np.concatenate([k == q] + [(k // (2 * n) == q // (2 * n)) & (k // n != q // n) for n in LEVELS], 1).astype(np.int32)


def level_sums():
    import numpy as np

    s, t = np.arange(P)[:, None], np.arange(P)[None, :]

    def within(n, d, strict):
        order = (s < t if strict else s <= t) if d == 0 else (s > t if strict else s >= t)
        return (s // n == t // n) & order

    blocks = []
    for d in range(2):
        blocks += [within(P, 1 - d, True), within(P, d, False)]
    for n in LEVELS:
        later = np.arange(P) % (2 * n) >= n
        for d in range(2):
            mine, other = (later, ~later) if d == 0 else (~later, later)
            blocks.append(within(n, d, False)[:, mine])
            if n > 1:
                blocks.append(within(n, 1 - d, True)[:, other])
    return np.concatenate(blocks, 1).astype(np.float32) / 16


def packed(inputs):
    import numpy as np

    c, f = shape_constants()
    col = np.zeros((P, NCOLS), np.float32)
    for name, (at, n) in COLS.items():
        if name == "cond":
            v = np.stack([np.asarray(inputs["c_2"]).reshape(KC, P), np.asarray(inputs["c_ctx_2"]).reshape(KC, P)], 1).reshape(-1, P)
        else:
            v = np.asarray(inputs[name]).reshape(n, -1)
        col[0:v.shape[1], at:at + n] = v.T
    at = FIRST["rope_gains"][0]
    f[:, at:at + ROPE] = np.broadcast_to(np.asarray(inputs["e_qn_rope"]).reshape(1, ROPE), (P, ROPE))
    f[:, at + ROPE:at + 2 * ROPE] = np.broadcast_to(np.asarray(inputs["e_kn_rope"]).reshape(1, ROPE), (P, ROPE))
    return {"const": c, "first": f, "cols": col, "mask": level_masks(), "tri": level_sums(),
            "pos": np.ascontiguousarray(np.asarray(inputs["positions"]).reshape(NT, P).T.astype(np.int32))}


def kernel(**inputs):
    import numpy as np
    import concourse.bacc as bacc
    from concourse import mybir as _mybir
    from concourse.bass_utils import run_bass_kernel_spmd

    nc = bacc.Bacc("TRN2", target_bir_lowering=False, num_devices=1)
    arrays = {name: np.ascontiguousarray(inputs[name]) for name in _BIG} | packed(inputs)
    io = {name: nc.dram_tensor("in_" + name, a.shape, _mybir.dt.from_np(a.dtype), kind="ExternalInput").ap()
          for name, a in arrays.items()}
    out = nc.dram_tensor("out", (1, S, D), _mybir.dt.float32, kind="ExternalOutput").ap()
    mixer_kernel(nc, io, out)
    run = run_bass_kernel_spmd(nc, [{"in_" + name: a for name, a in arrays.items()}], core_ids=[0])
    return run.results[0]["out"]
```
